# Optimizing a Trainium2 kernel written in Bass

```python
import math
import jax, jax.numpy as jnp
from jax import lax
import numpy as np

D_MODEL = 1024
BATCH = 1
SEQ = 512
DEPTH = 1

ROPE_THETA = 500000.0
NORM_EPS = 1e-6
Q_BLOCK = 128
DA_HEADS = 8
DA_HEAD_DIM = 64
DA_ROT = DA_HEAD_DIM // 4
DA_QK_W = DA_HEADS * 2 * DA_HEAD_DIM
DA_V_W = DA_HEADS * 2 * DA_HEAD_DIM
MLA_HEADS = 8
MLA_Q_LORA = 768
MLA_KV_LORA = 512
MLA_NOPE = 128
MLA_ROPE = 64
MLA_V = 128
N_EXPERTS = 32
TOP_K = 4
D_FF_EXPERT = 1024
SWIGLU_ALPHA = 1.702
SWIGLU_LIMIT = 7.0
EXPERT_BLOCK = 128
IN_SPLITS = (DA_QK_W, DA_QK_W, DA_V_W, MLA_Q_LORA, MLA_KV_LORA, MLA_ROPE, 2 * D_MODEL)
IN_WIDTH = sum(IN_SPLITS)
IN_OFFSETS = [int(o) for o in np.cumsum(IN_SPLITS)[:-1]]

kernel_name = "hybrid_diffattn_mla_gated_moe_encoder"

def rms_norm(x, g):
    xf = x.astype(jnp.float32)
    y = xf * lax.rsqrt(jnp.mean(xf * xf, axis=-1, keepdims=True) + NORM_EPS)
    return (y * g.astype(jnp.float32)).astype(x.dtype)

def apply_rope(x, positions, rot_dim):
    half = rot_dim // 2
    inv = ROPE_THETA ** (-jnp.arange(0, rot_dim, 2, dtype=jnp.float32) / rot_dim)
    ang = positions.astype(jnp.float32)[..., None] * inv
    shape = ang.shape[:2] + (1,) * (x.ndim - 3) + (half,)
    c = jnp.cos(ang).reshape(shape).astype(x.dtype)
    s = jnp.sin(ang).reshape(shape).astype(x.dtype)
    x1 = x[..., :half]
    x2 = x[..., half:rot_dim]
    return jnp.concatenate([x1 * c - x2 * s, x2 * c + x1 * s, x[..., rot_dim:]], axis=-1)

def _to_blocks(t):
    b, s = t.shape[:2]
    t = t.reshape((b, s // Q_BLOCK, Q_BLOCK) + t.shape[2:])
    return jnp.moveaxis(t, 1, 0)

def _from_blocks(t):
    t = jnp.moveaxis(t, 0, 1)
    return t.reshape((t.shape[0], t.shape[1] * t.shape[2]) + t.shape[3:])

def diff_attention(q, k, v, lam, lam_init, g_subln):
    scale = DA_HEAD_DIM ** -0.5

    def one_block(qb):
        s = jnp.einsum('bqhmd,bkhmd->bhmqk', qb, k).astype(jnp.float32) * scale
        p = jax.nn.softmax(s, axis=-1)
        a = (p[:, :, 0] - lam * p[:, :, 1]).astype(v.dtype)
        return jnp.einsum('bhqk,bkhe->bqhe', a, v)

    o = _from_blocks(lax.map(one_block, _to_blocks(q)))
    o = rms_norm(o, g_subln) * (1.0 - lam_init)
    return o.reshape(o.shape[:2] + (-1,))

def mla_attention(c_q, c_kv, k_rope, positions, g_q, g_kv, w_uq, w_ukv):
    b, s = c_q.shape[:2]
    q = (rms_norm(c_q, g_q) @ w_uq).reshape(b, s, MLA_HEADS, MLA_NOPE + MLA_ROPE)
    q_nope = q[..., :MLA_NOPE]
    q_rope = apply_rope(q[..., MLA_NOPE:], positions, MLA_ROPE)
    kv = (rms_norm(c_kv, g_kv) @ w_ukv).reshape(b, s, MLA_HEADS, MLA_NOPE + MLA_V)
    k_nope = kv[..., :MLA_NOPE]
    v = kv[..., MLA_NOPE:]
    k_r = apply_rope(k_rope, positions, MLA_ROPE)
    scale = (MLA_NOPE + MLA_ROPE) ** -0.5

    def one_block(qs):
        qn, qr = qs
        sc = (jnp.einsum('bqhd,bkhd->bhqk', qn, k_nope)
              + jnp.einsum('bqhr,bkr->bhqk', qr, k_r))
        p = jax.nn.softmax(sc.astype(jnp.float32) * scale, axis=-1).astype(v.dtype)
        return jnp.einsum('bhqk,bkhe->bqhe', p, v)

    o = _from_blocks(lax.map(one_block, (_to_blocks(q_nope), _to_blocks(q_rope))))
    return o.reshape(b, s, MLA_HEADS * MLA_V)

def moe_ffn(h, w_router, b_router, w_gate, b_gate, w_up, b_up, w_down, b_down):
    b, s, d = h.shape
    t = b * s
    hf = h.reshape(t, d)
    logits = (hf @ w_router + b_router).astype(jnp.float32)
    top_val, top_idx = lax.top_k(logits, TOP_K)
    top_w = jax.nn.softmax(top_val, axis=-1).astype(h.dtype)
    n_assign = t * TOP_K
    e_flat = top_idx.reshape(-1).astype(jnp.int32)
    w_flat = top_w.reshape(-1)
    tok_flat = jnp.arange(n_assign, dtype=jnp.int32) // TOP_K
    order = jnp.argsort(e_flat)
    e_sorted = e_flat[order]
    counts = jnp.bincount(e_flat, length=N_EXPERTS).astype(jnp.int32)
    padded = (counts + EXPERT_BLOCK - 1) // EXPERT_BLOCK * EXPERT_BLOCK
    padded_end = jnp.cumsum(padded)
    padded_start = padded_end - padded
    start = jnp.cumsum(counts) - counts
    dest = padded_start[e_sorted] + jnp.arange(n_assign, dtype=jnp.int32) - start[e_sorted]
    n_blocks = -(-n_assign // EXPERT_BLOCK) + N_EXPERTS
    n_rows = n_blocks * EXPERT_BLOCK
    row_tok = jnp.zeros((n_rows,), jnp.int32).at[dest].set(tok_flat[order])
    row_w = jnp.zeros((n_rows,), h.dtype).at[dest].set(w_flat[order])
    block_e = jnp.minimum(
        jnp.searchsorted(padded_end, jnp.arange(n_blocks, dtype=jnp.int32) * EXPERT_BLOCK,
                         side='right'), N_EXPERTS - 1)
    xs = hf[row_tok].reshape(n_blocks, EXPERT_BLOCK, d)

    def expert_block(args):
        xb, e = args
        gate = jnp.minimum(xb @ w_gate[e] + b_gate[e], SWIGLU_LIMIT)
        up = jnp.clip(xb @ w_up[e] + b_up[e], -SWIGLU_LIMIT, SWIGLU_LIMIT)
        act = (up + 1.0) * (gate * jax.nn.sigmoid(SWIGLU_ALPHA * gate))
        return act @ w_down[e] + b_down[e]

    ys = lax.map(expert_block, (xs, block_e)).reshape(n_rows, d)
    out = jax.ops.segment_sum(ys * row_w[:, None], row_tok, num_segments=t)
    return out.reshape(b, s, d)

def setup_inputs(seed: int = 0) -> dict:
    key = jax.random.key(seed)
    ks = iter(jax.random.split(key, 40))
    L = DEPTH

    def nrm(shape, scale):
        return jax.random.normal(next(ks), shape, jnp.float32) * scale

    def gain(shape):
        return 1.0 + nrm(shape, 0.02)

    x = jax.random.normal(next(ks), (BATCH, SEQ, D_MODEL), jnp.float32)
    offs = jax.random.randint(next(ks), (BATCH, 1), 0, SEQ, dtype=jnp.int32)
    positions = jnp.arange(SEQ, dtype=jnp.int32)[None, :] + offs
    E, F, D = N_EXPERTS, D_FF_EXPERT, D_MODEL
    return {
        "x": x,
        "positions": positions,
        "g_mix": gain((L, D)),
        "w_in": nrm((L, D, IN_WIDTH), D ** -0.5),
        "lam_q1": nrm((L, DA_HEAD_DIM), 0.1),
        "lam_k1": nrm((L, DA_HEAD_DIM), 0.1),
        "lam_q2": nrm((L, DA_HEAD_DIM), 0.1),
        "lam_k2": nrm((L, DA_HEAD_DIM), 0.1),
        "g_subln": gain((L, 2 * DA_HEAD_DIM)),
        "g_q": gain((L, MLA_Q_LORA)),
        "g_kv": gain((L, MLA_KV_LORA)),
        "w_uq": nrm((L, MLA_Q_LORA, MLA_HEADS * (MLA_NOPE + MLA_ROPE)), MLA_Q_LORA ** -0.5),
        "w_ukv": nrm((L, MLA_KV_LORA, MLA_HEADS * (MLA_NOPE + MLA_V)), MLA_KV_LORA ** -0.5),
        "w_o_diff": nrm((L, DA_V_W, D), DA_V_W ** -0.5),
        "w_o_mla": nrm((L, MLA_HEADS * MLA_V, D), (MLA_HEADS * MLA_V) ** -0.5),
        "b_gates": nrm((L, 2 * D), 0.1),
        "w_out": nrm((L, D, D), D ** -0.5),
        "g_ffn": gain((L, D)),
        "w_router": nrm((L, D, E), D ** -0.5),
        "b_router": nrm((L, E), 0.01),
        "w_gate": nrm((L, E, D, F), D ** -0.5),
        "b_gate": nrm((L, E, F), 0.02),
        "w_up": nrm((L, E, D, F), D ** -0.5),
        "b_up": nrm((L, E, F), 0.02),
        "w_down": nrm((L, E, F, D), F ** -0.5),
        "b_down": nrm((L, E, D), 0.02),
        "g_final": gain((D,)),
    }

def reference(x, positions, g_mix, w_in, lam_q1, lam_k1, lam_q2, lam_k2, g_subln, g_q, g_kv,
              w_uq, w_ukv, w_o_diff, w_o_mla, b_gates, w_out, g_ffn, w_router, b_router,
              w_gate, b_gate, w_up, b_up, w_down, b_down, g_final):
    b, s, d = x.shape
    for l in range(DEPTH):
        h = rms_norm(x, g_mix[l])
        z = h @ w_in[l]
        z_qa, z_ka, z_va, z_cq, z_ckv, z_kr, z_g = jnp.split(z, IN_OFFSETS, axis=-1)

        q_a = apply_rope(z_qa.reshape(b, s, DA_HEADS, 2, DA_HEAD_DIM), positions, DA_ROT)
        k_a = apply_rope(z_ka.reshape(b, s, DA_HEADS, 2, DA_HEAD_DIM), positions, DA_ROT)
        v_a = z_va.reshape(b, s, DA_HEADS, 2 * DA_HEAD_DIM)
        lam_init = 0.8 - 0.6 * math.exp(-0.3 * l)
        lam = (jnp.exp(jnp.sum(lam_q1[l].astype(jnp.float32) * lam_k1[l].astype(jnp.float32)))
               - jnp.exp(jnp.sum(lam_q2[l].astype(jnp.float32) * lam_k2[l].astype(jnp.float32)))
               + lam_init)
        o_a = diff_attention(q_a, k_a, v_a, lam, lam_init, g_subln[l])

        o_b = mla_attention(z_cq, z_ckv, z_kr, positions, g_q[l], g_kv[l], w_uq[l], w_ukv[l])

        gates = jax.nn.sigmoid(z_g + b_gates[l]).reshape(b, s, 2, d)
        merged = gates[:, :, 0] * (o_a @ w_o_diff[l]) + gates[:, :, 1] * (o_b @ w_o_mla[l])
        x = x + merged @ w_out[l]

        x = x + moe_ffn(rms_norm(x, g_ffn[l]), w_router[l], b_router[l], w_gate[l], b_gate[l],
                        w_up[l], b_up[l], w_down[l], b_down[l])
    return rms_norm(x, g_final)


_drawn_inputs = setup_inputs


def setup_inputs(seed=0):
    import zlib

    import numpy as np

    out = dict(_drawn_inputs(seed))
    spreads = {}
    factors = {'g_q': 8.0,
     'g_kv': 5.054,
     'b_gate': 6.649,
     'b_up': 22.82,
     'b_down': 26.755,
     'g_final': 22.046,
     'lam_q1': 2.92,
     'lam_k1': 6.093,
     'lam_q2': 5.274,
     'lam_k2': 3.275,
     'g_subln': 7.143,
     'g_ffn': 3.209,
     'b_router': 3.855}
    for name, (base, spread) in spreads.items():
        noise = np.random.default_rng([zlib.crc32(name.encode()), seed]).standard_normal(out[name].shape)
        drawn = base * np.exp(spread * noise) if base else spread * noise
        out[name] = __import__('jax').numpy.asarray(drawn.astype(out[name].dtype))
    for name, factor in factors.items():
        out[name] = (out[name] * factor).astype(out[name].dtype)
    return out
```

```python
import math
from contextlib import ExitStack

import numpy as np

import concourse.bass as bass
from concourse import mybir

F32 = mybir.dt.float32
F32R = mybir.dt.float32r
BF16 = mybir.dt.bfloat16
I32 = mybir.dt.int32
U32 = mybir.dt.uint32
ALU = mybir.AluOpType
ACT = mybir.ActivationFunctionType
AX_X = mybir.AxisListType.X

P = 128
SEQ = 512
D = 1024
HEADS = 8
DA_DIM = 64
DA_ROT = 16
Q_LORA = 768
KV_LORA = 512
NOPE = 128
ROPE = 64
E = 32
TOPK = 4
EPS = 1e-6
THETA = 500000.0
LAM_INIT = 0.8 - 0.6 * math.exp(-0.3 * 0)
ALPHA = 1.702
LIMIT = 7.0
QK_W = HEADS * 2 * DA_DIM
C_W = Q_LORA + KV_LORA + ROPE
C_COL = 3 * QK_W
G_COL = C_COL + C_W
IN_W = G_COL + 2 * D
NT = SEQ // P
KD = D // P
FH = DA_ROT // 2
FM = ROPE // 2
NF = FH + FM
NCT = (Q_LORA + KV_LORA) // P

ROUNDS = SEQ // P
BLOCKS = ROUNDS * E
NOWHERE = 1 << 14

RAW = 4
SPL = 2
MRAW = 6
MSPL = 3
CH = 2048


def groups_of_projection():
    g = []
    for n in range(2 * QK_W // 512):
        g.append(dict(w="w_in", col=512 * n, kt=KD, src="h", kind="rope_da", dst="qkT", row=512 * n, n=512))
    for n in range(QK_W // 512):
        g.append(dict(w="w_in", col=2 * QK_W + 512 * n, kt=KD, src="h", kind="rows", dst="va", row=512 * n, n=512))
    for c in range(0, C_W, 512):
        g.append(dict(w="w_in", col=C_COL + c, kt=KD, src="h", kind="latent", row=c, n=min(512, C_W - c)))
    for n in range(2 * D // 512):
        g.append(dict(w="w_in", col=G_COL + 512 * n, kt=KD, src="h", kind="gate", dst="gT", row=512 * n, n=512))
    for n in range(2):
        g.append(dict(w="uq_nope", col=4 * n, kt=Q_LORA // P, src="q", kind="cols", dst="qnT", row=512 * n, n=512))
    g.append(dict(w="uq_rope", col=0, kt=Q_LORA // P, src="q", kind="rope_mla", dst="qrT", row=0, n=512))
    for n in range(2):
        g.append(dict(w="ukv_nope", col=4 * n, kt=KV_LORA // P, src="kv", kind="cols", dst="knT", row=512 * n, n=512))
    for n in range(2):
        g.append(dict(w="ukv_v", col=4 * n, kt=KV_LORA // P, src="kv", kind="rows", dst="vb", row=512 * n, n=512))
    return g


def groups_of_output():
    g = []
    for n in range(2):
        g.append(dict(w="w_o_mla", col=512 * n, kt=KD, src="om", kind="merge_b", row=512 * n, n=512))
        g.append(dict(w="w_o_diff", col=512 * n, kt=KD, src="od", kind="merge_a", row=512 * n, n=512))
    for n in range(2):
        g.append(dict(w="w_out", col=512 * n, kt=KD, src="m", kind="resid", row=512 * n, n=512))
    return g


def hybrid_encoder_layer(nc, x, positions, g_mix, w_in, lam_q1, lam_k1, lam_q2, lam_k2, g_subln, g_q,
                         g_kv, w_uq, w_ukv, w_o_diff, w_o_mla, b_gates, w_out, g_ffn, w_router, b_router,
                         w_gate, b_gate, w_up, b_up, w_down, b_down, g_final, inv_freq, identity, out,
                         debug=None):
    PG = groups_of_projection()
    OG = groups_of_output()
    GROUPS = PG + OG
    NPG = len(PG)

    chunks = []
    for j, g in enumerate(GROUPS):
        per = 4 if g["kt"] % 4 == 0 else 3
        g["chunks"] = []
        for k0 in range(0, g["kt"], per):
            g["chunks"].append(len(chunks))
            chunks.append((j, k0, per))
    NCH = len(chunks)
    PCH = GROUPS[NPG]["chunks"][0]

    w2 = {
        "w_in": w_in[0], "w_o_mla": w_o_mla[0], "w_o_diff": w_o_diff[0], "w_out": w_out[0],
    }
    uq = w_uq[0].rearrange("(k p) (h c) -> p k h c", p=P, h=HEADS)
    ukv = w_ukv[0].rearrange("(k p) (h c) -> p k h c", p=P, h=HEADS)

    def chunk_parts(n):
        j, k0, per = chunks[n]
        g = GROUPS[j]
        c, w = g["col"], g["n"]
        dst = raw[n % RAW][:, 0:per * w].rearrange("p (k c) -> p k c", k=per)
        if g["w"] in w2:
            return [(w2[g["w"]].rearrange("(k p) c -> p k c", p=P)[:, k0:k0 + per, c:c + w], dst)]
        if g["w"] == "uq_nope":
            src = uq[:, k0:k0 + per, c:c + 4, 0:NOPE]
        elif g["w"] == "uq_rope":
            src = uq[:, k0:k0 + per, :, NOPE:]
        elif g["w"] == "ukv_nope":
            src = ukv[:, k0:k0 + per, c:c + 4, 0:NOPE]
        else:
            src = ukv[:, k0:k0 + per, c:c + 4, NOPE:]
        hh = src.shape[2]
        d4 = dst.rearrange("p k (h c) -> p k h c", h=hh)
        return [(src[:, k], d4[:, k]) for k in range(per)]

    qkT_d = nc.dram_tensor("qkT_scratch", [2 * QK_W, SEQ], F32).ap()
    qnT_d = nc.dram_tensor("qnT_scratch", [HEADS * NOPE, SEQ], F32).ap()
    knT_d = nc.dram_tensor("knT_scratch", [HEADS * NOPE, SEQ], F32).ap()
    qrT_d = nc.dram_tensor("qrT_scratch", [HEADS * ROPE, SEQ], F32).ap()
    gT_d = nc.dram_tensor("gT_scratch", [2 * D, SEQ], F32).ap()
    va_d = nc.dram_tensor("va_scratch", [SEQ, QK_W], F32).ap()
    vb_d = nc.dram_tensor("vb_scratch", [SEQ, HEADS * P], F32).ap()
    h2_d = nc.dram_tensor("h2_scratch", [SEQ, D], F32).ap()
    table_d = nc.dram_tensor("table_scratch", [BLOCKS * P, 4], I32).ap()
    y_d = nc.dram_tensor("y_scratch", [SEQ * TOPK, D], F32).ap()
    scratch = dict(qkT=qkT_d, qnT=qnT_d, knT=knT_d, qrT=qrT_d, gT=gT_d, va=va_d, vb=vb_d)

    base = (nc.sbuf_base + 63) // 64 * 64
    KB = 1024
    used = {}

    def at(name, kb, shape, dt=F32):
        used[name] = (kb, int(np.prod(shape[1:])) * (2 if dt == BF16 else 4) / KB)
        return nc.alloc_sbuf_tensor_at(name, shape, dt, offset=base + int(kb * KB))

    ident = at("ident", 0, [P, P])
    cos = at("cos", 0.5, [P, NT, NF])
    sin = at("sin", 1.125, [P, NT, NF])
    cols = at("cols", 1.75, [P, 48])
    GM, GQ, GKV, GSUB, BG, NCOL = 0, 8, 14, 18, 19, 35
    lam = at("lam", 2.0, [P, 8])
    stat = at("stat", 2.0625, [P, 32])
    stat2 = at("stat2", 2.25, [P, 32])
    half = at("half", 2.375, [P, 32])
    msr = at("msr", 2.5, [P, 32])
    soft = at("soft", 2.625, [P, 2, 8])
    onec = at("onec", 2.6875, [P, 4])
    further = at("further", 2.75, [P, 2], I32)
    krT_hi = at("krT_hi", 3, [ROPE, SEQ], F32R)
    krT_lo = at("krT_lo", 5, [ROPE, SEQ], F32R)
    raw = [at(f"raw{i}", 7 + 8 * i, [P, CH]) for i in range(RAW)]
    whi = [at(f"whi{i}", 39 + 8 * i, [P, CH], F32R) for i in range(SPL)]
    wlo = [at(f"wlo{i}", 55 + 8 * i, [P, CH], F32R) for i in range(SPL)]
    hT_hi = at("hT_hi", 71, [P, KD, SEQ], F32R)
    hT_lo = at("hT_lo", 87, [P, KD, SEQ], F32R)
    cbuf = at("cbuf", 103, [P, NT, C_W])
    cT_hi = at("cT_hi", 124, [P, NCT, SEQ], F32R)
    cT_lo = at("cT_lo", 144, [P, NCT, SEQ], F32R)
    rstage = at("rstage", 164, [P, NT, 512])
    ostage = [at(f"ostage{i}", 172 + 8 * i, [P, 4, 512]) for i in range(2)]
    xrows = at("xrows", 172, [P, NT, D])
    rtmp = at("rtmp", 188, [P, 4, NT * 8 * 32])
    angles = at("angles", 188, [P, 6, NT * NF])
    lamv = at("lamv", 200, [P, 6, DA_DIM])
    crows = at("crows", 201.5, [NCOL, P])
    posi = at("posi", 202.5, [P, NT], I32)
    posf = at("posf", 202.625, [P, NT])
    invf = at("invf", 202.75, [P, NF])
    sq_dump = at("sq_dump", 124, [P, D])
    om_hi = at("om_hi", 71, [P, HEADS, SEQ], F32R)
    om_lo = at("om_lo", 87, [P, HEADS, SEQ], F32R)
    oraw = at("oraw", 103, [P, HEADS, SEQ])
    q_raw = at("q_raw", 119, [P, SEQ])
    k_raw = at("k_raw", 121, [P, SEQ])
    v_raw = at("v_raw", 123, [P, NT, P])
    r_raw = at("r_raw", 125, [ROPE, SEQ])
    qs = [[at(f"q{s}{i}", 127 + 4 * i + 2 * (s == "lo"), [P, SEQ], F32R) for s in ("hi", "lo")] for i in range(2)]
    ks = [[at(f"k{s}{i}", 135 + 4 * i + 2 * (s == "lo"), [P, SEQ], F32R) for s in ("hi", "lo")] for i in range(2)]
    vs = [[at(f"v{s}{i}", 143 + 4 * i + 2 * (s == "lo"), [P, NT, P], F32R) for s in ("hi", "lo")] for i in range(2)]
    rs = [[at(f"r{s}{i}", 151 + 4 * i + 2 * (s == "lo"), [ROPE, SEQ], F32R) for s in ("hi", "lo")] for i in range(2)]
    probs = at("probs", 159, [P, 2, 2, SEQ])
    amap = at("amap", 167, [P, 2, SEQ])
    aterm = at("aterm", 171, [P, SEQ])
    aT_hi = at("aT_hi", 173, [P, NT, SEQ], F32R)
    aT_lo = at("aT_lo", 181, [P, NT, SEQ], F32R)
    osq = at("osq", 189, [P, SEQ])
    mT_hi = at("mT_hi", 119, [P, KD, SEQ], F32R)
    mT_lo = at("mT_lo", 135, [P, KD, SEQ], F32R)
    od_hi = at("od_hi", 151, [P, HEADS, SEQ], F32R)
    od_lo = at("od_lo", 167, [P, HEADS, SEQ], F32R)
    gstage = at("gstage", 183, [P, 4, SEQ])
    x2 = at("x2", 191, [P, NT, D])
    mtmp = at("mtmp", 103, [P, 4, SEQ])
    rbc = at("rbc", 191, [P, NT, P])
    h2 = at("h2", 71, [P, NT, D])
    h2T = at("h2T", 87, [P, KD, SEQ])
    gffn = at("gffn", 103, [P, D])
    wr = at("wr", 107, [P, KD, E])
    br = at("br", 108, [P, E])
    logits = at("logits", 108.5, [P, NT, E])
    top8 = at("top8", 109, [P, NT, 8])
    idx8 = at("idx8", 109.125, [P, NT, 8], U32)
    idxf = at("idxf", 109.25, [P, NT, 8])
    wexp = at("wexp", 109.375, [P, NT, 8])
    iota_e = at("iota_e", 109.5, [P, E])
    pick = at("pick", 110, [P, NT, TOPK, E])
    chosen = at("chosen", 112, [P, NT, E])
    chosen_b = at("chosen_b", 112.5, [P, NT, E], BF16)
    upper = at("upper", 112.75, [P, P], BF16)
    allone = at("allone", 113, [P, P], BF16)
    rowof = at("rowof", 113.25, [P, NT, E])
    over = at("over", 113.75, [P, 4, NT * E])
    wdense = at("wdense", 115.75, [P, NT, E])
    wdT = at("wdT", 116.25, [E, SEQ])
    bdown = at("bdown", 118.25, [E, D])
    ptmp = at("ptmp", 122.25, [P, NT, TOPK, E])
    rowsel = at("rowsel", 124.25, [P, NT * TOPK])
    rowidx = at("rowidx", 124.375, [P, NT * TOPK], I32)
    rec = at("rec", 124.5, [P, NT * TOPK, 4], I32)
    bsrc = at("bsrc", 125, [96, 2, D])
    bhi = at("bhi", 151, [96, 2, D])
    bpart = at("bpart", 133, [96, 2, D], BF16)
    selid = at("selid", 137, [96, E])
    padrec = at("padrec", 163, [P, BLOCKS, 4], I32)
    mraw = raw + [at(f"mraw{i}", 175 + 8 * i, [P, CH]) for i in range(2)]
    mwhi = whi + [at("mwhi2", 71, [P, CH], F32R)]
    mwlo = wlo + [at("mwlo2", 79, [P, CH], F32R)]
    xT_hi = at("xT_hi", 139, [P, KD, P], F32R)
    xT_lo = at("xT_lo", 143, [P, KD, P], F32R)
    aT2_hi = at("aT2_hi", 147, [P, KD, P], F32R)
    aT2_lo = at("aT2_lo", 151, [P, KD, P], F32R)
    xe = at("xe", 155, [P, D])
    ye = at("ye", 159, [P, D])
    gg = at("gg", 87, [P, D])
    sg = at("sg", 91, [P, D])
    uu = at("uu", 95, [P, D])
    ae = at("ae", 99, [P, D])
    lists = at("lists", 163, [P, BLOCKS + 2, 4], I32)
    gidx = at("gidx", 171.5, [P, 4], I32)
    sidx = at("sidx", 171.5625, [P, 4], I32)
    selb = at("selb", 171.75, [96, P], BF16)
    ybuf = [at(f"ybuf{i}", 7 + 16 * i, [P, TOPK, D]) for i in range(4)]
    gfin = at("gfin", 87, [P, D])
    fdump = at("fdump", 91, [P, D])

    ctx = ExitStack()
    with ctx:
        ps = ctx.enter_context(nc.psum_tensor("ps", [P, 8, 512], F32))

        def sem(name):
            return ctx.enter_context(nc.semaphore(name))

        consts_in = sem("consts_in")
        cols_turned = sem("cols_turned")
        cols_ready = sem("cols_ready")
        x_in = sem("x_in")
        act_step = sem("act_step")
        dve_step = sem("dve_step")
        pool_step = sem("pool_step")
        raw_in = [sem(f"raw_in{i}") for i in range(RAW)]
        hi_done = sem("hi_done")
        lo_done = sem("lo_done")
        chunk_used = sem("chunk_used")
        set_free = [sem("set_free0"), sem("set_free1")]
        turned = sem("turned")
        rope_in = sem("rope_in")
        roped = sem("roped")
        stage_full = sem("stage_full")
        stored = [sem("stored0"), sem("stored1")]
        h_hi = sem("h_hi")
        h_lo = sem("h_lo")
        c_rows = sem("c_rows")
        c_ready = sem("c_ready")
        c_hi = sem("c_hi")
        c_lo = sem("c_lo")
        ss_ready = sem("ss_ready")
        rs_ready = sem("rs_ready")

        block = ctx.enter_context(nc.Block())

        bank_set = lambda s: ps[:, 4 * s:4 * s + 4, :]
        NROPE = [j for j, g in enumerate(PG) if g["kind"].startswith("rope")]
        LAT = [j for j, g in enumerate(PG) if g["kind"] == "latent"]
        LATE = [j for j, g in enumerate(PG) if g["src"] in ("q", "kv")][0]
        uses = [1, 1]
        used_before = {}
        for j in range(len(GROUPS)):
            if j == LATE:
                used_before["c0"], used_before["c1"] = uses[0], uses[1]
                uses[0] += 2
                uses[1] += 1
            if j == NPG:
                uses = [0, 0]
            used_before[j] = uses[j % 2]
            uses[j % 2] += 1
        STORES = [j for j, g in enumerate(PG) if "dst" in g]
        store_no = {j: n for n, j in enumerate(STORES)}

        def wait_stage(eng, j):
            n = store_no[j]
            if n >= 2:
                eng.wait_ge(stored[n % 2], 16 * (n // 2))

        def sp_chunk(sp, n):
            if n >= RAW:
                sp.wait_ge(hi_done, n - RAW + 1)
                sp.wait_ge(lo_done, n - RAW + 1)
            parts = chunk_parts(n)
            for src, dst in parts:
                sp.dma_start(dst, src).then_inc(raw_in[n % RAW], 16)

        landed = []
        per_slot = [0] * RAW
        for n in range(NCH):
            per_slot[n % RAW] += 16 * len(chunk_parts(n))
            landed.append(per_slot[n % RAW])

        def sp_start(sp):
            sp.dma_start(xrows[:], x[0].rearrange("(t p) d -> p t d", p=P)).then_inc(x_in, 16)
            sp.dma_start(ident[:], identity).then_inc(consts_in, 16)
            sp.dma_start(crows[GM:GM + KD, :], g_mix[0].rearrange("(k p) -> k p", p=P)).then_inc(consts_in, 16)
            for n in range(RAW):
                sp_chunk(sp, n)
            sp.dma_start(invf[:], inv_freq).then_inc(consts_in, 16)
            sp.dma_start(posi[:], positions[0].rearrange("(t p) -> p t", p=P), allow_slow_non_contiguous=True).then_inc(consts_in, 16)
            sp.dma_start(crows[GQ:GQ + 6, :], g_q[0].rearrange("(k p) -> k p", p=P)).then_inc(consts_in, 16)
            sp.dma_start(crows[GKV:GKV + 4, :], g_kv[0].rearrange("(k p) -> k p", p=P)).then_inc(consts_in, 16)
            sp.dma_start(crows[GSUB:GSUB + 1, :], g_subln[0].rearrange("(k p) -> k p", p=P)).then_inc(consts_in, 16)
            sp.dma_start(crows[BG:BG + 16, :], b_gates[0].rearrange("(k p) -> k p", p=P)).then_inc(consts_in, 16)
            for i, v in enumerate((lam_q1, lam_k1, lam_q2, lam_k2)):
                sp.dma_start(lamv[:, i, :], v[0].partition_broadcast(P)).then_inc(consts_in, 16)

        N_CONSTS = 12

        def act_split(act, n):
            per, w = chunks[n][2], GROUPS[chunks[n][0]]["n"]
            act.wait_ge(raw_in[n % RAW], landed[n])
            if n >= SPL:
                act.wait_ge(chunk_used, n - SPL + 1)
            nc.scalar.activation(whi[n % SPL][:, 0:per * w], raw[n % RAW][:, 0:per * w], ACT.Copy).then_inc(hi_done, 1)

        def dve_split(dve, n):
            per, w = chunks[n][2], GROUPS[chunks[n][0]]["n"]
            dve.wait_ge(hi_done, n + 1)
            nc.vector.tensor_tensor(wlo[n % SPL][:, 0:per * w], raw[n % RAW][:, 0:per * w],
                                    whi[n % SPL][:, 0:per * w].bitcast(F32), ALU.subtract).then_inc(lo_done, 1)

        acts_of = {"h": (hT_hi, hT_lo, 0), "q": (cT_hi, cT_lo, 0), "kv": (cT_hi, cT_lo, Q_LORA // P),
                   "om": (om_hi, om_lo, 0), "od": (od_hi, od_lo, 0), "m": (mT_hi, mT_lo, 0)}
        free_sem = {}

        def pe_group(pe, j, frees):
            g = GROUPS[j]
            hi, lo, off = acts_of[g["src"]]
            s = j % 2
            if used_before[j]:
                pe.wait_ge(frees[s], used_before[j])
            rows = g["kind"] in ("rope_da", "rope_mla", "rows", "latent", "resid")
            for n in g["chunks"]:
                _, k0, per = chunks[n]
                pe.wait_ge(lo_done, n + 1)
                wh = whi[n % SPL][:, 0:per * g["n"]].rearrange("p (k c) -> p k c", k=per)
                wl = wlo[n % SPL][:, 0:per * g["n"]].rearrange("p (k c) -> p k c", k=per)
                for kk in range(per):
                    k = k0 + kk
                    first, last = k == 0, k == g["kt"] - 1
                    for t in range(4):
                        if rows:
                            o = ps[:, 4 * s + t, 0:g["n"]]
                            ah = hi[:, off + k, t * P:(t + 1) * P]
                            al = lo[:, off + k, t * P:(t + 1) * P]
                            nc.tensor.matmul(o, ah, wh[:, kk, :], start=first, stop=False)
                            nc.tensor.matmul(o, ah, wl[:, kk, :], start=False, stop=False)
                            mm = nc.tensor.matmul(o, al, wh[:, kk, :], start=False, stop=last)
                        else:
                            o = ps[:, 4 * s + t, :]
                            a_h, a_l = hi[:, off + k, :], lo[:, off + k, :]
                            w_h, w_l = wh[:, kk, t * P:(t + 1) * P], wl[:, kk, t * P:(t + 1) * P]
                            nc.tensor.matmul(o, w_h, a_h, start=first, stop=False)
                            nc.tensor.matmul(o, w_h, a_l, start=False, stop=False)
                            mm = nc.tensor.matmul(o, w_l, a_h, start=False, stop=last)
                mm.then_inc(chunk_used, 1)

        def wait_group(eng, j):
            eng.wait_ge(chunk_used, GROUPS[j]["chunks"][-1] + 1)

        class Kind:
            pass

        def attention_kind(name, units, score_tiles, scale, loads):
            k = Kind()
            k.name, k.units, k.scale, k.loads = name, units, scale, loads
            k.items = NT // units
            k.qk_in = sem(f"{name}_qk_in")
            k.v_in = sem(f"{name}_v_in")
            k.hi = sem(f"{name}_hi")
            k.lo = sem(f"{name}_lo")
            k.v_seen = sem(f"{name}_v_seen")
            k.v_hi = sem(f"{name}_v_hi")
            k.v_lo = sem(f"{name}_v_lo")
            k.scored = sem(f"{name}_scored")
            k.topped = sem(f"{name}_topped")
            k.biased = sem(f"{name}_biased")
            k.exped = sem(f"{name}_exped")
            k.inverse = sem(f"{name}_inverse")
            k.mapped = sem(f"{name}_mapped")
            k.turned = sem(f"{name}_turned")
            k.map_hi = sem(f"{name}_map_hi")
            k.map_lo = sem(f"{name}_map_lo")
            k.summed = sem(f"{name}_summed")
            k.taken = sem(f"{name}_taken")
            return k

        da = attention_kind("da", 4, 2, DA_DIM ** -0.5, 2)
        ml = attention_kind("mla", 2, 2, (NOPE + ROPE) ** -0.5, 3)
        squared = sem("squared")
        ms_out = sem("ms_out")
        rms_ready = sem("rms_ready")
        rbc_ready = sem("rbc_ready")
        rbc_turned = sem("rbc_turned")
        normed = sem("normed")

        def heads_loop(eng, one_head):
            for p in range(2):
                one_head(p, p, p == 0)
            with eng.Fori(1, HEADS // 2 - 1) as i:
                for p in range(2):
                    one_head(2 * i + p, p, False)
            for p in range(2):
                one_head(HEADS - 2 + p, p, False)

        def sp_attention(sp, kd):
            def qk_of(h):
                if kd is da:
                    return [(q_raw[:], qkT_d[bass.ds(h * P, P), :]), (k_raw[:], qkT_d[bass.ds(h * P + QK_W, P), :])]
                return [(q_raw[:], qnT_d[bass.ds(h * P, P), :]), (k_raw[:], knT_d[bass.ds(h * P, P), :]),
                        (r_raw[:], qrT_d[bass.ds(h * ROPE, ROPE), :])]

            values = (va_d if kd is da else vb_d).rearrange("(t p) (h c) -> h p t c", p=P, c=P)
            if kd is ml:
                sp.wait_ge(da.hi, 2 * HEADS)
                sp.wait_ge(da.lo, 2 * HEADS)
            for dst, src in qk_of(0):
                sp.dma_start(dst, src).then_inc(kd.qk_in, 16)
            if kd is ml:
                sp.wait_ge(da.v_hi, HEADS)
                sp.wait_ge(da.v_lo, HEADS)
            sp.dma_start(v_raw[:], values[0]).then_inc(kd.v_in, 16)
            with sp.Fori(1, HEADS) as h:
                pairs, v = qk_of(h), values[bass.ds(h, 1)].rearrange("h p t c -> p (h t) c")
                split_ = sp.snap(kd.loads * h)
                sp.wait_ge(kd.hi, split_)
                sp.wait_ge(kd.lo, split_)
                for dst, src in pairs:
                    sp.dma_start(dst, src).then_inc(kd.qk_in, 16)
                sp.wait_ge(kd.v_lo, h)
                nc.sync.sem_inc(kd.v_seen, 1)
                sp.dma_start(v_raw[:], v).then_inc(kd.v_in, 16)
            sp.wait_ge(kd.v_seen, HEADS - 1)

        def raws(kd):
            return [q_raw, k_raw, r_raw][:kd.loads]

        def parts(kd, p):
            return [qs[p], ks[p], rs[p]][:kd.loads]

        def act_qk(act, kd, h, p, scored, count):
            act.wait_ge(kd.qk_in, 16 * kd.loads * (h + 1))
            if scored is not None:
                act.wait_ge(scored, count)
            for r, (hi, _) in zip(raws(kd), parts(kd, p)):
                nc.scalar.activation(hi[:], r[:], ACT.Copy).then_inc(kd.hi, 1)

        def act_v(act, kd, h, p):
            act.wait_ge(kd.v_in, 16 * (h + 1))
            if not early(h):
                act.wait_ge(kd.summed, 2 * (h - 1))
            elif kd is ml:
                act.wait_ge(da.summed, 2 * (HEADS - 1 + h))
            nc.scalar.activation(vs[p][0][:], v_raw[:], ACT.Copy).then_inc(kd.v_hi, 1)

        def early(h):
            return isinstance(h, int) and h < 2

        def next_qk(h, kd):
            if not isinstance(h, int) or h + 1 < HEADS:
                return kd, h + 1
            return (ml, 0) if kd is da else (None, 0)

        def pool_qk(pool, kd, h, p):
            for n, (r, (hi, lo)) in enumerate(zip(raws(kd), parts(kd, p))):
                pool.wait_ge(kd.hi, kd.loads * h + n + 1)
                nc.gpsimd.tensor_tensor(lo[:], r[:], hi[:].bitcast(F32), ALU.subtract).then_inc(kd.lo, 1)

        def pool_v(pool, kd, h, p):
            pool.wait_ge(kd.v_hi, h + 1)
            nc.gpsimd.tensor_tensor(vs[p][1][:], v_raw[:], vs[p][0][:].bitcast(F32), ALU.subtract).then_inc(kd.v_lo, 1)

        def pool_attention(pool):
            def one_da(h, p, first):
                pool_v(pool, da, h, p)
                kd, n = next_qk(h, da)
                pool_qk(pool, kd, n, 1 - p)

            def one_mla(h, p, first):
                if isinstance(h, int) and h == 1:
                    pool.wait_ge(ms_out, 1)
                    nc.gpsimd.tensor_tensor(msr[:], msr[:], half[:], ALU.pow).then_inc(rms_ready, 1)
                kd, n = next_qk(h, ml)
                if kd:
                    pool_qk(pool, ml, n, 1 - p)
                pool_v(pool, ml, h, p)

            pool_qk(pool, da, 0, 0)
            heads_loop(pool, one_da)
            heads_loop(pool, one_mla)

        def pe_scores(pe, kd, h, p, u, first):
            U = kd.units * h + u
            if u == 0:
                pe.wait_ge(kd.lo, kd.loads * (h + 1))
            if not first or u >= 2:
                pe.wait_ge(kd.exped, 2 * (U - 1))
            elif kd is ml:
                pe.wait_ge(da.exped, 2 * (4 * HEADS - 1 + u))
            (qh, ql), (kh, kl) = qs[p], ks[p]
            for j in range(2):
                o = ps[:, 2 * (u % 2) + j, :]
                if kd is da:
                    r, c = slice(DA_DIM * j, DA_DIM * (j + 1)), slice(P * u, P * (u + 1))
                    nc.tensor.matmul(o, qh[r, c], kh[r, :], start=True, stop=False)
                    nc.tensor.matmul(o, qh[r, c], kl[r, :], start=False, stop=False)
                    mm = nc.tensor.matmul(o, ql[r, c], kh[r, :], start=False, stop=True)
                else:
                    c = slice(P * (2 * u + j), P * (2 * u + j + 1))
                    rh, rl = rs[p]
                    nc.tensor.matmul(o, qh[:, c], kh[:], start=True, stop=False)
                    nc.tensor.matmul(o, qh[:, c], kl[:], start=False, stop=False)
                    nc.tensor.matmul(o, ql[:, c], kh[:], start=False, stop=False)
                    nc.tensor.matmul(o, rh[:, c], krT_hi[:], start=False, stop=False)
                    nc.tensor.matmul(o, rh[:, c], krT_lo[:], start=False, stop=False)
                    mm = nc.tensor.matmul(o, rl[:, c], krT_hi[:], start=False, stop=True)
            mm.then_inc(kd.scored, 1)

        def pe_turn(pe, kd, h, t, first):
            T = NT * h + t
            pe.wait_ge(kd.mapped, T + 1)
            if not first or t >= 2:
                pe.wait_ge(kd.map_lo, T - 1)
            elif kd is ml:
                pe.wait_ge(da.map_lo, NT * HEADS - 1 + t)
            for k in range(NT):
                mm = nc.tensor.transpose(ps[:, 4 + t % 2, k * P:(k + 1) * P], amap[:, t % 2, k * P:(k + 1) * P],
                                         ident[:])
            mm.then_inc(kd.turned, 1)

        def pe_values(pe, kd, h, p, half_, first):
            pe.wait_ge(kd.map_lo, NT * h + 2 * half_ + 2)
            if half_ == 0:
                pe.wait_ge(kd.v_lo, h + 1)
                if not first:
                    pe.wait_ge(kd.taken, 2 * h)
                elif kd is ml:
                    pe.wait_ge(da.taken, 2 * HEADS)
            vh, vl = vs[p]
            c = slice(2 * P * half_, 2 * P * (half_ + 1))
            for k in range(NT):
                nc.tensor.matmul(ps[:, 6, c], vh[:, k, :], aT_hi[:, k, c], start=k == 0, stop=False)
                nc.tensor.matmul(ps[:, 6, c], vh[:, k, :], aT_lo[:, k, c], start=False, stop=False)
                mm = nc.tensor.matmul(ps[:, 6, c], vl[:, k, :], aT_hi[:, k, c], start=False, stop=k == NT - 1)
            mm.then_inc(kd.summed, 1)

        def pe_squares(pe, h):
            pe.wait_ge(da.taken, 2 * (h + 1))
            for t in range(NT):
                mm = nc.tensor.matmul(ps[:, 7, bass.ds(NT * h + t, 1)], osq[:, t * P:(t + 1) * P], onec[:, 0:1],
                                      start=True, stop=True)
            mm.then_inc(squared, 1)

        def pe_rms(pe, h, first):
            pe.wait_ge(rbc_ready, h + 1)
            if not first:
                pe.wait_ge(normed, h)
            for t in range(NT):
                mm = nc.tensor.transpose(ps[:, 7, t * P:(t + 1) * P], rbc[:, t, :], ident[:])
            mm.then_inc(rbc_turned, 1)

        is1 = lambda h: isinstance(h, int) and h == 1
        last = HEADS - 1

        def pe_attention(pe):
            def one_da(h, p, first):
                pe_scores(pe, da, h, p, 0, first)
                if not first:
                    pe_turn(pe, da, h - 1, 2, False)
                    pe_values(pe, da, h - 1, 1 - p, 0, is1(h))
                pe_scores(pe, da, h, p, 1, first)
                if not first:
                    pe_turn(pe, da, h - 1, 3, False)
                pe_scores(pe, da, h, p, 2, first)
                pe_turn(pe, da, h, 0, first)
                if not first:
                    pe_values(pe, da, h - 1, 1 - p, 1, is1(h))
                pe_scores(pe, da, h, p, 3, first)
                pe_turn(pe, da, h, 1, first)
                if not first:
                    pe_squares(pe, h - 1)

            def one_mla(h, p, first):
                pe_scores(pe, ml, h, p, 0, first)
                if first:
                    pe_turn(pe, da, last, 2, False)
                    pe_values(pe, da, last, 1, 0, False)
                    pe_turn(pe, da, last, 3, False)
                else:
                    pe_turn(pe, ml, h - 1, 2, False)
                    pe_turn(pe, ml, h - 1, 3, False)
                    pe_values(pe, ml, h - 1, 1 - p, 0, is1(h))
                pe_scores(pe, ml, h, p, 1, first)
                if first:
                    pe_values(pe, da, last, 1, 1, False)
                pe_turn(pe, ml, h, 0, first)
                pe_turn(pe, ml, h, 1, first)
                if first:
                    pe_squares(pe, last)
                else:
                    pe_values(pe, ml, h - 1, 1 - p, 1, is1(h))
                    pe_rms(pe, h - 1, is1(h))

            heads_loop(pe, one_da)
            heads_loop(pe, one_mla)
            pe_turn(pe, ml, last, 2, False)
            pe_turn(pe, ml, last, 3, False)
            pe_values(pe, ml, last, 1, 0, False)
            pe_values(pe, ml, last, 1, 1, False)
            pe_rms(pe, last, False)

        def act_exp(act, kd, h, u, first):
            U = kd.units * h + u
            act.wait_ge(kd.biased, U + 1)
            if not first or u >= 2:
                act.wait_ge(kd.mapped, kd.items * (U - 1))
            elif kd is ml:
                act.wait_ge(da.mapped, NT * HEADS - 1 + u)
            for j in range(2):
                nc.scalar.activation(probs[:, u % 2, j, :], ps[:, 2 * (u % 2) + j, :], ACT.Exp,
                                     bias=soft[:, u % 2, 2 + j:3 + j], scale=kd.scale,
                                     accum_out=soft[:, u % 2, 4 + j:5 + j]).then_inc(kd.exped, 1)

        def act_map(act, kd, h, t, first):
            T = NT * h + t
            act.wait_ge(kd.turned, T + 1)
            if not first:
                act.wait_ge(kd.summed, 2 * h - (t < 2))
            elif kd is ml:
                act.wait_ge(da.summed, 2 * HEADS - (t < 2))
            nc.scalar.activation(aT_hi[:, :, t * P:(t + 1) * P], ps[:, 4 + t % 2, :].rearrange("p (k q) -> p k q", k=NT),
                                 ACT.Copy).then_inc(kd.map_hi, 1)

        def act_take(act, kd, h, first):
            act.wait_ge(kd.summed, 2 * (h + 1))
            if kd is da:
                nc.scalar.activation(oraw[:, h, :], ps[:, 6, :], ACT.Copy).then_inc(kd.taken, 1)
                if not first:
                    act.wait_ge(squared, h)
                nc.scalar.activation(osq[:], ps[:, 6, :], ACT.Square).then_inc(kd.taken, 1)
            else:
                nc.scalar.activation(om_hi[:, h, :], ps[:, 6, :], ACT.Copy).then_inc(kd.taken, 1)

        def act_attention(act):
            def act_next(kd, h, p):
                nk, n = next_qk(h, kd)
                if nk is None:
                    return
                if isinstance(h, int) and h == 0:
                    act_qk(act, nk, n, 1 - p, da.scored if kd is ml else None, 4 * HEADS)
                else:
                    act_qk(act, nk, n, 1 - p, kd.scored, kd.units * h)

            def one_da(h, p, first):
                if not first:
                    act_map(act, da, h - 1, 2, is1(h))
                act_exp(act, da, h, 0, first)
                act_v(act, da, h, p)
                if not first:
                    act_map(act, da, h - 1, 3, is1(h))
                act_exp(act, da, h, 1, first)
                act_next(da, h, p)
                act_map(act, da, h, 0, first)
                act_exp(act, da, h, 2, first)
                if not first:
                    act_take(act, da, h - 1, is1(h))
                act_map(act, da, h, 1, first)
                act_exp(act, da, h, 3, first)

            def one_mla(h, p, first):
                if first:
                    act_map(act, da, last, 2, False)
                    act_exp(act, ml, h, 0, first)
                    act_map(act, da, last, 3, False)
                else:
                    act_map(act, ml, h - 1, 2, is1(h))
                    act_map(act, ml, h - 1, 3, is1(h))
                    act_exp(act, ml, h, 0, first)
                act_next(ml, h, p)
                act_map(act, ml, h, 0, first)
                act_map(act, ml, h, 1, first)
                act_exp(act, ml, h, 1, first)
                act_v(act, ml, h, p)
                if first:
                    act_take(act, da, last, False)
                else:
                    act_take(act, ml, h - 1, is1(h))

            act_qk(act, da, 0, 0, None, 0)
            heads_loop(act, one_da)
            heads_loop(act, one_mla)
            act_map(act, ml, last, 2, False)
            act_map(act, ml, last, 3, False)
            act_take(act, ml, last, False)

        def dve_top(dve, kd, h, u):
            U = kd.units * h + u
            dve.wait_ge(kd.scored, U + 1)
            s = soft[:, u % 2, :]
            nc.vector.tensor_reduce(s[:, 0:2], ps[:, 2 * (u % 2):2 * (u % 2) + 2, :], AX_X, ALU.max).then_inc(kd.topped, 1)
            dve.wait_ge(kd.topped, U + 1)
            nc.vector.tensor_scalar(s[:, 2:4], s[:, 0:2], -kd.scale, None, ALU.mult).then_inc(kd.biased, 1)

        def dve_combine(dve, kd, h, u, first):
            U = kd.units * h + u
            s = soft[:, u % 2, :]
            pr = probs[:, u % 2, :, :]
            dve.wait_ge(kd.exped, 2 * (U + 1))
            nc.vector.reciprocal(s[:, 6:8], s[:, 4:6]).then_inc(kd.inverse, 1)
            if kd is da:
                T = U
                dve.wait_ge(kd.inverse, 3 * U + 1)
                nc.vector.tensor_tensor(s[:, 7:8], s[:, 7:8], lam[:, 5:6], ALU.mult).then_inc(kd.inverse, 1)
                dve.wait_ge(kd.inverse, 3 * U + 2)
                nc.vector.tensor_scalar(aterm[:], pr[:, 1, :], s[:, 7:8], None, ALU.mult).then_inc(kd.inverse, 1)
                dve.wait_ge(kd.inverse, 3 * U + 3)
                if not first or u >= 2:
                    dve.wait_ge(kd.turned, T - 1)
                nc.vector.scalar_tensor_tensor(amap[:, u % 2, :], pr[:, 0, :], s[:, 6:7], aterm[:], ALU.mult,
                                               ALU.add).then_inc(kd.mapped, 1)
            else:
                dve.wait_ge(kd.inverse, U + 1)
                for j in range(2):
                    T = 2 * U + j
                    if not first or u >= 1:
                        dve.wait_ge(kd.turned, T - 1)
                    elif kd is ml:
                        dve.wait_ge(da.turned, NT * HEADS)
                    nc.vector.tensor_scalar(amap[:, j, :], pr[:, j, :], s[:, 6 + j:7 + j], None,
                                            ALU.mult).then_inc(kd.mapped, 1)

        def dve_map(dve, kd, h, t):
            T = NT * h + t
            dve.wait_ge(kd.map_hi, T + 1)
            sl = slice(t * P, (t + 1) * P)
            nc.vector.tensor_tensor(aT_lo[:, :, sl], ps[:, 4 + t % 2, :].rearrange("p (k q) -> p k q", k=NT),
                                    aT_hi[:, :, sl].bitcast(F32), ALU.subtract).then_inc(kd.map_lo, 1)

        def dve_take(dve, h):
            dve.wait_ge(ml.taken, 2 * h + 1)
            nc.vector.tensor_tensor(om_lo[:, h, :], ps[:, 6, :], om_hi[:, h, :].bitcast(F32),
                                    ALU.subtract).then_inc(ml.taken, 1)

        def dve_repeat(dve, h, first):
            if first:
                dve.wait_ge(rms_ready, 1)
            else:
                dve.wait_ge(rbc_turned, h)
            nc.vector.tensor_copy(rbc[:], msr[:, bass.ds(NT * h, NT)].unsqueeze(2).to_broadcast([P, NT, P])
                                  ).then_inc(rbc_ready, 1)

        def dve_norm(dve, h):
            dve.wait_ge(rbc_turned, h + 1)
            nc.vector.tensor_tensor(oraw[:, h, :], oraw[:, h, :], ps[:, 7, :], ALU.mult).then_inc(normed, 1)

        def dve_attention(dve, link):
            def one_da(h, p, first):
                dve_top(dve, da, h, 0)
                if not first:
                    dve_combine(dve, da, h - 1, 3, False)
                    dve_map(dve, da, h - 1, 2)
                dve_top(dve, da, h, 1)
                dve_combine(dve, da, h, 0, first)
                if not first:
                    dve_map(dve, da, h - 1, 3)
                dve_top(dve, da, h, 2)
                dve_combine(dve, da, h, 1, first)
                dve_map(dve, da, h, 0)
                dve_top(dve, da, h, 3)
                dve_combine(dve, da, h, 2, first)
                dve_map(dve, da, h, 1)

            def one_mla(h, p, first):
                if first:
                    dve_top(dve, ml, h, 0)
                    dve_combine(dve, da, last, 3, False)
                    dve_map(dve, da, last, 2)
                    dve_map(dve, da, last, 3)
                else:
                    dve_combine(dve, ml, h - 1, 1, False)
                    if is1(h):
                        dve.wait_ge(squared, HEADS)
                        link(nc.vector.tensor_scalar(msr[:], ps[:, 7, 0:NT * HEADS], 1.0 / P, EPS, ALU.mult, ALU.add))
                        nc.vector.sem_inc(ms_out, 1)
                    else:
                        dve_take(dve, h - 2)
                        dve_norm(dve, h - 2)
                    dve_top(dve, ml, h, 0)
                    dve_map(dve, ml, h - 1, 2)
                    dve_map(dve, ml, h - 1, 3)
                dve_combine(dve, ml, h, 0, first)
                dve_top(dve, ml, h, 1)
                dve_map(dve, ml, h, 0)
                dve_map(dve, ml, h, 1)
                if not first:
                    dve_repeat(dve, h - 1, is1(h))

            heads_loop(dve, one_da)
            heads_loop(dve, one_mla)
            dve_combine(dve, ml, last, 1, False)
            dve_take(dve, last - 1)
            dve_norm(dve, last - 1)
            dve_repeat(dve, last, False)
            dve_map(dve, ml, last, 2)
            dve_map(dve, ml, last, 3)
            dve_take(dve, last)
            dve_norm(dve, last)

        oset_free = [sem("oset_free0"), sem("oset_free1")]
        od_hi_done = sem("od_hi_done")
        od_lo_done = sem("od_lo_done")
        gate_in = sem("gate_in")
        gate_used = sem("gate_used")
        x2_in = sem("x2_in")
        merged = sem("merged")
        m_hi = sem("m_hi")
        m_lo = sem("m_lo")
        resid_done = sem("resid_done")
        OJ = range(NPG, len(GROUPS))

        def sp_output(sp):
            for n, j in enumerate(OJ[:4]):
                row = GROUPS[j]["row"] + (D if GROUPS[j]["kind"] == "merge_b" else 0)
                if n == 0:
                    sp.wait_ge(ml.summed, 2 * HEADS)
                    sp.wait_ge(ml.map_lo, NT * HEADS)
                    sp.wait_ge(rbc_turned, HEADS)
                else:
                    sp.wait_ge(gate_used, n)
                sp.dma_start(gstage[:], gT_d[row:row + 512, :].rearrange("(f p) t -> p f t", p=P)).then_inc(gate_in, 16)
                if n == 0:
                    sp.dma_start(x2[:], x[0].rearrange("(t p) d -> p t d", p=P)).then_inc(x2_in, 16)
                for c in range(PCH + RAW + 2 * n, PCH + RAW + 2 * n + 2):
                    sp_chunk(sp, c)
            for c in range(PCH + RAW + 8, NCH):
                sp_chunk(sp, c)

        def pe_output(pe):
            pe.wait_ge(ml.taken, 2 * HEADS)
            pe.wait_ge(normed, HEADS)
            for j in OJ:
                k = GROUPS[j]["kind"]
                if j == NPG + 1:
                    pe.wait_ge(od_lo_done, 1)
                if k == "resid":
                    pe.wait_ge(m_lo, 2)
                pe_group(pe, j, oset_free)

        def act_output(act, link):
            act.wait_ge(ml.summed, 2 * HEADS)
            act.wait_ge(ml.map_lo, NT * HEADS)
            act.wait_ge(normed, HEADS)
            nc.scalar.activation(od_hi[:], oraw[:], ACT.Copy, scale=cols[:, GSUB:GSUB + 1]).then_inc(od_hi_done, 1)
            for j in OJ:
                if j > NPG:
                    for n in GROUPS[j]["chunks"]:
                        act_split(act, n)
                if j >= NPG + 2 and GROUPS[j - 1]["kind"] == "merge_a":
                    half_ = GROUPS[j - 1]["row"] // 512
                    act.wait_ge(merged, half_ + 1)
                    nc.scalar.activation(mT_hi[:, 4 * half_:4 * half_ + 4, :], mtmp[:], ACT.Copy).then_inc(m_hi, 1)

        def dve_output(dve, link):
            dve.wait_ge(od_hi_done, 1)
            nc.vector.scalar_tensor_tensor(od_lo[:], oraw[:], cols[:, GSUB:GSUB + 1], od_hi[:].bitcast(F32),
                                           ALU.mult, ALU.subtract).then_inc(od_lo_done, 1)
            dve.wait_ge(od_lo_done, 1)
            for j in list(OJ) + [len(GROUPS)]:
                if NPG < j < len(GROUPS):
                    for n in GROUPS[j]["chunks"]:
                        dve_split(dve, n)
                if j == NPG:
                    continue
                g, s = GROUPS[j - 1], (j - 1) % 2
                n = j - 1 - NPG
                wait_group(dve, j - 1)
                if g["kind"] == "merge_b":
                    dve.wait_ge(gate_in, 16 * (n + 1))
                    if n:
                        dve.wait_ge(m_lo, 1)
                    link(nc.vector.tensor_tensor(mtmp[:], bank_set(s), gstage[:], ALU.mult))
                    nc.vector.sem_inc(gate_used, 1)
                    nc.vector.sem_inc(oset_free[s], 1)
                elif g["kind"] == "merge_a":
                    half_ = g["row"] // 512
                    dve.wait_ge(gate_in, 16 * (n + 1))
                    link(nc.vector.tensor_tensor(gstage[:], bank_set(s), gstage[:], ALU.mult))
                    nc.vector.sem_inc(oset_free[s], 1)
                    link(nc.vector.tensor_tensor(mtmp[:], mtmp[:], gstage[:], ALU.add))
                    nc.vector.sem_inc(gate_used, 1)
                    nc.vector.sem_inc(merged, 1)
                    dve.wait_ge(m_hi, half_ + 1)
                    nc.vector.tensor_tensor(mT_lo[:, 4 * half_:4 * half_ + 4, :], mtmp[:],
                                            mT_hi[:, 4 * half_:4 * half_ + 4, :].bitcast(F32),
                                            ALU.subtract).then_inc(m_lo, 1)
                else:
                    dve.wait_ge(x2_in, 16)
                    r = g["row"]
                    link(nc.vector.tensor_tensor(x2[:, :, r:r + 512], x2[:, :, r:r + 512], bank_set(s), ALU.add))
                    nc.vector.sem_inc(resid_done, 1)

        table_set = sem("table_set")
        r_consts = sem("r_consts")
        b_in = sem("b_in")
        b_done = sem("b_done")
        b_hi_done = sem("b_hi_done")
        router_in = sem("router_in")
        x2_sums = sem("x2_sums")
        x2_mean = sem("x2_mean")
        x2_rms = sem("x2_rms")
        h2_ready = sem("h2_ready")
        h2_stored = sem("h2_stored")
        h2_turned = sem("h2_turned")
        h2_copied = sem("h2_copied")
        routed = sem("routed")
        shifted = sem("shifted")
        weighted = sem("weighted")
        picked = sem("picked")
        ranked = sem("ranked")
        rows_ready = sem("rows_ready")
        wd_ready = sem("wd_ready")
        wd_turned = sem("wd_turned")
        wdT_ready = sem("wdT_ready")
        bias_summed = sem("bias_summed")
        bias_added = sem("bias_added")
        listed = sem("listed")
        lists_in = sem("lists_in")
        m_raw_in = [sem(f"m_raw_in{i}") for i in range(MRAW)]
        m_hi_done = sem("m_hi_done")
        m_lo_done = sem("m_lo_done")
        m_used = sem("m_used")
        sel_ready = sem("sel_ready")
        sel_used = sem("sel_used")
        xe_in = sem("xe_in")
        x_turned = sem("x_turned")
        x_hi = sem("x_hi")
        x_lo = sem("x_lo")
        gate_taken = sem("gate_taken")
        sig_done = sem("sig_done")
        gated = sem("gated")
        up_taken = sem("up_taken")
        act_done = sem("act_done")
        a_turned = sem("a_turned")
        a_hi = sem("a_hi")
        a_lo = sem("a_lo")
        y_taken = sem("y_taken")
        scattered = sem("scattered")
        idx_step = sem("idx_step")
        y_in = [sem(f"y_in{t}") for t in range(NT)]
        y_added = sem("y_added")
        out_sums = sem("out_sums")
        out_mean = sem("out_mean")
        out_rms = sem("out_rms")
        out_ready = sem("out_ready")
        out_stored = sem("out_stored")

        wg_rows = w_gate[0].rearrange("e d f -> (e d) f")
        wu_rows = w_up[0].rearrange("e d f -> (e d) f")
        wd_rows = w_down[0].rearrange("e d f -> (e d) f")
        KPC = CH // D
        CPM = KD // KPC
        PER = 3 * CPM
        HEAD = 2 * CPM
        assert PER % MRAW == 0 and PER % MSPL == 0

        def chunk_no(g, c):
            return c if isinstance(g, int) and g == 0 else PER * g + (HEAD - PER) + c

        def slot_of(g, c, ring):
            return (c if isinstance(g, int) and g == 0 else c + HEAD - PER) % ring

        def landed_in(g, c):
            if isinstance(g, int) and g == 0:
                return 16 * (c // MRAW + 1)
            return 16 * ((PER // MRAW) * g + (HEAD - PER + c) // MRAW + 1)

        def rounds_of(eng):
            eng.wait_ge(rows_ready, 1)
            more = eng.value_load(further[0:1, 0:1], min_val=0, max_val=ROUNDS - 1)
            return eng.snap(more * E + E)

        def sp_matrix(sp, rows, e_row, g, c0):
            srcs = [rows[bass.ds(e_row + c * KPC * P, KPC * P), :].rearrange("(k p) f -> p k f", p=P)
                    for c in range(CPM)]
            for c in range(CPM):
                n = chunk_no(g, c0 + c)
                if not (isinstance(g, int) and g == 0 and c0 + c < MRAW):
                    sp.wait_ge(m_hi_done, n - MRAW + 1)
                    sp.wait_ge(m_lo_done, n - MRAW + 1)
                s = slot_of(g, c0 + c, MRAW)
                sp.dma_start(mraw[s][:].rearrange("p (k f) -> p k f", k=KPC), srcs[c]).then_inc(m_raw_in[s], 16)

        def sp_moe(sp):
            sp.wait_ge(m_lo, 2)
            sp.dma_start(gffn[:], g_ffn[0].partition_broadcast(P)).then_inc(router_in, 16)
            sp.dma_start(wr[:], w_router[0].rearrange("(k p) e -> p k e", p=P)).then_inc(router_in, 16)
            sp.dma_start(br[:], b_router[0].partition_broadcast(P)).then_inc(router_in, 16)
            sp.wait_ge(hi_done, NCH)
            sp.wait_ge(lo_done, NCH)
            sp.wait_ge(chunk_used, OG[4]["chunks"][0])
            sp.wait_ge(gate_used, 4)
            for c in range(MRAW):
                rows = wg_rows if c < CPM else wu_rows
                k = (c % CPM) * KPC * P
                sp.dma_start(mraw[c][:].rearrange("p (k f) -> p k f", k=KPC),
                             rows[k:k + KPC * P, :].rearrange("(k p) f -> p k f", p=P)).then_inc(m_raw_in[c], 16)
            sp.wait_ge(resid_done, 2)
            sp.dma_start(bdown[:], b_down[0]).then_inc(b_in, 16)
            for i in range(3):
                sp.dma_start(bsrc[32 * i:32 * i + 32, 0, :], b_gate[0]).then_inc(b_in, 16)
                sp.dma_start(bsrc[32 * i:32 * i + 32, 1, :], b_up[0]).then_inc(b_in, 16)
            sp.wait_ge(h2_ready, 1)
            sp.dma_start(h2_d.rearrange("(t p) d -> p t d", p=P), h2[:]).then_inc(h2_stored, 16)
            sp.wait_ge(listed, 16 * NT * TOPK)
            sp.dma_start(lists[:, 1:BLOCKS + 1, :], table_d.rearrange("(p b) f -> p b f", p=P)).then_inc(lists_in, 16)
            G = rounds_of(sp)
            for c in range(MRAW, HEAD):
                n = c
                sp.wait_ge(m_hi_done, n - MRAW + 1)
                sp.wait_ge(m_lo_done, n - MRAW + 1)
                k = (c % CPM) * KPC * P
                sp.dma_start(mraw[c % MRAW][:].rearrange("p (k f) -> p k f", k=KPC),
                             wu_rows[k:k + KPC * P, :].rearrange("(k p) f -> p k f", p=P)).then_inc(m_raw_in[c % MRAW], 16)
            with sp.Fori(1, G) as g:
                now = sp.snap((g % E) * D)
                before = sp.snap(((g - 1) % E) * D)
                sp_matrix(sp, wg_rows, now, g, 0)
                sp_matrix(sp, wu_rows, now, g, CPM)
                sp_matrix(sp, wd_rows, before, g, 2 * CPM)
            sp_matrix(sp, wd_rows, (E - 1) * D, G, 0)
            sp.wait_ge(m_used, chunk_no(G, CPM - 1) + 1)
            sp.dma_start(gfin[:], g_final.partition_broadcast(P)).then_inc(b_in, 16)
            sp.wait_ge(scattered, 16 * (G + 1))
            yv = y_d.rearrange("(t p k) d -> t p k d", p=P, k=TOPK)
            for t in range(NT):
                sp.dma_start(ybuf[t][:], yv[t]).then_inc(y_in[t], 16)
            for t in range(NT):
                sp.wait_ge(out_ready, t + 1)
                sp.dma_start(out[0, t * P:(t + 1) * P, :], x2[:, t, :]).then_inc(out_stored, 16)
            sp.wait_ge(out_stored, 16 * NT)

        def act_moe(act, link):
            act.wait_ge(resid_done, 2)
            for t in range(NT):
                nc.scalar.activation(h2[:, t, :], x2[:, t, :], ACT.Square, accum_out=stat[:, t:t + 1]).then_inc(x2_sums, 1)
            for k in range(0, KD, 4):
                act.wait_ge(h2_turned, k // 4 + 1)
                nc.scalar.activation(h2T[:, k:k + 4, :], ps[:, k:k + 4, :], ACT.Copy).then_inc(h2_copied, 1)
            act.wait_ge(shifted, 1)
            nc.scalar.activation(wexp[:], wexp[:], ACT.Exp).then_inc(weighted, 1)
            act.wait_ge(wd_turned, 1)
            nc.scalar.activation(wdT[:], ps[0:E, 2, :], ACT.Copy).then_inc(wdT_ready, 1)
            G = rounds_of(act)

            def split(g, c):
                n = chunk_no(g, c)
                act.wait_ge(m_raw_in[slot_of(g, c, MRAW)], landed_in(g, c))
                if isinstance(g, int) and g == 0 and c < MSPL:
                    act.wait_ge(chunk_used, NCH)
                    if c == 2:
                        act.wait_ge(h2_stored, 16)
                        act.wait_ge(h2_turned, 2)
                else:
                    act.wait_ge(m_used, n - MSPL + 1)
                nc.scalar.activation(mwhi[slot_of(g, c, MSPL)][:], mraw[slot_of(g, c, MRAW)][:], ACT.Copy).then_inc(m_hi_done, 1)

            def sigmoid(g):
                act.wait_ge(gate_taken, g + 1)
                nc.scalar.activation(sg[:], gg[:], ACT.Sigmoid, scale=ALPHA).then_inc(sig_done, 1)

            def take_x(g):
                act.wait_ge(x_turned, g + 1)
                nc.scalar.activation(xT_hi[:].rearrange("p k t -> p (k t)"), ps[:, 6:8, :].rearrange("p b n -> p (b n)"),
                                     ACT.Copy).then_inc(x_hi, 1)

            def take_act(g):
                act.wait_ge(a_turned, g + 1)
                nc.scalar.activation(aT2_hi[:].rearrange("p k t -> p (k t)"), ps[:, 6:8, :].rearrange("p b n -> p (b n)"),
                                     ACT.Copy).then_inc(a_hi, 1)

            def take_y(g, done):
                act.wait_ge(m_used, done)
                act.wait_ge(scattered, 16 * (g + 1))
                nc.scalar.activation(ye[:], ps[:, 4:6, :].rearrange("p b n -> p (b n)"), ACT.Copy,
                                     scale=lists[:, bass.ds(g + 1, 1), 2:3].rearrange("p a b -> p (a b)").bitcast(F32)
                                     ).then_inc(y_taken, 1)

            take_x(0)
            act.wait_ge(lists_in, 16)
            for c in range(HEAD):
                split(0, c)
            sigmoid(0)
            take_x(1)
            with act.Fori(1, G) as g:
                for c in range(PER):
                    split(g, c)
                    if c == 2:
                        take_act(g - 1)
                        take_y(g - 2, chunk_no(g, 0))
                    if c == 7:
                        sigmoid(g)
                    if c == 10:
                        take_x(g + 1)
            for c in range(CPM):
                split(G, c)
                if c == 2:
                    take_act(G - 1)
                    take_y(G - 2, chunk_no(G, 0))
            take_y(G - 1, chunk_no(G, CPM))
            for t in range(NT):
                act.wait_ge(y_added, t + 1)
                if t:
                    act.wait_ge(out_sums, t)
                nc.scalar.activation(fdump[:], x2[:, t, :], ACT.Square, accum_out=stat[:, 16 + t:17 + t]).then_inc(out_sums, 1)

        def dve_moe(dve, link):
            dve.wait_ge(x2_sums, NT)
            link(nc.vector.tensor_scalar(stat2[:, 0:NT], stat[:, 0:NT], 1.0 / D, EPS, ALU.mult, ALU.add))
            nc.vector.sem_inc(x2_mean, 1)
            dve.wait_ge(x2_rms, 1)
            dve.wait_ge(router_in, 48)
            for t in range(NT):
                link(nc.vector.scalar_tensor_tensor(h2[:, t, :], x2[:, t, :], stat2[:, t:t + 1], gffn[:], ALU.mult, ALU.mult))
            nc.vector.sem_inc(h2_ready, 1)
            dve.wait_ge(routed, 1)
            link(nc.vector.tensor_tensor(logits[:], ps[:, 0, 0:NT * E].rearrange("p (t e) -> p t e", t=NT),
                                         br[:].unsqueeze(1).to_broadcast([P, NT, E]), ALU.add))
            for t in range(NT):
                link(nc.vector.max(top8[:, t, :], logits[:, t, :]))
                link(nc.vector.max_index(idx8[:, t, :], top8[:, t, :], logits[:, t, :]))
                link(nc.vector.tensor_scalar(wexp[:, t, :], top8[:, t, :], top8[:, t, 0:1], None, ALU.subtract))
            nc.vector.sem_inc(shifted, 1)
            link(nc.vector.tensor_copy(idxf[:], idx8[:]))
            dve.wait_ge(r_consts, 6)
            for t in range(NT):
                link(nc.vector.tensor_tensor(pick[:, t], iota_e[:].unsqueeze(1).to_broadcast([P, TOPK, E]),
                                             idxf[:, t, 0:TOPK].unsqueeze(2).to_broadcast([P, TOPK, E]), ALU.is_equal))
                link(nc.vector.tensor_reduce(chosen[:, t, :], pick[:, t].rearrange("p k e -> p e k"), AX_X, ALU.add))
            link(nc.vector.tensor_copy(chosen_b[:], chosen[:]))
            nc.vector.sem_inc(picked, 1)
            dve.wait_ge(weighted, 1)
            link(nc.vector.tensor_reduce(stat2[:, 8:12], wexp[:, :, 0:TOPK], AX_X, ALU.add))
            link(nc.vector.reciprocal(stat2[:, 12:16], stat2[:, 8:12]))
            link(nc.vector.tensor_tensor(wexp[:, :, 0:TOPK], wexp[:, :, 0:TOPK],
                                         stat2[:, 12:16].unsqueeze(2).to_broadcast([P, NT, TOPK]), ALU.mult))
            link(nc.vector.tensor_copy(rec[:, :, 2:3].bitcast(F32).rearrange("p (t k) a -> p t (k a)", t=NT),
                                       wexp[:, :, 0:TOPK]))
            dve.wait_ge(ranked, 1)
            rank = ps[:, 1, 0:NT * E]
            flat = rowof[:].rearrange("p t e -> p (t e)")
            for r in range(1, ROUNDS):
                link(nc.vector.tensor_scalar(over[:, r, :], rank, float(P * r), float(E - P * BLOCKS), ALU.is_ge, ALU.mult))
            link(nc.vector.tensor_scalar(flat, rank, float(BLOCKS), None, ALU.mult))
            for r in range(1, ROUNDS):
                link(nc.vector.tensor_tensor(flat, flat, over[:, r, :], ALU.add))
            link(nc.vector.tensor_tensor(rowof[:], rowof[:], iota_e[:].unsqueeze(1).to_broadcast([P, NT, E]), ALU.add))
            for t in range(NT):
                link(nc.vector.tensor_tensor(ptmp[:, t], pick[:, t], rowof[:, t, :].unsqueeze(1).to_broadcast([P, TOPK, E]),
                                             ALU.mult))
            link(nc.vector.tensor_reduce(rowsel[:], ptmp[:].rearrange("p t k e -> p (t k) e"), AX_X, ALU.add))
            link(nc.vector.tensor_copy(rowidx[:], rowsel[:]))
            link(nc.vector.tensor_reduce(stat2[:, 16:17], ps[:, 1, NT * E:NT * E + E], AX_X, ALU.max))
            for r in range(1, ROUNDS):
                link(nc.vector.tensor_scalar(stat2[:, 16 + r:17 + r], stat2[:, 16:17], float(P * r), None, ALU.is_gt))
            link(nc.vector.tensor_reduce(stat2[:, 20:21], stat2[:, 17:16 + ROUNDS], AX_X, ALU.add))
            link(nc.vector.tensor_copy(further[:, 0:1], stat2[:, 20:21]))
            nc.vector.sem_inc(rows_ready, 1)
            for t in range(NT):
                link(nc.vector.tensor_tensor(ptmp[:, t], pick[:, t],
                                             wexp[:, t, 0:TOPK].unsqueeze(2).to_broadcast([P, TOPK, E]), ALU.mult))
                link(nc.vector.tensor_reduce(wdense[:, t, :], ptmp[:, t].rearrange("p k e -> p e k"), AX_X, ALU.add))
            nc.vector.sem_inc(wd_ready, 1)
            dve.wait_ge(b_in, 16 * 7)
            flatb = lambda b, i: b[32 * i:32 * i + 32].rearrange("p m f -> p (m f)")
            for i in range(3):
                for r in range(i):
                    link(nc.vector.tensor_copy(flatb(bpart, i), flatb(bsrc, i)))
                    link(nc.vector.tensor_tensor(flatb(bsrc, i), flatb(bsrc, i), flatb(bpart, i), ALU.subtract))
                link(nc.vector.tensor_copy(flatb(bpart, i), flatb(bsrc, i)))
            nc.vector.sem_inc(b_done, 1)
            for n in range(2):
                dve.wait_ge(bias_summed, n + 1)
                link(nc.vector.tensor_tensor(x2[:, :, 512 * n:512 * n + 512], x2[:, :, 512 * n:512 * n + 512],
                                             ps[:, 4:8, :], ALU.add))
                nc.vector.sem_inc(bias_added, 1)
            G = rounds_of(dve)

            def split(g, c):
                dve.wait_ge(m_hi_done, chunk_no(g, c) + 1)
                s, r = slot_of(g, c, MSPL), slot_of(g, c, MRAW)
                nc.vector.tensor_tensor(mwlo[s][:], mraw[r][:], mwhi[s][:].bitcast(F32), ALU.subtract).then_inc(m_lo_done, 1)

            def take_gate(g, used):
                dve.wait_ge(m_used, used)
                nc.vector.tensor_scalar(gg[:], ps[:, 0:2, :].rearrange("p b n -> p (b n)"), LIMIT, None,
                                        ALU.min).then_inc(gate_taken, 1)

            def gate_it(g):
                dve.wait_ge(sig_done, g + 1)
                nc.vector.tensor_tensor(gg[:], gg[:], sg[:], ALU.mult).then_inc(gated, 1)

            def take_up(g, used):
                dve.wait_ge(m_used, used)
                nc.vector.tensor_scalar(uu[:], ps[:, 2:4, :].rearrange("p b n -> p (b n)"), LIMIT, -LIMIT,
                                        ALU.min, ALU.max).then_inc(up_taken, 1)
                dve.wait_ge(up_taken, g + 1)
                dve.wait_ge(gated, g + 1)
                if not (isinstance(g, int) and g == 0):
                    dve.wait_ge(a_turned, g)
                nc.vector.scalar_tensor_tensor(ae[:], uu[:], 1.0, gg[:], ALU.add, ALU.mult).then_inc(act_done, 1)

            def take_x(g):
                dve.wait_ge(x_hi, g + 1)
                nc.vector.tensor_tensor(xT_lo[:].rearrange("p k t -> p (k t)"), ps[:, 6:8, :].rearrange("p b n -> p (b n)"),
                                        xT_hi[:].rearrange("p k t -> p (k t)").bitcast(F32), ALU.subtract).then_inc(x_lo, 1)

            def take_act(g):
                dve.wait_ge(a_hi, g + 1)
                nc.vector.tensor_tensor(aT2_lo[:].rearrange("p k t -> p (k t)"), ps[:, 6:8, :].rearrange("p b n -> p (b n)"),
                                        aT2_hi[:].rearrange("p k t -> p (k t)").bitcast(F32), ALU.subtract).then_inc(a_lo, 1)

            take_x(0)
            for c in range(HEAD):
                split(0, c)
                if c == 6:
                    take_gate(0, CPM)
            gate_it(0)
            take_up(0, HEAD)
            take_x(1)
            with dve.Fori(1, G) as g:
                for c in range(PER):
                    split(g, c)
                    if c == 2:
                        take_act(g - 1)
                    if c == 6:
                        take_gate(g, chunk_no(g, CPM))
                    if c == 8:
                        gate_it(g)
                    if c == 10:
                        take_up(g, chunk_no(g, 2 * CPM))
                        take_x(g + 1)
            for c in range(CPM):
                split(G, c)
                if c == 2:
                    take_act(G - 1)
            for t in range(NT):
                dve.wait_ge(y_in[t], 16)
                for k in range(TOPK):
                    link(nc.vector.tensor_tensor(x2[:, t, :], x2[:, t, :], ybuf[t][:, k, :], ALU.add))
                nc.vector.sem_inc(y_added, 1)
            dve.wait_ge(b_in, 16 * 8)
            for t in range(NT):
                dve.wait_ge(out_sums, t + 1)
                link(nc.vector.tensor_scalar(stat2[:, t:t + 1], stat[:, 16 + t:17 + t], 1.0 / D, EPS, ALU.mult, ALU.add))
                nc.vector.sem_inc(out_mean, 1)
                dve.wait_ge(out_rms, t + 1)
                link(nc.vector.scalar_tensor_tensor(x2[:, t, :], x2[:, t, :], stat2[:, t:t + 1], gfin[:], ALU.mult, ALU.mult))
                nc.vector.sem_inc(out_ready, 1)

        def pool_moe(pool):
            pool.wait_ge(x2_mean, 1)
            nc.gpsimd.tensor_tensor(stat2[:, 0:NT], stat2[:, 0:NT], half[:, 0:NT], ALU.pow).then_inc(x2_rms, 1)
            nc.gpsimd.iota(iota_e[:], [[1, E]], base=0, channel_multiplier=0,
                           allow_small_or_imprecise_dtypes=True).then_inc(r_consts, 1)
            nc.gpsimd.memset(allone[:], 1.0).then_inc(r_consts, 1)
            pool.wait_ge(r_consts, 2)
            nc.gpsimd.affine_select(out=upper[:], in_=allone[:], compare_op=ALU.is_gt, fill=0.0, base=0,
                                    pattern=[[1, P]], channel_multiplier=-1).then_inc(r_consts, 1)
            nc.gpsimd.memset(rec[:], 0).then_inc(r_consts, 1)
            pool.wait_ge(r_consts, 4)
            nc.gpsimd.iota(rec[:, :, 0:1].rearrange("p (t k) a -> p t (k a)", t=NT), [[P * TOPK, NT], [1, TOPK]], base=0,
                           channel_multiplier=TOPK).then_inc(r_consts, 1)
            nc.gpsimd.iota(rec[:, :, 1:2].rearrange("p (t k) a -> p t (k a)", t=NT), [[P, NT], [0, TOPK]], base=0,
                           channel_multiplier=1).then_inc(r_consts, 1)
            nc.gpsimd.memset(padrec[:], NOWHERE).then_inc(r_consts, 1)
            pool.wait_ge(r_consts, 7)
            nc.gpsimd.memset(padrec[:, :, 2:4], 0).then_inc(r_consts, 1)
            pool.wait_ge(r_consts, 8)
            pool.dma_start(table_d.rearrange("(p b) f -> p b f", p=P), padrec[:]).then_inc(table_set, 16)
            nc.gpsimd.memset(selid[:], 0.0).then_inc(r_consts, 1)
            pool.wait_ge(r_consts, 9)
            for i in range(3):
                pool.wait_ge(r_consts, 9 + i)
                nc.gpsimd.affine_select(out=selid[:], in_=selid[:], compare_op=ALU.not_equal, fill=1.0, base=-32 * i,
                                        pattern=[[-1, E]], channel_multiplier=1).then_inc(r_consts, 1)
            nc.gpsimd.memset(xe[:], 0.0).then_inc(r_consts, 1)
            pool.wait_ge(table_set, 16)
            pool.wait_ge(r_consts, 13)
            pool.wait_ge(rows_ready, 1)
            for i in range(NT * TOPK):
                pool.indirect_dma_start(out=table_d, out_offset=bass.IndirectOffsetOnAxis(ap=rowidx[:, i:i + 1].bitcast(U32), axis=0),
                                        in_=rec[:, i, :], in_offset=None).then_inc(listed, 16)
            nc.gpsimd.memset(lists[:, 0:BLOCKS + 2:BLOCKS + 1, :], NOWHERE).then_inc(idx_step, 1)
            pool.wait_ge(idx_step, 1)
            nc.gpsimd.memset(lists[:, 0:BLOCKS + 2:BLOCKS + 1, 2:4], 0).then_inc(idx_step, 1)
            pool.wait_ge(idx_step, 2)
            pool.wait_ge(lists_in, 16)
            pool.wait_ge(h2_stored, 16)
            G = rounds_of(pool)
            last_token = pool.to_reg(SEQ - 1)
            last_row = pool.to_reg(SEQ * TOPK - 1)

            def gather(g):
                nc.gpsimd.tensor_copy(gidx[:], lists[:, bass.ds(g + 1, 1), :].rearrange("p a b -> p (a b)")).then_inc(gidx_ready, 1)
                pool.wait_ge(gidx_ready, g + 1)
                nc.gpsimd.sem_inc(idx_seen, 1)
                pool.indirect_dma_start(out=xe[:], out_offset=None, in_=h2_d,
                                        in_offset=bass.IndirectOffsetOnAxis(ap=gidx[:, 1:2].bitcast(U32), axis=0),
                                        bounds_check=last_token, oob_is_err=False).then_inc(xe_in, 16)

            def select(g):
                e = g % E
                nc.gpsimd.tensor_copy(selb[:], selid[:, bass.ds(e, 1)].to_broadcast([96, P])).then_inc(sel_ready, 1)

            def scatter(g):
                before = 16 * (g + 1) if isinstance(g, int) else pool.snap(16 * (g + 1))
                pool.wait_ge(y_taken, g + 2)
                pool.wait_ge(scattered, before)
                nc.gpsimd.tensor_copy(sidx[:], lists[:, bass.ds(g + 1, 1), :].rearrange("p a b -> p (a b)")).then_inc(sidx_ready, 1)
                pool.wait_ge(sidx_ready, g + 2)
                nc.gpsimd.sem_inc(idx_seen, 1)
                pool.indirect_dma_start(out=y_d, out_offset=bass.IndirectOffsetOnAxis(ap=sidx[:, 0:1].bitcast(U32), axis=0),
                                        in_=ye[:], in_offset=None, bounds_check=last_row,
                                        oob_is_err=False).then_inc(scattered, 16)

            gather(0)
            select(0)
            pool.wait_ge(x_turned, 1)
            gather(1)
            pool.wait_ge(sel_used, 1)
            select(1)
            with pool.Fori(1, G) as g:
                pool.wait_ge(x_turned, g + 1)
                gather(g + 1)
                pool.wait_ge(sel_used, g + 1)
                select(g + 1)
                scatter(g - 2)
            scatter(G - 2)
            scatter(G - 1)
            pool.wait_ge(idx_seen, 2 * G + 2)
            for t in range(NT):
                pool.wait_ge(out_mean, t + 1)
                nc.gpsimd.tensor_tensor(stat2[:, t:t + 1], stat2[:, t:t + 1], half[:, 0:1], ALU.pow).then_inc(out_rms, 1)

        gidx_ready = sem("gidx_ready")
        sidx_ready = sem("sidx_ready")
        idx_seen = sem("idx_seen")

        def pe_moe(pe):
            pe.wait_ge(h2_ready, 1)
            pe.wait_ge(resid_done, 2)
            for k in range(KD):
                for t in range(NT):
                    mm = nc.tensor.transpose(ps[:, k, t * P:(t + 1) * P], h2[:, t, k * P:(k + 1) * P], ident[:])
                if k % 4 == 3:
                    mm.then_inc(h2_turned, 1)
            pe.wait_ge(router_in, 48)
            pe.wait_ge(h2_copied, 2)
            for t in range(NT):
                for k in range(KD):
                    mm = nc.tensor.matmul(ps[:, 0, t * E:(t + 1) * E], h2T[:, k, t * P:(t + 1) * P], wr[:, k, :],
                                          start=k == 0, stop=k == KD - 1)
            mm.then_inc(routed, 1)
            pe.wait_ge(picked, 1)
            pe.wait_ge(r_consts, 3)
            for t in range(NT):
                for s in range(t + 1):
                    nc.tensor.matmul(ps[:, 1, t * E:(t + 1) * E], upper[:] if s == t else allone[:], chosen_b[:, s, :],
                                     start=s == 0, stop=s == t)
            for s in range(NT):
                mm = nc.tensor.matmul(ps[:, 1, NT * E:NT * E + E], allone[:], chosen_b[:, s, :], start=s == 0,
                                      stop=s == NT - 1)
            mm.then_inc(ranked, 1)
            pe.wait_ge(wd_ready, 1)
            for t in range(NT):
                mm = nc.tensor.transpose(ps[0:E, 2, t * P:(t + 1) * P], wdense[:, t, :], ident[:])
            mm.then_inc(wd_turned, 1)
            pe.wait_ge(wdT_ready, 1)
            pe.wait_ge(b_in, 16 * 7)
            for n in range(2):
                if n:
                    pe.wait_ge(bias_added, n)
                for t in range(NT):
                    mm = nc.tensor.matmul(ps[:, 4 + t, :], wdT[:, t * P:(t + 1) * P], bdown[:, 512 * n:512 * n + 512],
                                          start=True, stop=True)
                mm.then_inc(bias_summed, 1)
            pe.wait_ge(bias_added, 2)
            pe.wait_ge(b_done, 1)
            G = rounds_of(pe)

            def turn_x(g):
                pe.wait_ge(xe_in, 16 * (g + 1))
                for k in range(KD):
                    mm = nc.tensor.transpose(ps[:, 6 + k // 4, (k % 4) * P:(k % 4 + 1) * P], xe[:, k * P:(k + 1) * P], ident[:])
                mm.then_inc(x_turned, 1)

            def turn_act(g):
                pe.wait_ge(act_done, g + 1)
                pe.wait_ge(x_lo, g + 2)
                for k in range(KD):
                    mm = nc.tensor.transpose(ps[:, 6 + k // 4, (k % 4) * P:(k % 4 + 1) * P], ae[:, k * P:(k + 1) * P], ident[:])
                mm.then_inc(a_turned, 1)

            def product(g, c0, hi, lo, bank, bias):
                if bias is not None:
                    for n in range(2):
                        mm = nc.tensor.matmul(ps[:, bank + n, :], selb[:], bpart[:, bias, 512 * n:512 * n + 512],
                                              start=True, stop=False)
                    if bias == 1:
                        mm.then_inc(sel_used, 1)
                for c in range(CPM):
                    pe.wait_ge(m_lo_done, chunk_no(g, c0 + c) + 1)
                    s = slot_of(g, c0 + c, MSPL)
                    for kk in range(KPC):
                        k = c * KPC + kk
                        first = bias is None and k == 0
                        last = k == KD - 1
                        for w, l in ((mwhi, False), (mwlo, False)):
                            for n in range(2):
                                nc.tensor.matmul(ps[:, bank + n, :], hi[:, k, :], w[s][:, kk * D + 512 * n:kk * D + 512 * n + 512],
                                                 start=first and w is mwhi, stop=False)
                        for n in range(2):
                            mm = nc.tensor.matmul(ps[:, bank + n, :], lo[:, k, :],
                                                  mwhi[s][:, kk * D + 512 * n:kk * D + 512 * n + 512],
                                                  start=False, stop=last)
                    mm.then_inc(m_used, 1)

            def gate_up(g):
                pe.wait_ge(x_lo, g + 1)
                pe.wait_ge(sel_ready, g + 1)
                if not (isinstance(g, int) and g == 0):
                    pe.wait_ge(gate_taken, g)
                product(g, 0, xT_hi, xT_lo, 0, 0)
                if not (isinstance(g, int) and g == 0):
                    pe.wait_ge(up_taken, g)
                product(g, CPM, xT_hi, xT_lo, 2, 1)

            def down(g, at_step, c0):
                pe.wait_ge(a_lo, g + 1)
                pe.wait_ge(y_taken, g + 1)
                product(at_step, c0, aT2_hi, aT2_lo, 4, None)

            turn_x(0)
            gate_up(0)
            turn_x(1)
            with pe.Fori(1, G) as g:
                turn_act(g - 1)
                gate_up(g)
                pe.wait_ge(a_lo, g)
                turn_x(g + 1)
                down(g - 1, g, 2 * CPM)
            turn_act(G - 1)
            down(G - 1, G, 0)

        def sp_rest(sp):
            for s in range(2):
                sp.wait_ge(stored[s], 16 * ((len(STORES) - s + 1) // 2))
            sp_attention(sp, da)
            sp_attention(sp, ml)
            sp_output(sp)
            if debug == "O":
                sp.wait_ge(resid_done, 2)
                sp.dma_start(out[0].rearrange("(t p) d -> p t d", p=P), x2[:]).then_inc(x2_in, 16)
                sp.wait_ge(x2_in, 32)
                return
            sp_moe(sp)

        def pool_rest(pool):
            pool_attention(pool)
            if debug == "O":
                return
            pool_moe(pool)

        def act_rest(act, link):
            for n in GROUPS[NPG]["chunks"]:
                act_split(act, n)
            act_attention(act)
            act_output(act, link)
            if debug == "O":
                return
            act_moe(act, link)

        def dve_rest(dve, link):
            for n in GROUPS[NPG]["chunks"]:
                dve_split(dve, n)
            dve_attention(dve, link)
            dve_output(dve, link)
            if debug == "O":
                return
            dve_moe(dve, link)

        def pe_rest(pe):
            pe_attention(pe)
            pe_output(pe)
            if debug == "O":
                return
            pe_moe(pe)

        @block.sync
        def _(sp):
            sp_start(sp)
            for n in range(RAW, PCH + (0 if debug == "P" else RAW)):
                sp_chunk(sp, n)
            if debug == "P":
                return
            sp_rest(sp)

        @block.gpsimd
        def _(pool):
            nc.gpsimd.memset(half[:], -0.5).then_inc(pool_step, 1)
            nc.gpsimd.memset(onec[:], 1.0).then_inc(pool_step, 1)
            pool.wait_ge(pool_step, 2)
            pool.wait_ge(ss_ready, 1)
            nc.gpsimd.tensor_tensor(stat2[:, 0:4], stat2[:, 0:4], half[:, 0:4], ALU.pow).then_inc(rs_ready, 1)
            for j in STORES:
                g, n = PG[j], store_no[j]
                if n == store_no[LATE] - 4:
                    pool.wait_ge(ss_ready, 2)
                    nc.gpsimd.tensor_tensor(stat2[:, 8:16], stat2[:, 8:16], half[:, 0:8], ALU.pow).then_inc(rs_ready, 1)
                pool.wait_ge(stage_full, n + 1)
                st = ostage[n % 2]
                if g["kind"] == "rows":
                    dst = scratch[g["dst"]][:, g["row"]:g["row"] + 512].rearrange("(t p) c -> p t c", p=P)
                else:
                    dst = scratch[g["dst"]][g["row"]:g["row"] + 512, :].rearrange("(f p) t -> p f t", p=P)
                pool.dma_start(dst, st[:]).then_inc(stored[n % 2], 16)
            for s in range(2):
                pool.wait_ge(stored[s], 16 * ((len(STORES) - s + 1) // 2))
            if debug == "P":
                return
            pool_rest(pool)

        @block.scalar
        def _(act):
            step = [0]

            def link(ins):
                step[0] += 1
                ins.then_inc(act_step, 1)
                act.wait_ge(act_step, step[0])

            act.wait_ge(cols_turned, 1)
            nc.scalar.activation(cols[:, 0:NCOL], ps[:, 7, 0:NCOL], ACT.Copy).then_inc(cols_ready, 1)
            act.wait_ge(x_in, 16)
            for t in range(NT):
                ins = nc.scalar.activation(sq_dump[:], xrows[:, t, :], ACT.Square, accum_out=stat[:, t:t + 1])
                link(ins)
            act.wait_ge(rope_in, 1)
            a = lambda i: angles[:, i, :]
            link(nc.scalar.activation(sin[:].rearrange("p t f -> p (t f)"), a(2), ACT.Sin))
            link(nc.scalar.activation(cos[:].rearrange("p t f -> p (t f)"), a(3), ACT.Sin))
            act.wait_ge(rope_in, 2)
            link(nc.scalar.activation(lam[:, 2:4], lam[:, 0:2], ACT.Exp))
            for k in range(KD):
                act.wait_ge(turned, k + 1)
                nc.scalar.activation(hT_hi[:, k, :], ps[:, k, :], ACT.Copy, scale=cols[:, GM + k:GM + k + 1]).then_inc(h_hi, 1)
            turns = [KD]

            def finish(j):
                g = PG[j]
                s = j % 2
                wait_group(act, j)
                if g["kind"].startswith("rope"):
                    n = NROPE.index(j)
                    if n >= 1:
                        act.wait_ge(turned, KD + n + (NCT + 1 if j > LATE else 0))
                    nc.scalar.activation(rstage[:], bank_set(s), ACT.Copy).then_inc(rope_in, 1)
                elif g["kind"] == "latent":
                    nc.scalar.activation(cbuf[:, :, g["row"]:g["row"] + g["n"]], bank_set(s)[:, :, 0:g["n"]],
                                         ACT.Copy).then_inc(c_rows, 1)
                    act.wait_ge(c_rows, LAT.index(j) + 1)
                    nc.scalar.sem_inc(set_free[s], 1)
                    if j == LAT[-1]:
                        for t in range(NT):
                            link(nc.scalar.activation(sq_dump[:, 0:Q_LORA], cbuf[:, t, 0:Q_LORA], ACT.Square,
                                                      accum_out=stat[:, 8 + t:9 + t]))
                            link(nc.scalar.activation(sq_dump[:, 0:KV_LORA], cbuf[:, t, Q_LORA:Q_LORA + KV_LORA],
                                                      ACT.Square, accum_out=stat[:, 12 + t:13 + t]))
                        nc.scalar.sem_inc(c_rows, 1)
                elif g["kind"] == "gate":
                    wait_stage(act, j)
                    for f in range(4):
                        c = BG + g["row"] // P + f
                        ins = nc.scalar.activation(ostage[store_no[j] % 2][:, f, :], ps[:, 4 * s + f, :], ACT.Sigmoid,
                                                   bias=cols[:, c:c + 1])
                        link(ins)
                    nc.scalar.sem_inc(stage_full, 1)
                    nc.scalar.sem_inc(set_free[s], 1)
                else:
                    wait_stage(act, j)
                    link(nc.scalar.activation(ostage[store_no[j] % 2][:], bank_set(s), ACT.Copy))
                    nc.scalar.sem_inc(stage_full, 1)
                    nc.scalar.sem_inc(set_free[s], 1)

            def finish_turn(j):
                n = NROPE.index(j)
                act.wait_ge(turned, KD + n + 1 + (NCT + 1 if j > LATE else 0))
                wait_stage(act, j)
                link(nc.scalar.activation(ostage[store_no[j] % 2][:], bank_set(j % 2), ACT.Copy))
                nc.scalar.sem_inc(stage_full, 1)
                nc.scalar.sem_inc(set_free[j % 2], 1)

            for j in range(NPG + 2):
                if j < NPG:
                    if j == LATE:
                        finish(j - 1)
                        before = KD + len([r for r in NROPE if r < LATE])
                        for f in range(NCT + 1):
                            act.wait_ge(turned, before + f + 1)
                            if f < NCT:
                                c = GQ + f
                                nc.scalar.activation(cT_hi[:, f, :], ps[:, f % 8, :], ACT.Copy,
                                                     scale=cols[:, c:c + 1]).then_inc(c_hi, 1)
                            else:
                                nc.scalar.activation(krT_hi[:], ps[0:ROPE, f % 8, :], ACT.Copy).then_inc(c_hi, 1)
                    for n in PG[j]["chunks"]:
                        act_split(act, n)
                if j >= 2 and PG[j - 2]["kind"].startswith("rope"):
                    finish_turn(j - 2)
                if 1 <= j <= NPG and j != LATE:
                    finish(j - 1)
            if debug == "P":
                return
            act_rest(act, link)

        @block.vector
        def _(dve):
            step = [0]

            def link(ins):
                step[0] += 1
                ins.then_inc(dve_step, 1)
                dve.wait_ge(dve_step, step[0])

            a = lambda i: angles[:, i, :]
            dve.wait_ge(x_in, 16)
            dve.wait_ge(act_step, NT)
            link(nc.vector.tensor_scalar(stat2[:, 0:4], stat[:, 0:4], 1.0 / D, EPS, ALU.mult, ALU.add))
            nc.vector.sem_inc(ss_ready, 1)
            dve.wait_ge(rs_ready, 1)
            for t in range(NT):
                link(nc.vector.tensor_scalar(xrows[:, t, :], xrows[:, t, :], stat2[:, t:t + 1], None, ALU.mult))
            nc.vector.sem_inc(c_ready, 1)
            dve.wait_ge(consts_in, 16 * N_CONSTS)
            link(nc.vector.tensor_copy(posf[:], posi[:]))
            for t in range(NT):
                link(nc.vector.tensor_scalar(angles[:, 0, t * NF:(t + 1) * NF], invf[:], posf[:, t:t + 1], None, ALU.mult))
            MAGIC = 12582912.0
            TWO_PI = 2 * math.pi
            c1 = 6.28125
            c2 = float(np.float32(round((TWO_PI - c1) * 2 ** 21) / 2 ** 21))
            c3 = float(np.float32(TWO_PI - c1 - c2))
            link(nc.vector.tensor_scalar(a(1), a(0), 1.0 / TWO_PI, MAGIC, ALU.mult, ALU.add))
            link(nc.vector.tensor_scalar(a(1), a(1), -MAGIC, None, ALU.add))
            link(nc.vector.scalar_tensor_tensor(a(2), a(1), -c1, a(0), ALU.mult, ALU.add))
            link(nc.vector.scalar_tensor_tensor(a(2), a(1), -c2, a(2), ALU.mult, ALU.add))
            link(nc.vector.scalar_tensor_tensor(a(2), a(1), -c3, a(2), ALU.mult, ALU.add))
            link(nc.vector.tensor_scalar(a(3), a(2), math.pi / 2, None, ALU.add))
            link(nc.vector.tensor_scalar(a(4), a(3), math.pi, None, ALU.is_gt))
            link(nc.vector.scalar_tensor_tensor(a(3), a(4), -TWO_PI, a(3), ALU.mult, ALU.add))
            PI_IN = 3.1415925
            link(nc.vector.tensor_scalar(a(3), a(3), PI_IN, -PI_IN, ALU.min, ALU.max))
            link(nc.vector.tensor_scalar(a(2), a(2), PI_IN, -PI_IN, ALU.min, ALU.max))
            nc.vector.sem_inc(rope_in, 1)
            link(nc.vector.tensor_tensor(lamv[:, 4, :], lamv[:, 0, :], lamv[:, 1, :], ALU.mult))
            link(nc.vector.tensor_tensor(lamv[:, 5, :], lamv[:, 2, :], lamv[:, 3, :], ALU.mult))
            link(nc.vector.tensor_reduce(lam[:, 0:2], lamv[:, 4:6, :], AX_X, ALU.add))
            nc.vector.sem_inc(rope_in, 1)
            dve.wait_ge(cols_ready, 1)
            link(nc.vector.tensor_scalar(cols[:, GSUB:GSUB + 1], cols[:, GSUB:GSUB + 1], 1.0 - LAM_INIT, None, ALU.mult))
            dve.wait_ge(act_step, NT + 3)
            link(nc.vector.tensor_tensor(lam[:, 4:5], lam[:, 3:4], lam[:, 2:3], ALU.subtract))
            link(nc.vector.tensor_scalar(lam[:, 5:6], lam[:, 4:5], -LAM_INIT, None, ALU.add))
            for k in range(KD):
                dve.wait_ge(h_hi, k + 1)
                ins = nc.vector.scalar_tensor_tensor(hT_lo[:, k, :], ps[:, k, :], cols[:, GM + k:GM + k + 1],
                                                     hT_hi[:, k, :].bitcast(F32), ALU.mult, ALU.subtract)
                ins.then_inc(h_lo, 1)
                if k % 4 == 3:
                    dve.wait_ge(h_lo, k + 1)
                    nc.vector.sem_inc(set_free[k // 4], 1)

            def rotate(v, f0, nf, groups):
                n = NT * groups * nf
                c4 = cos[:, :, f0:f0 + nf].unsqueeze(2).to_broadcast([P, NT, groups, nf])
                s4 = sin[:, :, f0:f0 + nf].unsqueeze(2).to_broadcast([P, NT, groups, nf])
                x1, x2_ = v[:, :, :, 0:nf], v[:, :, :, nf:2 * nf]
                tm = [rtmp[:, i, 0:n].rearrange("p (t g f) -> p t g f", t=NT, g=groups) for i in range(4)]
                nc.vector.tensor_tensor(tm[0], x1, c4, ALU.mult).then_inc(dve_step, 1)
                nc.vector.tensor_tensor(tm[1], x2_, s4, ALU.mult).then_inc(dve_step, 1)
                nc.vector.tensor_tensor(tm[2], x2_, c4, ALU.mult).then_inc(dve_step, 1)
                nc.vector.tensor_tensor(tm[3], x1, s4, ALU.mult).then_inc(dve_step, 1)
                step[0] += 4
                dve.wait_ge(dve_step, step[0])
                nc.vector.tensor_tensor(x1, tm[0], tm[1], ALU.subtract).then_inc(dve_step, 1)
                nc.vector.tensor_tensor(x2_, tm[2], tm[3], ALU.add).then_inc(dve_step, 1)
                step[0] += 2
                dve.wait_ge(dve_step, step[0])

            def finish(j):
                g = PG[j]
                if g["kind"].startswith("rope"):
                    dve.wait_ge(rope_in, 2 + NROPE.index(j) + 1)
                    v = rstage[:].rearrange("p t (g c) -> p t g c", c=DA_DIM)
                    if g["kind"] == "rope_da":
                        rotate(v, 0, FH, 8)
                    else:
                        rotate(v, FH, FM, 8)
                    nc.vector.sem_inc(roped, 1)
                elif j == LAT[-1]:
                    dve.wait_ge(c_rows, len(LAT) + 1)
                    link(nc.vector.tensor_scalar(stat2[:, 8:12], stat[:, 8:12], 1.0 / Q_LORA, EPS, ALU.mult, ALU.add))
                    link(nc.vector.tensor_scalar(stat2[:, 12:16], stat[:, 12:16], 1.0 / KV_LORA, EPS, ALU.mult, ALU.add))
                    nc.vector.sem_inc(ss_ready, 1)
                    rotate(cbuf[:, :, Q_LORA + KV_LORA:].unsqueeze(2), FH, FM, 1)
                    dve.wait_ge(rs_ready, 2)
                    for t in range(NT):
                        link(nc.vector.tensor_scalar(cbuf[:, t, 0:Q_LORA], cbuf[:, t, 0:Q_LORA],
                                                     stat2[:, 8 + t:9 + t], None, ALU.mult))
                        link(nc.vector.tensor_scalar(cbuf[:, t, Q_LORA:Q_LORA + KV_LORA],
                                                     cbuf[:, t, Q_LORA:Q_LORA + KV_LORA],
                                                     stat2[:, 12 + t:13 + t], None, ALU.mult))
                    nc.vector.sem_inc(c_ready, 1)

            for j in range(NPG + 1):
                if j == LATE:
                    for f in range(NCT + 1):
                        dve.wait_ge(c_hi, f + 1)
                        if f < NCT:
                            c = GQ + f
                            ins = nc.vector.scalar_tensor_tensor(cT_lo[:, f, :], ps[:, f % 8, :], cols[:, c:c + 1],
                                                                 cT_hi[:, f, :].bitcast(F32), ALU.mult, ALU.subtract)
                        else:
                            ins = nc.vector.tensor_tensor(krT_lo[:], ps[0:ROPE, f % 8, :], krT_hi[:].bitcast(F32),
                                                          ALU.subtract)
                        ins.then_inc(c_lo, 1)
                        if f in (3, 7, NCT):
                            dve.wait_ge(c_lo, f + 1)
                            nc.vector.sem_inc(set_free[0 if f != 7 else 1], 1)
                if j < NPG:
                    for n in PG[j]["chunks"]:
                        dve_split(dve, n)
                if j >= 1:
                    finish(j - 1)
            if debug == "P":
                return
            dve_rest(dve, link)

        @block.tensor
        def _(pe):
            pe.wait_ge(consts_in, 16 * N_CONSTS)
            nc.tensor.transpose(ps[:, 7, 0:NCOL], crows[:], ident[0:NCOL, 0:NCOL]).then_inc(cols_turned, 1)
            pe.wait_ge(cols_ready, 1)
            pe.wait_ge(c_ready, 1)
            for k in range(KD):
                for t in range(NT):
                    mm = nc.tensor.transpose(ps[:, k, t * P:(t + 1) * P], xrows[:, t, k * P:(k + 1) * P], ident[:])
                mm.then_inc(turned, 1)
            pe.wait_ge(h_lo, KD)
            for j in range(NPG + 1):
                if j == LATE:
                    pe.wait_ge(c_ready, 2)
                    for f in range(NCT + 1):
                        if f == 0:
                            pe.wait_ge(set_free[0], used_before["c0"])
                        if f == 4:
                            pe.wait_ge(set_free[1], used_before["c1"])
                        if f == 8:
                            pe.wait_ge(set_free[0], used_before["c0"] + 1)
                        w = P if f < NCT else ROPE
                        for t in range(NT):
                            mm = nc.tensor.transpose(ps[0:w, f % 8, t * P:(t + 1) * P],
                                                     cbuf[:, t, f * P:f * P + w], ident[:])
                        mm.then_inc(turned, 1)
                    pe.wait_ge(c_lo, NCT + 1)
                if j < NPG:
                    pe_group(pe, j, set_free)
                if j >= 1 and PG[j - 1]["kind"].startswith("rope"):
                    i = j - 1
                    pe.wait_ge(roped, NROPE.index(i) + 1)
                    for f in range(4):
                        for t in range(NT):
                            mm = nc.tensor.transpose(ps[:, 4 * (i % 2) + f, t * P:(t + 1) * P],
                                                     rstage[:, t, f * P:(f + 1) * P], ident[:])
                    mm.then_inc(turned, 1)
            if debug == "P":
                return
            pe_rest(pe)


_INS = ["x", "positions", "g_mix", "w_in", "lam_q1", "lam_k1", "lam_q2", "lam_k2", "g_subln", "g_q", "g_kv",
        "w_uq", "w_ukv", "w_o_diff", "w_o_mla", "b_gates", "w_out", "g_ffn", "w_router", "b_router", "w_gate",
        "b_gate", "w_up", "b_up", "w_down", "b_down", "g_final"]


def kernel(**inputs):
    import concourse.bacc as bacc
    from concourse.bass_utils import run_bass_kernel_spmd

    nc = bacc.Bacc("TRN2", target_bir_lowering=False, num_devices=1)
    arrays = {name: np.ascontiguousarray(inputs[name]) for name in _INS}
    inv = [np.float32(THETA) ** (-np.arange(0, r, 2, dtype=np.float32) / r) for r in (DA_ROT, ROPE)]
    arrays["inv_freq"] = np.tile(np.concatenate(inv).astype(np.float32), (P, 1))
    arrays["identity"] = np.eye(P, dtype=np.float32)
    aps, feeds = {}, {}
    for name, a in arrays.items():
        feeds[f"in_{name}"] = a
        aps[name] = nc.dram_tensor(f"in_{name}", a.shape, mybir.dt.from_np(a.dtype), kind="ExternalInput").ap()
    out = nc.dram_tensor("out_0", (1, SEQ, D), F32, kind="ExternalOutput").ap()
    hybrid_encoder_layer(nc, out=out, **aps)
    r = run_bass_kernel_spmd(nc, [feeds], core_ids=[0])
    return r.results[0]["out_0"]
```

```python
import math
from contextlib import ExitStack

import numpy as np

import concourse.bass as bass
from concourse import mybir

F32 = mybir.dt.float32
F32R = mybir.dt.float32r
BF16 = mybir.dt.bfloat16
I32 = mybir.dt.int32
U32 = mybir.dt.uint32
ALU = mybir.AluOpType
ACT = mybir.ActivationFunctionType
AX_X = mybir.AxisListType.X

P = 128
SEQ = 512
D = 1024
HEADS = 8
DA_DIM = 64
DA_ROT = 16
Q_LORA = 768
KV_LORA = 512
NOPE = 128
ROPE = 64
E = 32
TOPK = 4
EPS = 1e-6
THETA = 500000.0
LAM_INIT = 0.8 - 0.6 * math.exp(-0.3 * 0)
ALPHA = 1.702
LIMIT = 7.0
QK_W = HEADS * 2 * DA_DIM
C_W = Q_LORA + KV_LORA + ROPE
C_COL = 3 * QK_W
G_COL = C_COL + C_W
IN_W = G_COL + 2 * D
NT = SEQ // P
KD = D // P
FH = DA_ROT // 2
FM = ROPE // 2
NF = FH + FM
NCT = (Q_LORA + KV_LORA) // P

ROUNDS = SEQ // P
BLOCKS = ROUNDS * E
NOWHERE = 1 << 14

RAW = 4
SPL = 2
MRAW = 12
MSPL = 3
CH = 2048


def groups_of_projection():
    g = []
    for n in range(2 * QK_W // 512):
        g.append(dict(w="w_in", col=512 * n, kt=KD, src="h", kind="rope_da", dst="qkT", row=512 * n, n=512))
    for n in range(QK_W // 512):
        g.append(dict(w="w_in", col=2 * QK_W + 512 * n, kt=KD, src="h", kind="rows", dst="va", row=512 * n, n=512))
    for c in range(0, C_W, 512):
        g.append(dict(w="w_in", col=C_COL + c, kt=KD, src="h", kind="latent", row=c, n=min(512, C_W - c)))
    for n in range(2 * D // 512):
        g.append(dict(w="w_in", col=G_COL + 512 * n, kt=KD, src="h", kind="gate", dst="gT", row=512 * n, n=512))
    for n in range(2):
        g.append(dict(w="uq_nope", col=4 * n, kt=Q_LORA // P, src="q", kind="cols", dst="qnT", row=512 * n, n=512))
    g.append(dict(w="uq_rope", col=0, kt=Q_LORA // P, src="q", kind="rope_mla", dst="qrT", row=0, n=512))
    for n in range(2):
        g.append(dict(w="ukv_nope", col=4 * n, kt=KV_LORA // P, src="kv", kind="cols", dst="knT", row=512 * n, n=512))
    for n in range(2):
        g.append(dict(w="ukv_v", col=4 * n, kt=KV_LORA // P, src="kv", kind="rows", dst="vb", row=512 * n, n=512))
    return g


def groups_of_output():
    g = []
    for n in range(2):
        g.append(dict(w="w_o_mla", col=512 * n, kt=KD, src="om", kind="merge_b", row=512 * n, n=512))
        g.append(dict(w="w_o_diff", col=512 * n, kt=KD, src="od", kind="merge_a", row=512 * n, n=512))
    for n in range(2):
        g.append(dict(w="w_out", col=512 * n, kt=KD, src="m", kind="resid", row=512 * n, n=512))
    return g


def hybrid_encoder_layer(nc, x, positions, g_mix, w_in, lam_q1, lam_k1, lam_q2, lam_k2, g_subln, g_q,
                         g_kv, w_uq, w_ukv, w_o_diff, w_o_mla, b_gates, w_out, g_ffn, w_router, b_router,
                         w_gate, b_gate, w_up, b_up, w_down, b_down, g_final, inv_freq, identity, out):
    PG = groups_of_projection()
    OG = groups_of_output()
    GROUPS = PG + OG
    NPG = len(PG)

    chunks = []
    for j, g in enumerate(GROUPS):
        per = 4 if g["kt"] % 4 == 0 else 3
        g["chunks"] = []
        for k0 in range(0, g["kt"], per):
            g["chunks"].append(len(chunks))
            chunks.append((j, k0, per))
    NCH = len(chunks)
    PCH = GROUPS[NPG]["chunks"][0]

    w2 = {
        "w_in": w_in[0], "w_o_mla": w_o_mla[0], "w_o_diff": w_o_diff[0], "w_out": w_out[0],
    }
    uq = w_uq[0].rearrange("(k p) (h c) -> p k h c", p=P, h=HEADS)
    ukv = w_ukv[0].rearrange("(k p) (h c) -> p k h c", p=P, h=HEADS)

    def chunk_parts(n):
        j, k0, per = chunks[n]
        g = GROUPS[j]
        c, w = g["col"], g["n"]
        dst = raw[n % RAW][:, 0:per * w].rearrange("p (k c) -> p k c", k=per)
        if g["w"] in w2:
            return [(w2[g["w"]].rearrange("(k p) c -> p k c", p=P)[:, k0:k0 + per, c:c + w], dst)]
        if g["w"] == "uq_nope":
            src = uq[:, k0:k0 + per, c:c + 4, 0:NOPE]
        elif g["w"] == "uq_rope":
            src = uq[:, k0:k0 + per, :, NOPE:]
        elif g["w"] == "ukv_nope":
            src = ukv[:, k0:k0 + per, c:c + 4, 0:NOPE]
        else:
            src = ukv[:, k0:k0 + per, c:c + 4, NOPE:]
        hh = src.shape[2]
        d4 = dst.rearrange("p k (h c) -> p k h c", h=hh)
        return [(src[:, k], d4[:, k]) for k in range(per)]

    qkT_d = nc.dram_tensor("qkT_scratch", [2 * QK_W, SEQ], F32).ap()
    qnT_d = nc.dram_tensor("qnT_scratch", [HEADS * NOPE, SEQ], F32).ap()
    knT_d = nc.dram_tensor("knT_scratch", [HEADS * NOPE, SEQ], F32).ap()
    qrT_d = nc.dram_tensor("qrT_scratch", [HEADS * ROPE, SEQ], F32).ap()
    gT_d = nc.dram_tensor("gT_scratch", [2 * D, SEQ], F32).ap()
    va_d = nc.dram_tensor("va_scratch", [SEQ, QK_W], F32).ap()
    vb_d = nc.dram_tensor("vb_scratch", [SEQ, HEADS * P], F32).ap()
    h2_d = nc.dram_tensor("h2_scratch", [SEQ, D], F32).ap()
    table_d = nc.dram_tensor("table_scratch", [BLOCKS * P, 4], I32).ap()
    y_d = nc.dram_tensor("y_scratch", [SEQ * TOPK, D], F32).ap()
    scratch = dict(qkT=qkT_d, qnT=qnT_d, knT=knT_d, qrT=qrT_d, gT=gT_d, va=va_d, vb=vb_d)

    base = (nc.sbuf_base + 63) // 64 * 64
    KB = 1024
    used = {}

    def at(name, kb, shape, dt=F32):
        used[name] = (kb, int(np.prod(shape[1:])) * (2 if dt == BF16 else 4) / KB)
        return nc.alloc_sbuf_tensor_at(name, shape, dt, offset=base + int(kb * KB))

    ident = at("ident", 0, [P, P])
    cos = at("cos", 0.5, [P, NT, NF])
    sin = at("sin", 1.125, [P, NT, NF])
    cols = at("cols", 1.75, [P, 48])
    GM, GQ, GKV, GSUB, BG, NCOL = 0, 8, 14, 18, 19, 35
    lam = at("lam", 2.0, [P, 8])
    stat = at("stat", 2.0625, [P, 32])
    stat2 = at("stat2", 2.25, [P, 32])
    half = at("half", 2.375, [P, 32])
    msr = at("msr", 2.5, [P, 32])
    soft = at("soft", 2.625, [P, 2, 8])
    onec = at("onec", 2.6875, [P, 4])
    further = at("further", 2.75, [P, 2], I32)
    krT_hi = at("krT_hi", 3, [ROPE, SEQ], F32R)
    krT_lo = at("krT_lo", 5, [ROPE, SEQ], F32R)
    raw = [at(f"raw{i}", 7 + 8 * i, [P, CH]) for i in range(RAW)]
    whi = [at(f"whi{i}", 39 + 8 * i, [P, CH], F32R) for i in range(SPL)]
    wlo = [at(f"wlo{i}", 55 + 8 * i, [P, CH], F32R) for i in range(SPL)]
    hT_hi = at("hT_hi", 71, [P, KD, SEQ], F32R)
    hT_lo = at("hT_lo", 87, [P, KD, SEQ], F32R)
    cbuf = at("cbuf", 103, [P, NT, C_W])
    cT_hi = at("cT_hi", 124, [P, NCT, SEQ], F32R)
    cT_lo = at("cT_lo", 144, [P, NCT, SEQ], F32R)
    rstage = at("rstage", 164, [P, NT, 512])
    ostage = [at(f"ostage{i}", 172 + 8 * i, [P, 4, 512]) for i in range(2)]
    xrows = at("xrows", 172, [P, NT, D])
    rtmp = at("rtmp", 188, [P, 4, NT * 8 * 32])
    angles = at("angles", 188, [P, 6, NT * NF])
    lamv = at("lamv", 200, [P, 6, DA_DIM])
    crows = at("crows", 201.5, [NCOL, P])
    posi = at("posi", 202.5, [P, NT], I32)
    posf = at("posf", 202.625, [P, NT])
    invf = at("invf", 202.75, [P, NF])
    sq_dump = at("sq_dump", 124, [P, D])
    om_hi = at("om_hi", 119, [P, HEADS, SEQ], F32R)
    om_lo = at("om_lo", 135, [P, HEADS, SEQ], F32R)
    oraw = at("oraw", 103, [P, HEADS, SEQ])
    q_raw = at("q_raw", 71, [P, SEQ])
    k_raw = at("k_raw", 73, [P, SEQ])
    v_raw = at("v_raw", 75, [P, NT, P])
    r_raw = at("r_raw", 77, [ROPE, SEQ])
    qs = [[at(f"q{s}{i}", 79 + 4 * i + 2 * (s == "lo"), [P, SEQ], F32R) for s in ("hi", "lo")] for i in range(2)]
    ks = [[at(f"k{s}{i}", 87 + 4 * i + 2 * (s == "lo"), [P, SEQ], F32R) for s in ("hi", "lo")] for i in range(2)]
    vs = [[at(f"v{s}{i}", 95 + 4 * i + 2 * (s == "lo"), [P, NT, P], F32R) for s in ("hi", "lo")] for i in range(2)]
    rs = [[at(f"r{s}{i}", 151 + 4 * i + 2 * (s == "lo"), [ROPE, SEQ], F32R) for s in ("hi", "lo")] for i in range(2)]
    probs = at("probs", 159, [P, 2, 2, SEQ])
    amap = at("amap", 167, [P, 2, SEQ])
    aterm = at("aterm", 203, [P, 2, SEQ])
    aT_hi = at("aT_hi", 173, [P, NT, SEQ], F32R)
    aT_lo = at("aT_lo", 181, [P, NT, SEQ], F32R)
    osq = at("osq", 189, [P, SEQ])
    mT_hi = at("mT_hi", 71, [P, KD, SEQ], F32R)
    mT_lo = at("mT_lo", 87, [P, KD, SEQ], F32R)
    od_hi = at("od_hi", 151, [P, HEADS, SEQ], F32R)
    od_lo = at("od_lo", 167, [P, HEADS, SEQ], F32R)
    gstage = at("gstage", 183, [P, 4, SEQ])
    x2 = at("x2", 191, [P, NT, D])
    mtmp = at("mtmp", 103, [P, 4, SEQ])
    rbc = at("rbc", 191, [P, NT, P])
    h2 = at("h2", 71, [P, NT, D])
    h2T = at("h2T", 87, [P, KD, SEQ])
    gffn = at("gffn", 103, [P, D])
    wr = at("wr", 107, [P, KD, E])
    br = at("br", 108, [P, E])
    logits = at("logits", 108.5, [P, NT, E])
    top8 = at("top8", 109, [P, NT, 8])
    idx8 = at("idx8", 109.125, [P, NT, 8], U32)
    idxf = at("idxf", 109.25, [P, NT, 8])
    wexp = at("wexp", 109.375, [P, NT, 8])
    iota_e = at("iota_e", 109.5, [P, E])
    pick = at("pick", 110, [P, NT, TOPK, E])
    chosen = at("chosen", 112, [P, NT, E])
    chosen_b = at("chosen_b", 112.5, [P, NT, E], BF16)
    upper = at("upper", 112.75, [P, P], BF16)
    allone = at("allone", 113, [P, P], BF16)
    wdense = at("wdense", 115.75, [P, NT, E])
    wdT = at("wdT", 116.25, [E, SEQ])
    logT = at("logT", 116.25, [E, SEQ])
    bdown = at("bdown", 118.25, [E, D])
    ptmp = at("ptmp", 122.25, [P, NT, TOPK, E])
    rowsel = at("rowsel", 124.25, [P, NT * TOPK])
    rowidx = at("rowidx", 124.375, [P, NT * TOPK], I32)
    rec = at("rec", 124.5, [P, NT * TOPK, 4], I32)
    bsrc = at("bsrc", 135, [96, 2, D])
    sq_half = at("sq_half", 127, [P, NT, 512])
    mcount = at("mcount", 99, [P, NT * TOPK])
    over_k = at("over_k", 99.125, [P, NT * TOPK])
    bpart = at("bpart", 127, [96, 2, D], BF16)
    selid = at("selid", 5.125, [96, E])
    padrec = at("padrec", 133, [P, BLOCKS, 4], I32)
    mraw = raw + [at(f"mraw{4 + i}", kb, [P, CH]) for i, kb in enumerate((175, 183, 143, 151, 159, 167, 135, 103))]
    EARLY = MRAW - 2
    mwhi = whi + [at("mwhi2", 71, [P, CH], F32R)]
    mwlo = wlo + [at("mwlo2", 79, [P, CH], F32R)]
    xT_hi = at("xT_hi", 119, [P, KD, P], F32R)
    xT_lo = at("xT_lo", 123, [P, KD, P], F32R)
    aT2_hi = at("aT2_hi", 111, [P, KD, P], F32R)
    aT2_lo = at("aT2_lo", 115, [P, KD, P], F32R)
    xe = at("xe", 131, [P, D])
    ye = at("ye", 99, [P, D])
    gg = at("gg", 87, [P, D])
    uu = at("uu", 91, [P, D])
    sg = uu
    ae = at("ae", 95, [P, D])
    lists = at("lists", 3, [P, BLOCKS + 2, 4], I32)
    gidx = at("gidx", 5.5, [P, 4], I32)
    sidx = at("sidx", 5.5625, [P, 4], I32)
    selb = at("selb", 5.25, [96, P], BF16)
    ybuf = [at(f"ybuf{i}", 7 + 16 * i, [P, TOPK, D]) for i in range(4)]
    gfin = at("gfin", 87, [P, D])
    fdump = at("fdump", 91, [P, D])

    ctx = ExitStack()
    with ctx:
        ps = ctx.enter_context(nc.psum_tensor("ps", [P, 8, 512], F32))

        def sem(name):
            return ctx.enter_context(nc.semaphore(name))

        consts_in = sem("consts_in")
        cols_turned = sem("cols_turned")
        cols_ready = sem("cols_ready")
        x_in = [sem(f"x_in{t}") for t in range(NT)]
        lam_in = sem("lam_in")
        angles_in = sem("angles_in")
        act_step = sem("act_step")
        dve_step = sem("dve_step")
        pool_step = sem("pool_step")
        raw_in = [sem(f"raw_in{i}") for i in range(RAW)]
        hi_done = sem("hi_done")
        lo_done = sem("lo_done")
        chunk_used = sem("chunk_used")
        set_free = [sem("set_free0"), sem("set_free1")]
        turned = sem("turned")
        rope_in = sem("rope_in")
        roped = sem("roped")
        stage_full = sem("stage_full")
        stored = [sem("stored0"), sem("stored1")]
        h_hi = sem("h_hi")
        h_lo = sem("h_lo")
        c_rows = sem("c_rows")
        c_ready = sem("c_ready")
        c_hi = sem("c_hi")
        c_lo = sem("c_lo")
        ss_ready = sem("ss_ready")
        rs_ready = sem("rs_ready")

        block = ctx.enter_context(nc.Block())

        bank_set = lambda s: ps[:, 4 * s:4 * s + 4, :]
        NROPE = [j for j, g in enumerate(PG) if g["kind"].startswith("rope")]
        LAT = [j for j, g in enumerate(PG) if g["kind"] == "latent"]
        LATE = [j for j, g in enumerate(PG) if g["src"] in ("q", "kv")][0]
        uses = [1, 1]
        used_before = {}
        for j in range(len(GROUPS)):
            if j == LATE:
                used_before["c0"], used_before["c1"] = uses[0], uses[1]
                uses[0] += 2
                uses[1] += 1
            if j == NPG:
                used_at_end = uses
                uses = [0, 0]
            used_before[j] = uses[j % 2]
            uses[j % 2] += 1
        STORES = [j for j, g in enumerate(PG) if "dst" in g]
        store_no = {j: n for n, j in enumerate(STORES)}

        def wait_stage(eng, j):
            n = store_no[j]
            if n >= 2:
                eng.wait_ge(stored[n % 2], 16 * (n // 2))

        def sp_chunk(sp, n):
            if n >= RAW:
                sp.wait_ge(hi_done, n - RAW + 1)
                sp.wait_ge(lo_done, n - RAW + 1)
            parts = chunk_parts(n)
            for src, dst in parts:
                sp.dma_start(dst, src).then_inc(raw_in[n % RAW], 16)

        landed = []
        per_slot = [0] * RAW
        for n in range(NCH):
            per_slot[n % RAW] += 16 * len(chunk_parts(n))
            landed.append(per_slot[n % RAW])

        def sp_start(sp):
            sp.dma_start(invf[:], inv_freq).then_inc(angles_in, 16)
            sp.dma_start(posi[:], positions[0].rearrange("(t p) -> p t", p=P), allow_slow_non_contiguous=True).then_inc(angles_in, 16)
            for t in range(NT):
                sp.dma_start(xrows[:, t, :], x[0, t * P:(t + 1) * P, :]).then_inc(x_in[t], 16)
            sp.dma_start(ident[:], identity).then_inc(consts_in, 16)
            sp.dma_start(crows[GM:GM + KD, :], g_mix[0].rearrange("(k p) -> k p", p=P)).then_inc(consts_in, 16)
            sp.dma_start(crows[GQ:GQ + 6, :], g_q[0].rearrange("(k p) -> k p", p=P)).then_inc(consts_in, 16)
            sp.dma_start(crows[GKV:GKV + 4, :], g_kv[0].rearrange("(k p) -> k p", p=P)).then_inc(consts_in, 16)
            sp.dma_start(crows[GSUB:GSUB + 1, :], g_subln[0].rearrange("(k p) -> k p", p=P)).then_inc(consts_in, 16)
            sp.dma_start(crows[BG:BG + 16, :], b_gates[0].rearrange("(k p) -> k p", p=P)).then_inc(consts_in, 16)
            for i, v in enumerate((lam_q1, lam_k1, lam_q2, lam_k2)):
                sp.dma_start(lamv[:, i, :], v[0].partition_broadcast(P)).then_inc(lam_in, 16)
            for n in range(RAW):
                sp_chunk(sp, n)

        N_CONSTS = 6

        def act_split(act, n):
            per, w = chunks[n][2], GROUPS[chunks[n][0]]["n"]
            act.wait_ge(raw_in[n % RAW], landed[n])
            if n >= SPL:
                act.wait_ge(chunk_used, n - SPL + 1)
            nc.scalar.activation(whi[n % SPL][:, 0:per * w], raw[n % RAW][:, 0:per * w], ACT.Copy).then_inc(hi_done, 1)

        def dve_split(dve, n):
            per, w = chunks[n][2], GROUPS[chunks[n][0]]["n"]
            dve.wait_ge(hi_done, n + 1)
            nc.vector.tensor_tensor(wlo[n % SPL][:, 0:per * w], raw[n % RAW][:, 0:per * w],
                                    whi[n % SPL][:, 0:per * w].bitcast(F32), ALU.subtract).then_inc(lo_done, 1)

        acts_of = {"h": (hT_hi, hT_lo, 0), "q": (cT_hi, cT_lo, 0), "kv": (cT_hi, cT_lo, Q_LORA // P),
                   "om": (om_hi, om_lo, 0), "od": (od_hi, od_lo, 0), "m": (mT_hi, mT_lo, 0)}
        free_sem = {}

        def pe_turn_rows(pe, i):
            pe.wait_ge(roped, NROPE.index(i) + 1)
            for f in range(4):
                for t in range(NT):
                    mm = nc.tensor.transpose(ps[:, 4 * (i % 2) + f, t * P:(t + 1) * P],
                                             rstage[:, t, f * P:(f + 1) * P], ident[:])
            mm.then_inc(turned, 1)

        def pe_group(pe, j, frees):
            g = GROUPS[j]
            hi, lo, off = acts_of[g["src"]]
            s = j % 2
            if used_before[j]:
                pe.wait_ge(frees[s], used_before[j])
            rows = g["kind"] in ("rope_da", "rope_mla", "rows", "latent", "resid")
            for n in g["chunks"]:
                _, k0, per = chunks[n]
                pe.wait_ge(lo_done, n + 1)
                if g["kind"] == "resid":
                    pe.wait_ge(m_lo, 1 if k0 + per <= KD // 2 else 2)
                wh = whi[n % SPL][:, 0:per * g["n"]].rearrange("p (k c) -> p k c", k=per)
                wl = wlo[n % SPL][:, 0:per * g["n"]].rearrange("p (k c) -> p k c", k=per)
                for kk in range(per):
                    k = k0 + kk
                    if j == 0:
                        pe.wait_ge(h_lo, k + 1)
                    first, last = k == 0, k == g["kt"] - 1
                    for t in range(4):
                        if rows:
                            o = ps[:, 4 * s + t, 0:g["n"]]
                            ah = hi[:, off + k, t * P:(t + 1) * P]
                            al = lo[:, off + k, t * P:(t + 1) * P]
                            nc.tensor.matmul(o, ah, wh[:, kk, :], start=first, stop=False)
                            nc.tensor.matmul(o, ah, wl[:, kk, :], start=False, stop=False)
                            mm = nc.tensor.matmul(o, al, wh[:, kk, :], start=False, stop=last)
                        else:
                            o = ps[:, 4 * s + t, :]
                            a_h, a_l = hi[:, off + k, :], lo[:, off + k, :]
                            w_h, w_l = wh[:, kk, t * P:(t + 1) * P], wl[:, kk, t * P:(t + 1) * P]
                            nc.tensor.matmul(o, w_h, a_h, start=first, stop=False)
                            nc.tensor.matmul(o, w_h, a_l, start=False, stop=False)
                            mm = nc.tensor.matmul(o, w_l, a_h, start=False, stop=last)
                mm.then_inc(chunk_used, 1)
                if n == g["chunks"][0] and j - 1 in NROPE:
                    pe_turn_rows(pe, j - 1)

        def wait_group(eng, j):
            eng.wait_ge(chunk_used, GROUPS[j]["chunks"][-1] + 1)

        class Kind:
            pass

        v_seen = sem("v_seen")

        def attention_kind(name, units, score_tiles, scale, loads):
            k = Kind()
            k.name, k.units, k.scale, k.loads = name, units, scale, loads
            k.items = NT // units
            k.qk_in = sem(f"{name}_qk_in")
            k.v_in = sem(f"{name}_v_in")
            k.hi = sem(f"{name}_hi")
            k.lo = sem(f"{name}_lo")
            k.v_hi = sem(f"{name}_v_hi")
            k.v_lo = sem(f"{name}_v_lo")
            k.scored = sem(f"{name}_scored")
            k.topped = sem(f"{name}_topped")
            k.biased = sem(f"{name}_biased")
            k.exped = sem(f"{name}_exped")
            k.inverse = sem(f"{name}_inverse")
            k.mapped = sem(f"{name}_mapped")
            k.turned = sem(f"{name}_turned")
            k.map_hi = sem(f"{name}_map_hi")
            k.map_lo = sem(f"{name}_map_lo")
            k.summed = sem(f"{name}_summed")
            k.taken = sem(f"{name}_taken")
            return k

        da = attention_kind("da", 4, 2, DA_DIM ** -0.5, 2)
        ml = attention_kind("mla", 2, 2, (NOPE + ROPE) ** -0.5, 3)
        termed = sem("termed")
        squared = sem("squared")
        ms_out = sem("ms_out")
        rms_ready = sem("rms_ready")
        rbc_ready = sem("rbc_ready")
        rbc_turned = sem("rbc_turned")
        normed = sem("normed")

        def heads_loop(eng, one_head):
            for p in range(2):
                one_head(p, p, p == 0)
            with eng.Fori(1, HEADS // 2 - 1) as i:
                for p in range(2):
                    one_head(2 * i + p, p, False)
            for p in range(2):
                one_head(HEADS - 2 + p, p, False)

        def sp_attention(sp, kd, first_only=False):
            def qk_of(h):
                if kd is da:
                    return [(q_raw[:], qkT_d[bass.ds(h * P, P), :]), (k_raw[:], qkT_d[bass.ds(h * P + QK_W, P), :])]
                return [(q_raw[:], qnT_d[bass.ds(h * P, P), :]), (k_raw[:], knT_d[bass.ds(h * P, P), :]),
                        (r_raw[:], qrT_d[bass.ds(h * ROPE, ROPE), :])]

            values = (va_d if kd is da else vb_d).rearrange("(t p) (h c) -> h p t c", p=P, c=P)
            def first_head():
                for dst, src in qk_of(0):
                    sp.dma_start(dst, src).then_inc(kd.qk_in, 16)
                if kd is ml:
                    sp.wait_ge(da.v_hi, HEADS)
                    sp.wait_ge(da.v_lo, HEADS)
                sp.dma_start(v_raw[:], values[0]).then_inc(kd.v_in, 16)

            if first_only:
                sp.wait_ge(chunk_used, PG[LATE]["chunks"][0])
                for s in range(2):
                    sp.wait_ge(stored[s], 16 * 3)
                first_head()
                return
            if kd is ml:
                for s in range(2):
                    sp.wait_ge(stored[s], 16 * ((len(STORES) - s + 1) // 2))
                sp.wait_ge(da.hi, 2 * HEADS)
                sp.wait_ge(da.lo, 2 * HEADS)
                first_head()
            with sp.Fori(1, HEADS) as h:
                pairs, v = qk_of(h), values[bass.ds(h, 1)].rearrange("h p t c -> p (h t) c")
                split_ = sp.snap(kd.loads * h)
                sp.wait_ge(kd.hi, split_)
                sp.wait_ge(kd.lo, split_)
                for dst, src in pairs:
                    sp.dma_start(dst, src).then_inc(kd.qk_in, 16)
                sp.wait_ge(kd.v_lo, h)
                nc.sync.sem_inc(v_seen, 1)
                sp.dma_start(v_raw[:], v).then_inc(kd.v_in, 16)
            sp.wait_ge(v_seen, (HEADS - 1) * (1 if kd is da else 2))

        def raws(kd):
            return [q_raw, k_raw, r_raw][:kd.loads]

        def parts(kd, p):
            return [qs[p], ks[p], rs[p]][:kd.loads]

        def act_qk(act, kd, h, p, scored, count):
            act.wait_ge(kd.qk_in, 16 * kd.loads * (h + 1))
            if scored is not None:
                act.wait_ge(scored, count)
            for r, (hi, _) in zip(raws(kd), parts(kd, p)):
                nc.scalar.activation(hi[:], r[:], ACT.Copy).then_inc(kd.hi, 1)

        def act_v(act, kd, h, p):
            act.wait_ge(kd.v_in, 16 * (h + 1))
            if not early(h):
                act.wait_ge(kd.summed, 2 * (h - 1))
            elif kd is ml:
                act.wait_ge(da.summed, 2 * (HEADS - 1 + h))
            nc.scalar.activation(vs[p][0][:], v_raw[:], ACT.Copy).then_inc(kd.v_hi, 1)

        def early(h):
            return isinstance(h, int) and h < 2

        def next_qk(h, kd):
            if not isinstance(h, int) or h + 1 < HEADS:
                return kd, h + 1
            return (ml, 0) if kd is da else (None, 0)

        def pool_qk(pool, kd, h, p):
            for n, (r, (hi, lo)) in enumerate(zip(raws(kd), parts(kd, p))):
                pool.wait_ge(kd.hi, kd.loads * h + n + 1)
                nc.gpsimd.tensor_tensor(lo[:], r[:], hi[:].bitcast(F32), ALU.subtract).then_inc(kd.lo, 1)

        def pool_v(pool, kd, h, p):
            pool.wait_ge(kd.v_hi, h + 1)
            nc.gpsimd.tensor_tensor(vs[p][1][:], v_raw[:], vs[p][0][:].bitcast(F32), ALU.subtract).then_inc(kd.v_lo, 1)

        def pool_attention(pool):
            def one_da(h, p, first):
                pool_v(pool, da, h, p)
                kd, n = next_qk(h, da)
                pool_qk(pool, kd, n, 1 - p)

            def one_mla(h, p, first):
                if isinstance(h, int) and h == 1:
                    pool.wait_ge(ms_out, 1)
                    nc.gpsimd.tensor_tensor(msr[:], msr[:], half[:], ALU.pow).then_inc(rms_ready, 1)
                kd, n = next_qk(h, ml)
                if kd:
                    pool_qk(pool, ml, n, 1 - p)
                pool_v(pool, ml, h, p)

            heads_loop(pool, one_da)
            heads_loop(pool, one_mla)

        def pe_scores(pe, kd, h, p, u, first):
            U = kd.units * h + u
            if u == 0:
                pe.wait_ge(kd.lo, kd.loads * (h + 1))
            if not first or u >= 2:
                pe.wait_ge(kd.exped, 2 * (U - 1))
            elif kd is ml:
                pe.wait_ge(da.exped, 2 * (4 * HEADS - 1 + u))
            (qh, ql), (kh, kl) = qs[p], ks[p]
            for j in range(2):
                o = ps[:, 2 * (u % 2) + j, :]
                if kd is da:
                    r, c = slice(DA_DIM * j, DA_DIM * (j + 1)), slice(P * u, P * (u + 1))
                    nc.tensor.matmul(o, qh[r, c], kh[r, :], start=True, stop=False)
                    nc.tensor.matmul(o, qh[r, c], kl[r, :], start=False, stop=False)
                    mm = nc.tensor.matmul(o, ql[r, c], kh[r, :], start=False, stop=True)
                else:
                    c = slice(P * (2 * u + j), P * (2 * u + j + 1))
                    rh, rl = rs[p]
                    nc.tensor.matmul(o, qh[:, c], kh[:], start=True, stop=False)
                    nc.tensor.matmul(o, qh[:, c], kl[:], start=False, stop=False)
                    nc.tensor.matmul(o, ql[:, c], kh[:], start=False, stop=False)
                    nc.tensor.matmul(o, rh[:, c], krT_hi[:], start=False, stop=False)
                    nc.tensor.matmul(o, rh[:, c], krT_lo[:], start=False, stop=False)
                    mm = nc.tensor.matmul(o, rl[:, c], krT_hi[:], start=False, stop=True)
            mm.then_inc(kd.scored, 1)

        def pe_turn(pe, kd, h, t, first):
            T = NT * h + t
            pe.wait_ge(kd.mapped, T + 1)
            if not first or t >= 2:
                pe.wait_ge(kd.map_lo, T - 1)
            elif kd is ml:
                pe.wait_ge(da.map_lo, NT * HEADS - 1 + t)
            for k in range(NT):
                mm = nc.tensor.transpose(ps[:, 4 + t % 2, k * P:(k + 1) * P], amap[:, t % 2, k * P:(k + 1) * P],
                                         ident[:])
            mm.then_inc(kd.turned, 1)

        def pe_values(pe, kd, h, p, half_, first):
            pe.wait_ge(kd.map_lo, NT * h + 2 * half_ + 2)
            if half_ == 0:
                pe.wait_ge(kd.v_lo, h + 1)
                if not first:
                    pe.wait_ge(kd.taken, 2 * h)
                elif kd is ml:
                    pe.wait_ge(da.taken, 2 * HEADS)
            vh, vl = vs[p]
            c = slice(2 * P * half_, 2 * P * (half_ + 1))
            for k in range(NT):
                nc.tensor.matmul(ps[:, 6, c], vh[:, k, :], aT_hi[:, k, c], start=k == 0, stop=False)
                nc.tensor.matmul(ps[:, 6, c], vh[:, k, :], aT_lo[:, k, c], start=False, stop=False)
                mm = nc.tensor.matmul(ps[:, 6, c], vl[:, k, :], aT_hi[:, k, c], start=False, stop=k == NT - 1)
            mm.then_inc(kd.summed, 1)

        def pe_squares(pe, h):
            pe.wait_ge(da.taken, 2 * (h + 1))
            for t in range(NT):
                mm = nc.tensor.matmul(ps[:, 7, bass.ds(NT * h + t, 1)], osq[:, t * P:(t + 1) * P], onec[:, 0:1],
                                      start=True, stop=True)
            mm.then_inc(squared, 1)

        def pe_rms(pe, h, first):
            pe.wait_ge(rbc_ready, h + 1)
            if not first:
                pe.wait_ge(normed, h)
            for t in range(NT):
                mm = nc.tensor.transpose(ps[:, 7, t * P:(t + 1) * P], rbc[:, t, :], ident[:])
            mm.then_inc(rbc_turned, 1)

        is1 = lambda h: isinstance(h, int) and h == 1
        last = HEADS - 1

        def pe_attention(pe):
            for s in range(2):
                pe.wait_ge(set_free[s], used_at_end[s])

            def one_da(h, p, first):
                pe_scores(pe, da, h, p, 0, first)
                if not first:
                    pe_turn(pe, da, h - 1, 2, False)
                    pe_values(pe, da, h - 1, 1 - p, 0, is1(h))
                pe_scores(pe, da, h, p, 1, first)
                if not first:
                    pe_turn(pe, da, h - 1, 3, False)
                pe_scores(pe, da, h, p, 2, first)
                pe_turn(pe, da, h, 0, first)
                if not first:
                    pe_values(pe, da, h - 1, 1 - p, 1, is1(h))
                pe_scores(pe, da, h, p, 3, first)
                pe_turn(pe, da, h, 1, first)
                if not first:
                    pe_squares(pe, h - 1)

            def one_mla(h, p, first):
                pe_scores(pe, ml, h, p, 0, first)
                if first:
                    pe_turn(pe, da, last, 2, False)
                    pe_values(pe, da, last, 1, 0, False)
                    pe_turn(pe, da, last, 3, False)
                else:
                    pe_turn(pe, ml, h - 1, 2, False)
                    pe_turn(pe, ml, h - 1, 3, False)
                    pe_values(pe, ml, h - 1, 1 - p, 0, is1(h))
                pe_scores(pe, ml, h, p, 1, first)
                if first:
                    pe_values(pe, da, last, 1, 1, False)
                pe_turn(pe, ml, h, 0, first)
                pe_turn(pe, ml, h, 1, first)
                if first:
                    pe_squares(pe, last)
                else:
                    pe_values(pe, ml, h - 1, 1 - p, 1, is1(h))
                    pe_rms(pe, h - 1, is1(h))

            heads_loop(pe, one_da)
            heads_loop(pe, one_mla)
            pe_turn(pe, ml, last, 2, False)
            pe_turn(pe, ml, last, 3, False)
            pe_values(pe, ml, last, 1, 0, False)
            pe_values(pe, ml, last, 1, 1, False)
            pe_rms(pe, last, False)

        def act_exp(act, kd, h, u, first):
            U = kd.units * h + u
            act.wait_ge(kd.biased, U + 1)
            if not first or u >= 2:
                act.wait_ge(kd.mapped, kd.items * (U - 1))
            elif kd is ml:
                act.wait_ge(da.mapped, NT * HEADS - 1 + u)
            for j in range(2):
                nc.scalar.activation(probs[:, u % 2, j, :], ps[:, 2 * (u % 2) + j, :], ACT.Exp,
                                     bias=soft[:, u % 2, 2 + j:3 + j], scale=kd.scale,
                                     accum_out=soft[:, u % 2, 4 + j:5 + j]).then_inc(kd.exped, 1)

        def act_map(act, kd, h, t, first):
            T = NT * h + t
            act.wait_ge(kd.turned, T + 1)
            if not first:
                act.wait_ge(kd.summed, 2 * h - (t < 2))
            elif kd is ml:
                act.wait_ge(da.summed, 2 * HEADS - (t < 2))
            nc.scalar.activation(aT_hi[:, :, t * P:(t + 1) * P], ps[:, 4 + t % 2, :].rearrange("p (k q) -> p k q", k=NT),
                                 ACT.Copy).then_inc(kd.map_hi, 1)

        def act_take(act, kd, h, first):
            act.wait_ge(kd.summed, 2 * (h + 1))
            if kd is da:
                nc.scalar.activation(oraw[:, h, :], ps[:, 6, :], ACT.Copy).then_inc(kd.taken, 1)
                if not first:
                    act.wait_ge(squared, h)
                nc.scalar.activation(osq[:], ps[:, 6, :], ACT.Square).then_inc(kd.taken, 1)
            else:
                nc.scalar.activation(om_hi[:, h, :], ps[:, 6, :], ACT.Copy).then_inc(kd.taken, 1)

        def act_attention(act):
            def act_next(kd, h, p):
                nk, n = next_qk(h, kd)
                if nk is None:
                    return
                if isinstance(h, int) and h == 0:
                    act_qk(act, nk, n, 1 - p, da.scored if kd is ml else None, 4 * HEADS)
                else:
                    act_qk(act, nk, n, 1 - p, kd.scored, kd.units * h)

            def one_da(h, p, first):
                if not first:
                    act_term(act, h - 1, 3, False)
                    act_map(act, da, h - 1, 2, is1(h))
                if first:
                    for s in range(2):
                        act.wait_ge(stored[s], 16 * ((len(STORES) - s + 1) // 2))
                act_exp(act, da, h, 0, first)
                act_v(act, da, h, p)
                act_term(act, h, 0, first)
                if not first:
                    act_map(act, da, h - 1, 3, is1(h))
                act_exp(act, da, h, 1, first)
                act_next(da, h, p)
                act_term(act, h, 1, first)
                act_map(act, da, h, 0, first)
                act_exp(act, da, h, 2, first)
                if not first:
                    act_take(act, da, h - 1, is1(h))
                act_term(act, h, 2, first)
                act_map(act, da, h, 1, first)
                act_exp(act, da, h, 3, first)

            def one_mla(h, p, first):
                if first:
                    act_term(act, last, 3, False)
                    act_map(act, da, last, 2, False)
                    act_exp(act, ml, h, 0, first)
                    act_map(act, da, last, 3, False)
                else:
                    act_map(act, ml, h - 1, 2, is1(h))
                    act_map(act, ml, h - 1, 3, is1(h))
                    act_exp(act, ml, h, 0, first)
                act_next(ml, h, p)
                act_map(act, ml, h, 0, first)
                act_map(act, ml, h, 1, first)
                act_exp(act, ml, h, 1, first)
                act_v(act, ml, h, p)
                if first:
                    act_take(act, da, last, False)
                else:
                    act_take(act, ml, h - 1, is1(h))

            heads_loop(act, one_da)
            heads_loop(act, one_mla)
            act_map(act, ml, last, 2, False)
            act_map(act, ml, last, 3, False)
            act_split(act, GROUPS[NPG]["chunks"][0])
            act_take(act, ml, last, False)
            act_split(act, GROUPS[NPG]["chunks"][1])

        def dve_top(dve, kd, h, u):
            U = kd.units * h + u
            dve.wait_ge(kd.scored, U + 1)
            s = soft[:, u % 2, :]
            nc.vector.tensor_reduce(s[:, 0:2], ps[:, 2 * (u % 2):2 * (u % 2) + 2, :], AX_X, ALU.max).then_inc(kd.topped, 1)
            dve.wait_ge(kd.topped, U + 1)
            nc.vector.tensor_scalar(s[:, 2:4], s[:, 0:2], -kd.scale, None, ALU.mult).then_inc(kd.biased, 1)

        def dve_inverse(dve, h, u):
            U = da.units * h + u
            s = soft[:, u % 2, :]
            dve.wait_ge(da.exped, 2 * (U + 1))
            nc.vector.reciprocal(s[:, 6:8], s[:, 4:6]).then_inc(da.inverse, 1)
            dve.wait_ge(da.inverse, 2 * U + 1)
            nc.vector.tensor_tensor(s[:, 7:8], s[:, 7:8], lam[:, 5:6], ALU.mult).then_inc(da.inverse, 1)

        def act_term(act, h, u, first):
            U = da.units * h + u
            act.wait_ge(da.inverse, 2 * U + 2)
            if not first or u >= 2:
                act.wait_ge(da.mapped, U - 1)
            nc.scalar.activation(aterm[:, u % 2, :], probs[:, u % 2, 1, :], ACT.Copy,
                                 scale=soft[:, u % 2, 7:8]).then_inc(termed, 1)

        def dve_combine(dve, kd, h, u, first):
            U = kd.units * h + u
            s = soft[:, u % 2, :]
            pr = probs[:, u % 2, :, :]
            if kd is da:
                T = U
                dve.wait_ge(termed, U + 1)
                if not first or u >= 2:
                    dve.wait_ge(kd.turned, T - 1)
                nc.vector.scalar_tensor_tensor(amap[:, u % 2, :], pr[:, 0, :], s[:, 6:7], aterm[:, u % 2, :], ALU.mult,
                                               ALU.add).then_inc(kd.mapped, 1)
            else:
                dve.wait_ge(kd.exped, 2 * (U + 1))
                nc.vector.reciprocal(s[:, 6:8], s[:, 4:6]).then_inc(kd.inverse, 1)
                dve.wait_ge(kd.inverse, U + 1)
                for j in range(2):
                    T = 2 * U + j
                    if not first or u >= 1:
                        dve.wait_ge(kd.turned, T - 1)
                    elif kd is ml:
                        dve.wait_ge(da.turned, NT * HEADS)
                    nc.vector.tensor_scalar(amap[:, j, :], pr[:, j, :], s[:, 6 + j:7 + j], None,
                                            ALU.mult).then_inc(kd.mapped, 1)

        def dve_map(dve, kd, h, t):
            T = NT * h + t
            dve.wait_ge(kd.map_hi, T + 1)
            sl = slice(t * P, (t + 1) * P)
            nc.vector.tensor_tensor(aT_lo[:, :, sl], ps[:, 4 + t % 2, :].rearrange("p (k q) -> p k q", k=NT),
                                    aT_hi[:, :, sl].bitcast(F32), ALU.subtract).then_inc(kd.map_lo, 1)

        def dve_take(dve, h):
            dve.wait_ge(ml.taken, 2 * h + 1)
            nc.vector.tensor_tensor(om_lo[:, h, :], ps[:, 6, :], om_hi[:, h, :].bitcast(F32),
                                    ALU.subtract).then_inc(ml.taken, 1)

        def dve_repeat(dve, h, first):
            if first:
                dve.wait_ge(rms_ready, 1)
            else:
                dve.wait_ge(rbc_turned, h)
            nc.vector.tensor_copy(rbc[:], msr[:, bass.ds(NT * h, NT)].unsqueeze(2).to_broadcast([P, NT, P])
                                  ).then_inc(rbc_ready, 1)

        def dve_norm(dve, h):
            dve.wait_ge(rbc_turned, h + 1)
            nc.vector.tensor_tensor(oraw[:, h, :], oraw[:, h, :], ps[:, 7, :], ALU.mult).then_inc(normed, 1)

        def dve_attention(dve, link):
            def one_da(h, p, first):
                if not first:
                    dve_inverse(dve, h - 1, 3)
                dve_top(dve, da, h, 0)
                if not first:
                    dve_map(dve, da, h - 1, 2)
                    dve_combine(dve, da, h - 1, 3, False)
                dve_inverse(dve, h, 0)
                dve_top(dve, da, h, 1)
                if not first:
                    dve_map(dve, da, h - 1, 3)
                dve_combine(dve, da, h, 0, first)
                dve_inverse(dve, h, 1)
                dve_top(dve, da, h, 2)
                dve_map(dve, da, h, 0)
                dve_combine(dve, da, h, 1, first)
                dve_inverse(dve, h, 2)
                dve_top(dve, da, h, 3)
                dve_map(dve, da, h, 1)
                dve_combine(dve, da, h, 2, first)

            def one_mla(h, p, first):
                if first:
                    dve_inverse(dve, last, 3)
                    dve_top(dve, ml, h, 0)
                    dve_map(dve, da, last, 2)
                    dve_combine(dve, da, last, 3, False)
                    dve_map(dve, da, last, 3)
                else:
                    dve_combine(dve, ml, h - 1, 1, False)
                    if is1(h):
                        dve.wait_ge(squared, HEADS)
                        link(nc.vector.tensor_scalar(msr[:], ps[:, 7, 0:NT * HEADS], 1.0 / P, EPS, ALU.mult, ALU.add))
                        nc.vector.sem_inc(ms_out, 1)
                    else:
                        dve_take(dve, h - 2)
                        dve_norm(dve, h - 2)
                    dve_top(dve, ml, h, 0)
                    dve_map(dve, ml, h - 1, 2)
                    dve_map(dve, ml, h - 1, 3)
                dve_combine(dve, ml, h, 0, first)
                dve_top(dve, ml, h, 1)
                dve_map(dve, ml, h, 0)
                dve_map(dve, ml, h, 1)
                if not first:
                    dve_repeat(dve, h - 1, is1(h))

            heads_loop(dve, one_da)
            heads_loop(dve, one_mla)
            dve_combine(dve, ml, last, 1, False)
            dve_take(dve, last - 1)
            dve_norm(dve, last - 1)
            dve_repeat(dve, last, False)
            dve_map(dve, ml, last, 2)
            dve_map(dve, ml, last, 3)
            dve_split(dve, GROUPS[NPG]["chunks"][0])
            dve_take(dve, last)
            dve_norm(dve, last)
            dve_split(dve, GROUPS[NPG]["chunks"][1])

        oset_free = [sem("oset_free0"), sem("oset_free1")]
        od_hi_done = sem("od_hi_done")
        od_lo_done = sem("od_lo_done")
        gate_in = sem("gate_in")
        gate_used = sem("gate_used")
        x2_in = sem("x2_in")
        merged = sem("merged")
        m_hi = sem("m_hi")
        m_lo = sem("m_lo")
        resid_done = sem("resid_done")
        OJ = range(NPG, len(GROUPS))

        def sp_output(sp):
            for n, j in enumerate(OJ[:4]):
                row = GROUPS[j]["row"] + (D if GROUPS[j]["kind"] == "merge_b" else 0)
                if n == 0:
                    sp.wait_ge(ml.summed, 2 * HEADS)
                    sp.wait_ge(ml.map_lo, NT * HEADS)
                    sp.wait_ge(rbc_turned, HEADS)
                else:
                    sp.wait_ge(gate_used, n)
                sp.dma_start(gstage[:], gT_d[row:row + 512, :].rearrange("(f p) t -> p f t", p=P)).then_inc(gate_in, 16)
                if n == 0:
                    sp.dma_start(x2[:], x[0].rearrange("(t p) d -> p t d", p=P)).then_inc(x2_in, 16)
                for c in range(PCH + RAW + 2 * n, PCH + RAW + 2 * n + 2):
                    sp_chunk(sp, c)
            for c in range(PCH + RAW + 8, NCH):
                sp_chunk(sp, c)

        def pe_output(pe):
            pe.wait_ge(ml.taken, 2 * HEADS)
            pe.wait_ge(normed, HEADS)
            for j in OJ:
                k = GROUPS[j]["kind"]
                if j == NPG + 1:
                    pe.wait_ge(od_lo_done, 1)
                pe_group(pe, j, oset_free)

        def act_output(act, link):
            act.wait_ge(ml.summed, 2 * HEADS)
            act.wait_ge(ml.map_lo, NT * HEADS)
            act.wait_ge(normed, HEADS)
            nc.scalar.activation(od_hi[:], oraw[:], ACT.Copy, scale=cols[:, GSUB:GSUB + 1]).then_inc(od_hi_done, 1)
            for j in OJ:
                if j > NPG:
                    for n in GROUPS[j]["chunks"]:
                        act_split(act, n)
                if j >= NPG + 2 and GROUPS[j - 1]["kind"] == "merge_a":
                    half_ = GROUPS[j - 1]["row"] // 512
                    act.wait_ge(merged, half_ + 1)
                    nc.scalar.activation(mT_hi[:, 4 * half_:4 * half_ + 4, :], mtmp[:], ACT.Copy).then_inc(m_hi, 1)

        def dve_output(dve, link):
            dve.wait_ge(od_hi_done, 1)
            nc.vector.scalar_tensor_tensor(od_lo[:], oraw[:], cols[:, GSUB:GSUB + 1], od_hi[:].bitcast(F32),
                                           ALU.mult, ALU.subtract).then_inc(od_lo_done, 1)
            dve.wait_ge(od_lo_done, 1)
            for j in list(OJ) + [len(GROUPS)]:
                if NPG < j < len(GROUPS):
                    for n in GROUPS[j]["chunks"]:
                        dve_split(dve, n)
                if j == NPG:
                    continue
                g, s = GROUPS[j - 1], (j - 1) % 2
                n = j - 1 - NPG
                wait_group(dve, j - 1)
                if g["kind"] == "merge_b":
                    dve.wait_ge(gate_in, 16 * (n + 1))
                    if n:
                        dve.wait_ge(m_lo, 1)
                    link(nc.vector.tensor_tensor(mtmp[:], bank_set(s), gstage[:], ALU.mult))
                    nc.vector.sem_inc(gate_used, 1)
                    nc.vector.sem_inc(oset_free[s], 1)
                elif g["kind"] == "merge_a":
                    half_ = g["row"] // 512
                    dve.wait_ge(gate_in, 16 * (n + 1))
                    link(nc.vector.tensor_tensor(gstage[:], bank_set(s), gstage[:], ALU.mult))
                    nc.vector.sem_inc(oset_free[s], 1)
                    link(nc.vector.tensor_tensor(mtmp[:], mtmp[:], gstage[:], ALU.add))
                    nc.vector.sem_inc(gate_used, 1)
                    nc.vector.sem_inc(merged, 1)
                    dve.wait_ge(m_hi, half_ + 1)
                    nc.vector.tensor_tensor(mT_lo[:, 4 * half_:4 * half_ + 4, :], mtmp[:],
                                            mT_hi[:, 4 * half_:4 * half_ + 4, :].bitcast(F32),
                                            ALU.subtract).then_inc(m_lo, 1)
                else:
                    dve.wait_ge(x2_in, 16)
                    r = g["row"]
                    for t in range(NT):
                        nc.vector.tensor_tensor(x2[:, t, r:r + 512], x2[:, t, r:r + 512], ps[:, 4 * s + t, :],
                                                ALU.add).then_inc(resid_done, 1)

        table_set = sem("table_set")
        r_consts = sem("r_consts")
        b_in = sem("b_in")
        b_done = sem("b_done")
        router_in = sem("router_in")
        x2_sums = sem("x2_sums")
        x2_mean = sem("x2_mean")
        x2_rms = sem("x2_rms")
        h2_ready = sem("h2_ready")
        h2_stored = sem("h2_stored")
        h2_turned = sem("h2_turned")
        h2_copied = sem("h2_copied")
        routed = sem("routed")
        shifted = sem("shifted")
        weighted = sem("weighted")
        picked = sem("picked")
        ranked = sem("ranked")
        rows_listed = sem("rows_listed")
        rows_ready = sem("rows_ready")
        wd_ready = sem("wd_ready")
        wd_turned = sem("wd_turned")
        wdT_ready = sem("wdT_ready")
        bias_summed = sem("bias_summed")
        bias_added = sem("bias_added")
        listed = sem("listed")
        lists_in = sem("lists_in")
        m_raw_in = [sem(f"m_raw_in{i}") for i in range(MRAW)]
        m_hi_done = sem("m_hi_done")
        m_lo_done = sem("m_lo_done")
        m_used = sem("m_used")
        sel_ready = sem("sel_ready")
        sel_used = sem("sel_used")
        xe_in = sem("xe_in")
        x_turned = sem("x_turned")
        x_hi = sem("x_hi")
        x_lo = sem("x_lo")
        gate_taken = sem("gate_taken")
        sig_done = sem("sig_done")
        gated = sem("gated")
        up_taken = sem("up_taken")
        act_done = sem("act_done")
        a_turned = sem("a_turned")
        a_hi = sem("a_hi")
        a_lo = sem("a_lo")
        y_taken = sem("y_taken")
        scattered = sem("scattered")
        idx_step = sem("idx_step")
        y_in = x_in + raw_in
        y_before = [16] * NT + per_slot

        def y_landed(i):
            return y_in[i], y_before[i] + 16
        y_paired = sem("y_paired")
        y_added = sem("y_added")
        out_sums = sem("out_sums")
        out_mean = sem("out_mean")
        out_rms = sem("out_rms")
        out_ready = sem("out_ready")
        out_stored = sem("out_stored")

        wg_rows = w_gate[0].rearrange("e d f -> (e d) f")
        wu_rows = w_up[0].rearrange("e d f -> (e d) f")
        wd_rows = w_down[0].rearrange("e d f -> (e d) f")
        KPC = CH // D
        CPM = KD // KPC
        PER = 3 * CPM
        HEAD = 2 * CPM
        assert MRAW == HEAD + CPM and PER % MRAW == 0 and PER % MSPL == 0

        def chunk_no(g, c):
            return c if isinstance(g, int) and g == 0 else PER * g + (HEAD - PER) + c

        def slot_of(g, c, ring):
            return (c if isinstance(g, int) and g == 0 else c + HEAD - PER) % ring

        def landed_in(g, c):
            if isinstance(g, int) and g == 0:
                return 16 * (c // MRAW + 1)
            return 16 * ((PER // MRAW) * g + (HEAD - PER + c) // MRAW + 1)

        def rounds_of(eng):
            eng.wait_ge(rows_ready, 1)
            more = eng.value_load(further[0:1, 0:1], min_val=0, max_val=ROUNDS - 1)
            return eng.snap(more * E + E)

        def sp_matrix(sp, rows, e_row, g, c0):
            srcs = [rows[bass.ds(e_row + c * KPC * P, KPC * P), :].rearrange("(k p) f -> p k f", p=P)
                    for c in range(CPM)]
            for c in range(CPM):
                n = chunk_no(g, c0 + c)
                if not (isinstance(g, int) and g == 0 and c0 + c < MRAW):
                    sp.wait_ge(m_hi_done, n - MRAW + 1)
                    sp.wait_ge(m_lo_done, n - MRAW + 1)
                s = slot_of(g, c0 + c, MRAW)
                sp.dma_start(mraw[s][:].rearrange("p (k f) -> p k f", k=KPC), srcs[c]).then_inc(m_raw_in[s], 16)

        def sp_moe(sp):
            sp.wait_ge(m_lo, 2)
            sp.dma_start(gffn[:], g_ffn[0].partition_broadcast(P)).then_inc(router_in, 16)
            sp.dma_start(wr[:], w_router[0].rearrange("(k p) e -> p k e", p=P)).then_inc(router_in, 16)
            sp.dma_start(br[:], b_router[0].partition_broadcast(P)).then_inc(router_in, 16)
            sp.wait_ge(hi_done, NCH)
            sp.wait_ge(lo_done, NCH)
            sp.wait_ge(chunk_used, OG[4]["chunks"][0])
            sp.wait_ge(gate_used, 4)
            sp.dma_start(bdown[:], b_down[0]).then_inc(b_in, 16)
            for i in range(3):
                sp.dma_start(bsrc[32 * i:32 * i + 32, 0, :], b_gate[0]).then_inc(b_in, 16)
                sp.dma_start(bsrc[32 * i:32 * i + 32, 1, :], b_up[0]).then_inc(b_in, 16)
            def ahead(n):
                rows = wu_rows if CPM <= n < 2 * CPM else wg_rows
                k = (n // HEAD) * D + (n % CPM) * KPC * P
                sp.dma_start(mraw[n][:].rearrange("p (k f) -> p k f", k=KPC),
                             rows[k:k + KPC * P, :].rearrange("(k p) f -> p k f", p=P)).then_inc(m_raw_in[n], 16)

            for n in range(EARLY):
                ahead(n)
            sp.wait_ge(h2_ready, NT)
            sp.dma_start(h2_d.rearrange("(t p) d -> p t d", p=P), h2[:]).then_inc(h2_stored, 16)
            sp.wait_ge(b_done, 1)
            ahead(EARLY)
            sp.wait_ge(wd_ready, 1)
            ahead(EARLY + 1)
            sp.wait_ge(listed, 16 * NT * TOPK)
            sp.dma_start(lists[:, 1:BLOCKS + 1, :], table_d.rearrange("(p b) f -> p b f", p=P)).then_inc(lists_in, 16)
            G = rounds_of(sp)
            sp_matrix(sp, wu_rows, D, 1, CPM)
            sp_matrix(sp, wd_rows, 0, 1, 2 * CPM)
            with sp.Fori(2, G) as g:
                now = sp.snap((g % E) * D)
                before = sp.snap(((g - 1) % E) * D)
                sp_matrix(sp, wg_rows, now, g, 0)
                sp_matrix(sp, wu_rows, now, g, CPM)
                sp_matrix(sp, wd_rows, before, g, 2 * CPM)
            sp_matrix(sp, wd_rows, (E - 1) * D, G, 0)
            sp.wait_ge(m_used, chunk_no(G, CPM - 1) + 1)
            sp.dma_start(gfin[:], g_final.partition_broadcast(P)).then_inc(b_in, 16)
            sp.wait_ge(scattered, 16 * (G + 1))
            yv = y_d.rearrange("(t p k) d -> t p k d", p=P, k=TOPK)
            for t in range(NT):
                for k in range(0, TOPK, 2):
                    sp.dma_start(ybuf[t][:, k:k + 2, :], yv[t, :, k:k + 2, :]).then_inc(y_in[2 * t + k // 2], 16)
            for t in range(NT):
                sp.wait_ge(out_ready, t + 1)
                sp.dma_start(out[0, t * P:(t + 1) * P, :], x2[:, t, :]).then_inc(out_stored, 16)
            sp.wait_ge(out_stored, 16 * NT)

        def act_moe(act, link):
            for n in range(2):
                for t in range(NT):
                    act.wait_ge(resid_done, NT * n + t + 1)
                    nc.scalar.activation(sq_half[:, t, :], x2[:, t, 512 * n:512 * n + 512], ACT.Square,
                                         accum_out=stat[:, NT * n + t:NT * n + t + 1]).then_inc(x2_sums, 1)
                if n == 0:
                    act.wait_ge(x2_sums, NT)
            for k in range(0, KD, 4):
                act.wait_ge(h2_turned, k // 4 + 1)
                nc.scalar.activation(h2T[:, k:k + 4, :], ps[:, k:k + 4, :], ACT.Copy).then_inc(h2_copied, 1)
            act.wait_ge(routed, 1)
            nc.scalar.activation(logT[:], ps[0:E, 0, :], ACT.Copy).then_inc(h2_copied, 1)
            act.wait_ge(shifted, 1)
            nc.scalar.activation(wexp[:], wexp[:], ACT.Exp).then_inc(weighted, 1)
            act.wait_ge(wd_turned, 1)
            nc.scalar.activation(wdT[:], ps[0:E, 2, :], ACT.Copy).then_inc(wdT_ready, 1)
            G = rounds_of(act)

            def split(g, c):
                n = chunk_no(g, c)
                act.wait_ge(m_raw_in[slot_of(g, c, MRAW)], landed_in(g, c))
                if isinstance(g, int) and g == 0 and c < MSPL:
                    act.wait_ge(chunk_used, NCH)
                    if c == 2:
                        act.wait_ge(h2_stored, 16)
                        act.wait_ge(h2_turned, 2)
                else:
                    act.wait_ge(m_used, n - MSPL + 1)
                nc.scalar.activation(mwhi[slot_of(g, c, MSPL)][:], mraw[slot_of(g, c, MRAW)][:], ACT.Copy).then_inc(m_hi_done, 1)

            def sigmoid(g):
                act.wait_ge(gate_taken, g + 1)
                if not (isinstance(g, int) and g == 0):
                    act.wait_ge(act_done, g)
                nc.scalar.activation(sg[:], gg[:], ACT.Sigmoid, scale=ALPHA).then_inc(sig_done, 1)

            def take_x(g):
                act.wait_ge(x_turned, g + 1)
                nc.scalar.activation(xT_hi[:].rearrange("p k t -> p (k t)"), ps[:, 6:8, :].rearrange("p b n -> p (b n)"),
                                     ACT.Copy).then_inc(x_hi, 1)

            def take_act(g):
                act.wait_ge(a_turned, g + 1)
                nc.scalar.activation(aT2_hi[:].rearrange("p k t -> p (k t)"), ps[:, 6:8, :].rearrange("p b n -> p (b n)"),
                                     ACT.Copy).then_inc(a_hi, 1)

            def take_y(g, done):
                act.wait_ge(m_used, done)
                act.wait_ge(scattered, 16 * (g + 1))
                nc.scalar.activation(ye[:], ps[:, 4:6, :].rearrange("p b n -> p (b n)"), ACT.Copy,
                                     scale=lists[:, bass.ds(g + 1, 1), 2:3].rearrange("p a b -> p (a b)").bitcast(F32)
                                     ).then_inc(y_taken, 1)

            for c in range(HEAD):
                if c == MSPL:
                    take_x(0)
                    act.wait_ge(lists_in, 16)
                split(0, c)
            sigmoid(0)
            take_x(1)
            with act.Fori(1, G) as g:
                for c in range(PER):
                    split(g, c)
                    if c == 2:
                        take_act(g - 1)
                        take_y(g - 2, chunk_no(g, 0))
                    if c == 7:
                        sigmoid(g)
                    if c == 10:
                        take_x(g + 1)
            for c in range(CPM):
                split(G, c)
                if c == 2:
                    take_act(G - 1)
                    take_y(G - 2, chunk_no(G, 0))
            take_y(G - 1, chunk_no(G, CPM))
            for t in range(NT):
                act.wait_ge(y_added, t + 1)
                if t:
                    act.wait_ge(out_sums, t)
                nc.scalar.activation(fdump[:], x2[:, t, :], ACT.Square, accum_out=stat[:, 16 + t:17 + t]).then_inc(out_sums, 1)

        def dve_moe(dve, link):
            dve.wait_ge(x2_sums, 2 * NT)
            link(nc.vector.tensor_tensor(stat2[:, 0:NT], stat[:, 0:NT], stat[:, NT:2 * NT], ALU.add))
            link(nc.vector.tensor_scalar(stat2[:, 0:NT], stat2[:, 0:NT], 1.0 / D, EPS, ALU.mult, ALU.add))
            nc.vector.sem_inc(x2_mean, 1)
            dve.wait_ge(x2_rms, 1)
            dve.wait_ge(router_in, 48)
            for t in range(NT):
                nc.vector.scalar_tensor_tensor(h2[:, t, :], x2[:, t, :], stat2[:, t:t + 1], gffn[:], ALU.mult,
                                               ALU.mult).then_inc(h2_ready, 1)
            dve.wait_ge(b_in, 16 * 7)
            link(nc.vector.tensor_scalar(bsrc[:, 1, :], bsrc[:, 1, :], 1.0, None, ALU.add))
            flatb = lambda b, i: b[32 * i:32 * i + 32].rearrange("p m f -> p (m f)")
            for i in range(3):
                for r in range(i):
                    link(nc.vector.tensor_copy(flatb(bpart, i), flatb(bsrc, i)))
                    link(nc.vector.tensor_tensor(flatb(bsrc, i), flatb(bsrc, i), flatb(bpart, i), ALU.subtract))
                link(nc.vector.tensor_copy(flatb(bpart, i), flatb(bsrc, i)))
            nc.vector.sem_inc(b_done, 1)
            dve.wait_ge(routed, 2)
            link(nc.vector.tensor_tensor(logits[:], ps[:, 1, 0:NT * E].rearrange("p (t e) -> p t e", t=NT),
                                         br[:].unsqueeze(1).to_broadcast([P, NT, E]), ALU.add))
            for t in range(NT):
                link(nc.vector.max(top8[:, t, :], logits[:, t, :]))
                link(nc.vector.max_index(idx8[:, t, :], top8[:, t, :], logits[:, t, :]))
            link(nc.vector.tensor_tensor(wexp[:], top8[:], top8[:, :, 0:1].to_broadcast([P, NT, 8]), ALU.subtract))
            nc.vector.sem_inc(shifted, 1)
            link(nc.vector.tensor_copy(idxf[:], idx8[:]))
            dve.wait_ge(r_consts, 6)
            link(nc.vector.tensor_tensor(pick[:], iota_e[:].unsqueeze(1).unsqueeze(1).to_broadcast([P, NT, TOPK, E]),
                                         idxf[:, :, 0:TOPK].unsqueeze(3).to_broadcast([P, NT, TOPK, E]), ALU.is_equal))
            link(nc.vector.tensor_reduce(chosen[:], pick[:].rearrange("p t k e -> p t e k"), AX_X, ALU.add))
            link(nc.vector.tensor_copy(chosen_b[:], chosen[:]))
            nc.vector.sem_inc(picked, 1)
            dve.wait_ge(weighted, 1)
            link(nc.vector.tensor_reduce(stat2[:, 8:12], wexp[:, :, 0:TOPK], AX_X, ALU.add))
            link(nc.vector.reciprocal(stat2[:, 12:16], stat2[:, 8:12]))
            link(nc.vector.tensor_tensor(wexp[:, :, 0:TOPK], wexp[:, :, 0:TOPK],
                                         stat2[:, 12:16].unsqueeze(2).to_broadcast([P, NT, TOPK]), ALU.mult))
            link(nc.vector.tensor_copy(rec[:, :, 2:3].bitcast(F32).rearrange("p (t k) a -> p t (k a)", t=NT),
                                       wexp[:, :, 0:TOPK]))
            dve.wait_ge(ranked, 1)
            rank = ps[:, 0, 0:NT * E].rearrange("p (t e) -> p t e", t=NT)
            link(nc.vector.tensor_tensor(ptmp[:], pick[:], rank.unsqueeze(2).to_broadcast([P, NT, TOPK, E]), ALU.mult))
            link(nc.vector.tensor_reduce(mcount[:], ptmp[:].rearrange("p t k e -> p (t k) e"), AX_X, ALU.add))
            link(nc.vector.scalar_tensor_tensor(rowsel[:].rearrange("p (t k) -> p t k", t=NT),
                                                mcount[:].rearrange("p (t k) -> p t k", t=NT), float(BLOCKS),
                                                idxf[:, :, 0:TOPK], ALU.mult, ALU.add))
            for r in range(1, ROUNDS):
                link(nc.vector.tensor_scalar(over_k[:], mcount[:], float(P * r), float(E - P * BLOCKS), ALU.is_ge, ALU.mult))
                link(nc.vector.tensor_tensor(rowsel[:], rowsel[:], over_k[:], ALU.add))
            link(nc.vector.tensor_copy(rowidx[:], rowsel[:]))
            nc.vector.sem_inc(rows_listed, 1)
            link(nc.vector.tensor_reduce(stat2[:, 16:17], ps[:, 0, NT * E:NT * E + E], AX_X, ALU.max))
            for r in range(1, ROUNDS):
                link(nc.vector.tensor_scalar(stat2[:, 16 + r:17 + r], stat2[:, 16:17], float(P * r), None, ALU.is_gt))
            link(nc.vector.tensor_reduce(stat2[:, 20:21], stat2[:, 17:16 + ROUNDS], AX_X, ALU.add))
            link(nc.vector.tensor_copy(further[:, 0:1], stat2[:, 20:21]))
            nc.vector.sem_inc(rows_ready, 1)
            link(nc.vector.tensor_tensor(ptmp[:], pick[:], wexp[:, :, 0:TOPK].unsqueeze(3).to_broadcast([P, NT, TOPK, E]),
                                         ALU.mult))
            link(nc.vector.tensor_reduce(wdense[:], ptmp[:].rearrange("p t k e -> p t e k"), AX_X, ALU.add))
            nc.vector.sem_inc(wd_ready, 1)
            for n in range(2):
                dve.wait_ge(bias_summed, n + 1)
                link(nc.vector.tensor_tensor(x2[:, :, 512 * n:512 * n + 512], x2[:, :, 512 * n:512 * n + 512],
                                             ps[:, 4:8, :], ALU.add))
                nc.vector.sem_inc(bias_added, 1)
            G = rounds_of(dve)

            def split(g, c):
                dve.wait_ge(m_hi_done, chunk_no(g, c) + 1)
                s, r = slot_of(g, c, MSPL), slot_of(g, c, MRAW)
                nc.vector.tensor_tensor(mwlo[s][:], mraw[r][:], mwhi[s][:].bitcast(F32), ALU.subtract).then_inc(m_lo_done, 1)

            def take_gate(g, used):
                dve.wait_ge(m_used, used)
                if not (isinstance(g, int) and g == 0):
                    dve.wait_ge(act_done, g)
                nc.vector.tensor_scalar(gg[:], ps[:, 0:2, :].rearrange("p b n -> p (b n)"), LIMIT, None,
                                        ALU.min).then_inc(gate_taken, 1)

            def take_up(g, used):
                dve.wait_ge(m_used, used)
                dve.wait_ge(gated, g + 1)
                nc.vector.tensor_scalar(uu[:], ps[:, 2:4, :].rearrange("p b n -> p (b n)"), 1.0 + LIMIT, 1.0 - LIMIT,
                                        ALU.min, ALU.max).then_inc(up_taken, 1)

            def take_x(g):
                dve.wait_ge(x_hi, g + 1)
                nc.vector.tensor_tensor(xT_lo[:].rearrange("p k t -> p (k t)"), ps[:, 6:8, :].rearrange("p b n -> p (b n)"),
                                        xT_hi[:].rearrange("p k t -> p (k t)").bitcast(F32), ALU.subtract).then_inc(x_lo, 1)

            def take_act(g):
                dve.wait_ge(a_hi, g + 1)
                nc.vector.tensor_tensor(aT2_lo[:].rearrange("p k t -> p (k t)"), ps[:, 6:8, :].rearrange("p b n -> p (b n)"),
                                        aT2_hi[:].rearrange("p k t -> p (k t)").bitcast(F32), ALU.subtract).then_inc(a_lo, 1)

            for c in range(HEAD):
                if c == MSPL:
                    take_x(0)
                split(0, c)
                if c == 6:
                    take_gate(0, CPM)
            take_up(0, HEAD)
            take_x(1)
            with dve.Fori(1, G) as g:
                for c in range(PER):
                    split(g, c)
                    if c == 2:
                        take_act(g - 1)
                    if c == 6:
                        take_gate(g, chunk_no(g, CPM))
                    if c == 10:
                        take_up(g, chunk_no(g, 2 * CPM))
                        take_x(g + 1)
            for c in range(CPM):
                split(G, c)
                if c == 2:
                    take_act(G - 1)
            def norm(t):
                dve.wait_ge(out_sums, t + 1)
                link(nc.vector.tensor_scalar(stat2[:, t:t + 1], stat[:, 16 + t:17 + t], 1.0 / D, EPS, ALU.mult, ALU.add))
                nc.vector.sem_inc(out_mean, 1)
                dve.wait_ge(out_rms, t + 1)
                link(nc.vector.scalar_tensor_tensor(x2[:, t, :], x2[:, t, :], stat2[:, t:t + 1], gfin[:], ALU.mult, ALU.mult))
                nc.vector.sem_inc(out_ready, 1)

            dve.wait_ge(b_in, 16 * 8)
            for t in range(NT):
                dve.wait_ge(y_paired, t + 1)
                for k in (0, 2, 3):
                    if k == 2:
                        dve.wait_ge(*y_landed(2 * t + 1))
                    link(nc.vector.tensor_tensor(x2[:, t, :], x2[:, t, :], ybuf[t][:, k, :], ALU.add))
                    if t and k == 0:
                        norm(t - 1)
                nc.vector.sem_inc(y_added, 1)
            norm(NT - 1)

        def pool_moe(pool):
            pool.wait_ge(x2_mean, 1)
            nc.gpsimd.tensor_tensor(stat2[:, 0:NT], stat2[:, 0:NT], half[:, 0:NT], ALU.pow).then_inc(x2_rms, 1)
            nc.gpsimd.iota(iota_e[:], [[1, E]], base=0, channel_multiplier=0,
                           allow_small_or_imprecise_dtypes=True).then_inc(r_consts, 1)
            nc.gpsimd.memset(allone[:], 1.0).then_inc(r_consts, 1)
            pool.wait_ge(r_consts, 2)
            nc.gpsimd.affine_select(out=upper[:], in_=allone[:], compare_op=ALU.is_gt, fill=0.0, base=0,
                                    pattern=[[1, P]], channel_multiplier=-1).then_inc(r_consts, 1)
            nc.gpsimd.memset(rec[:], 0).then_inc(r_consts, 1)
            pool.wait_ge(r_consts, 4)
            nc.gpsimd.iota(rec[:, :, 0:1].rearrange("p (t k) a -> p t (k a)", t=NT), [[P * TOPK, NT], [1, TOPK]], base=0,
                           channel_multiplier=TOPK).then_inc(r_consts, 1)
            nc.gpsimd.iota(rec[:, :, 1:2].rearrange("p (t k) a -> p t (k a)", t=NT), [[P, NT], [0, TOPK]], base=0,
                           channel_multiplier=1).then_inc(r_consts, 1)
            nc.gpsimd.memset(padrec[:], NOWHERE).then_inc(r_consts, 1)
            pool.wait_ge(r_consts, 7)
            nc.gpsimd.memset(padrec[:, :, 2:4], 0).then_inc(r_consts, 1)
            pool.wait_ge(r_consts, 8)
            pool.dma_start(table_d.rearrange("(p b) f -> p b f", p=P), padrec[:]).then_inc(table_set, 16)
            nc.gpsimd.memset(selid[:], 0.0).then_inc(r_consts, 1)
            pool.wait_ge(r_consts, 9)
            for i in range(3):
                pool.wait_ge(r_consts, 9 + i)
                nc.gpsimd.affine_select(out=selid[:], in_=selid[:], compare_op=ALU.not_equal, fill=1.0, base=-32 * i,
                                        pattern=[[-1, E]], channel_multiplier=1).then_inc(r_consts, 1)
            pool.wait_ge(table_set, 16)
            nc.gpsimd.memset(xe[:], 0.0).then_inc(r_consts, 1)
            pool.wait_ge(r_consts, 13)
            pool.wait_ge(rows_listed, 1)
            for i in range(NT * TOPK):
                pool.indirect_dma_start(out=table_d, out_offset=bass.IndirectOffsetOnAxis(ap=rowidx[:, i:i + 1].bitcast(U32), axis=0),
                                        in_=rec[:, i, :], in_offset=None).then_inc(listed, 16)
            nc.gpsimd.memset(lists[:, 0:BLOCKS + 2:BLOCKS + 1, :], NOWHERE).then_inc(idx_step, 1)
            pool.wait_ge(idx_step, 1)
            nc.gpsimd.memset(lists[:, 0:BLOCKS + 2:BLOCKS + 1, 2:4], 0).then_inc(idx_step, 1)
            pool.wait_ge(idx_step, 2)
            pool.wait_ge(lists_in, 16)
            pool.wait_ge(h2_stored, 16)
            G = rounds_of(pool)
            last_token = pool.to_reg(SEQ - 1)
            last_row = pool.to_reg(SEQ * TOPK - 1)

            def gather(g):
                nc.gpsimd.tensor_copy(gidx[:], lists[:, bass.ds(g + 1, 1), :].rearrange("p a b -> p (a b)")).then_inc(gidx_ready, 1)
                pool.wait_ge(gidx_ready, g + 1)
                nc.gpsimd.sem_inc(idx_seen, 1)
                pool.indirect_dma_start(out=xe[:], out_offset=None, in_=h2_d,
                                        in_offset=bass.IndirectOffsetOnAxis(ap=gidx[:, 1:2].bitcast(U32), axis=0),
                                        bounds_check=last_token, oob_is_err=False).then_inc(xe_in, 16)

            def gate_it(g):
                pool.wait_ge(sig_done, g + 1)
                nc.gpsimd.tensor_tensor(gg[:], gg[:], sg[:], ALU.mult).then_inc(gated, 1)

            def activate(g):
                pool.wait_ge(up_taken, g + 1)
                pool.wait_ge(gated, g + 1)
                if not (isinstance(g, int) and g == 0):
                    pool.wait_ge(a_turned, g)
                nc.gpsimd.tensor_tensor(ae[:], uu[:], gg[:], ALU.mult).then_inc(act_done, 1)

            def select(g):
                e = g % E
                nc.gpsimd.tensor_copy(selb[:], selid[:, bass.ds(e, 1)].to_broadcast([96, P])).then_inc(sel_ready, 1)

            def scatter(g):
                before = 16 * (g + 1) if isinstance(g, int) else pool.snap(16 * (g + 1))
                pool.wait_ge(y_taken, g + 2)
                pool.wait_ge(scattered, before)
                nc.gpsimd.tensor_copy(sidx[:], lists[:, bass.ds(g + 1, 1), :].rearrange("p a b -> p (a b)")).then_inc(sidx_ready, 1)
                pool.wait_ge(sidx_ready, g + 2)
                nc.gpsimd.sem_inc(idx_seen, 1)
                pool.indirect_dma_start(out=y_d, out_offset=bass.IndirectOffsetOnAxis(ap=sidx[:, 0:1].bitcast(U32), axis=0),
                                        in_=ye[:], in_offset=None, bounds_check=last_row,
                                        oob_is_err=False).then_inc(scattered, 16)

            gather(0)
            select(0)
            pool.wait_ge(x_turned, 1)
            gather(1)
            pool.wait_ge(sel_used, 1)
            select(1)
            gate_it(0)
            activate(0)
            with pool.Fori(1, G) as g:
                pool.wait_ge(x_turned, g + 1)
                gather(g + 1)
                scatter(g - 2)
                pool.wait_ge(sel_used, g + 1)
                select(g + 1)
                gate_it(g)
                activate(g)
            scatter(G - 2)
            scatter(G - 1)
            pool.wait_ge(idx_seen, 2 * G + 2)

            def rms(t):
                pool.wait_ge(out_mean, t + 1)
                nc.gpsimd.tensor_tensor(stat2[:, t:t + 1], stat2[:, t:t + 1], half[:, 0:1], ALU.pow).then_inc(out_rms, 1)

            for t in range(NT):
                pool.wait_ge(*y_landed(2 * t))
                nc.gpsimd.tensor_tensor(ybuf[t][:, 0, :], ybuf[t][:, 0, :], ybuf[t][:, 1, :], ALU.add).then_inc(y_paired, 1)
                if t:
                    rms(t - 1)
            rms(NT - 1)

        gidx_ready = sem("gidx_ready")
        sidx_ready = sem("sidx_ready")
        idx_seen = sem("idx_seen")

        def pe_moe(pe):
            pe.wait_ge(h2_ready, 1)
            pe.wait_ge(resid_done, 2 * NT)
            for t in range(NT):
                pe.wait_ge(h2_ready, t + 1)
                for k in range(KD):
                    mm = nc.tensor.transpose(ps[:, k, t * P:(t + 1) * P], h2[:, t, k * P:(k + 1) * P], ident[:])
                    if t == NT - 1 and k % 4 == 3:
                        mm.then_inc(h2_turned, 1)
            pe.wait_ge(router_in, 48)
            for k in range(KD):
                if k % 4 == 0:
                    pe.wait_ge(h2_copied, k // 4 + 1)
                mm = nc.tensor.matmul(ps[0:E, 0, :], wr[:, k, :], h2T[:, k, :], start=k == 0, stop=k == KD - 1)
            mm.then_inc(routed, 1)
            pe.wait_ge(h2_copied, 3)
            for t in range(NT):
                mm = nc.tensor.transpose(ps[:, 1, t * E:(t + 1) * E], logT[:, t * P:(t + 1) * P], ident[0:E, 0:E])
            mm.then_inc(routed, 1)
            pe.wait_ge(picked, 1)
            pe.wait_ge(r_consts, 3)
            for t in range(NT):
                for s in range(t + 1):
                    nc.tensor.matmul(ps[:, 0, t * E:(t + 1) * E], upper[:] if s == t else allone[:], chosen_b[:, s, :],
                                     start=s == 0, stop=s == t)
            for s in range(NT):
                mm = nc.tensor.matmul(ps[:, 0, NT * E:NT * E + E], allone[:], chosen_b[:, s, :], start=s == 0,
                                      stop=s == NT - 1)
            mm.then_inc(ranked, 1)
            pe.wait_ge(wd_ready, 1)
            for t in range(NT):
                mm = nc.tensor.transpose(ps[0:E, 2, t * P:(t + 1) * P], wdense[:, t, :], ident[:])
            mm.then_inc(wd_turned, 1)
            pe.wait_ge(wdT_ready, 1)
            pe.wait_ge(b_in, 16 * 7)
            for n in range(2):
                if n:
                    pe.wait_ge(bias_added, n)
                for t in range(NT):
                    mm = nc.tensor.matmul(ps[:, 4 + t, :], wdT[:, t * P:(t + 1) * P], bdown[:, 512 * n:512 * n + 512],
                                          start=True, stop=True)
                mm.then_inc(bias_summed, 1)
            pe.wait_ge(bias_added, 2)
            pe.wait_ge(b_done, 1)
            G = rounds_of(pe)

            def turn_x(g):
                pe.wait_ge(xe_in, 16 * (g + 1))
                for k in range(KD):
                    mm = nc.tensor.transpose(ps[:, 6 + k // 4, (k % 4) * P:(k % 4 + 1) * P], xe[:, k * P:(k + 1) * P], ident[:])
                mm.then_inc(x_turned, 1)

            def turn_act(g):
                pe.wait_ge(act_done, g + 1)
                pe.wait_ge(x_lo, g + 2)
                for k in range(KD):
                    mm = nc.tensor.transpose(ps[:, 6 + k // 4, (k % 4) * P:(k % 4 + 1) * P], ae[:, k * P:(k + 1) * P], ident[:])
                mm.then_inc(a_turned, 1)

            def product(g, c0, hi, lo, bank, bias):
                if bias is not None:
                    for n in range(2):
                        mm = nc.tensor.matmul(ps[:, bank + n, :], selb[:], bpart[:, bias, 512 * n:512 * n + 512],
                                              start=True, stop=False)
                    if bias == 1:
                        mm.then_inc(sel_used, 1)
                for c in range(CPM):
                    pe.wait_ge(m_lo_done, chunk_no(g, c0 + c) + 1)
                    s = slot_of(g, c0 + c, MSPL)
                    for kk in range(KPC):
                        k = c * KPC + kk
                        first = bias is None and k == 0
                        last = k == KD - 1
                        for w, l in ((mwhi, False), (mwlo, False)):
                            for n in range(2):
                                nc.tensor.matmul(ps[:, bank + n, :], hi[:, k, :], w[s][:, kk * D + 512 * n:kk * D + 512 * n + 512],
                                                 start=first and w is mwhi, stop=False)
                        for n in range(2):
                            mm = nc.tensor.matmul(ps[:, bank + n, :], lo[:, k, :],
                                                  mwhi[s][:, kk * D + 512 * n:kk * D + 512 * n + 512],
                                                  start=False, stop=last)
                    mm.then_inc(m_used, 1)

            def gate_up(g):
                pe.wait_ge(x_lo, g + 1)
                pe.wait_ge(sel_ready, g + 1)
                if not (isinstance(g, int) and g == 0):
                    pe.wait_ge(gate_taken, g)
                product(g, 0, xT_hi, xT_lo, 0, 0)
                if not (isinstance(g, int) and g == 0):
                    pe.wait_ge(up_taken, g)
                product(g, CPM, xT_hi, xT_lo, 2, 1)

            def down(g, at_step, c0):
                pe.wait_ge(a_lo, g + 1)
                pe.wait_ge(y_taken, g + 1)
                product(at_step, c0, aT2_hi, aT2_lo, 4, None)

            turn_x(0)
            gate_up(0)
            turn_x(1)
            with pe.Fori(1, G) as g:
                turn_act(g - 1)
                gate_up(g)
                pe.wait_ge(a_lo, g)
                turn_x(g + 1)
                down(g - 1, g, 2 * CPM)
            turn_act(G - 1)
            down(G - 1, G, 0)

        def sp_rest(sp):
            sp_attention(sp, da)
            sp_attention(sp, ml)
            sp_output(sp)
            sp_moe(sp)

        def pool_rest(pool):
            pool_attention(pool)
            pool_moe(pool)

        def act_rest(act, link):
            act_attention(act)
            act_output(act, link)
            act_moe(act, link)

        def dve_rest(dve, link):
            dve_attention(dve, link)
            dve_output(dve, link)
            dve_moe(dve, link)

        def pe_rest(pe):
            pe_attention(pe)
            pe_output(pe)
            pe_moe(pe)

        @block.sync
        def _(sp):
            sp_start(sp)
            for n in range(RAW, PCH + RAW):
                if n == PCH:
                    sp_attention(sp, da, first_only=True)
                sp_chunk(sp, n)
            sp_rest(sp)

        @block.gpsimd
        def _(pool):
            nc.gpsimd.memset(half[:], -0.5).then_inc(pool_step, 1)
            nc.gpsimd.memset(onec[:], 1.0).then_inc(pool_step, 1)
            pool.wait_ge(pool_step, 2)
            pool.wait_ge(ss_ready, 1)
            nc.gpsimd.tensor_tensor(stat2[:, 0:4], stat2[:, 0:4], half[:, 0:4], ALU.pow).then_inc(rs_ready, 1)
            for j in STORES:
                g, n = PG[j], store_no[j]
                if n == store_no[LATE] - 4:
                    pool.wait_ge(ss_ready, 2)
                    nc.gpsimd.tensor_tensor(stat2[:, 8:16], stat2[:, 8:16], half[:, 0:8], ALU.pow).then_inc(rs_ready, 1)
                if n == len(STORES) - 1:
                    pool_qk(pool, da, 0, 0)
                pool.wait_ge(stage_full, n + 1)
                st = ostage[n % 2]
                if g["kind"] == "rows":
                    dst = scratch[g["dst"]][:, g["row"]:g["row"] + 512].rearrange("(t p) c -> p t c", p=P)
                else:
                    dst = scratch[g["dst"]][g["row"]:g["row"] + 512, :].rearrange("(f p) t -> p f t", p=P)
                pool.dma_start(dst, st[:]).then_inc(stored[n % 2], 16)
            pool_rest(pool)

        @block.scalar
        def _(act):
            step = [0]

            def link(ins):
                step[0] += 1
                ins.then_inc(act_step, 1)
                act.wait_ge(act_step, step[0])

            act.wait_ge(cols_turned, 1)
            nc.scalar.activation(cols[:, 0:NCOL], ps[:, 7, 0:NCOL], ACT.Copy).then_inc(cols_ready, 1)
            for t in range(NT):
                act.wait_ge(x_in[t], 16)
                ins = nc.scalar.activation(sq_dump[:], xrows[:, t, :], ACT.Square, accum_out=stat[:, t:t + 1])
                link(ins)
            act.wait_ge(rope_in, 1)
            a = lambda i: angles[:, i, :]
            link(nc.scalar.activation(sin[:].rearrange("p t f -> p (t f)"), a(2), ACT.Sin))
            link(nc.scalar.activation(cos[:].rearrange("p t f -> p (t f)"), a(3), ACT.Sin))
            act.wait_ge(rope_in, 2)
            link(nc.scalar.activation(lam[:, 2:4], lam[:, 0:2], ACT.Exp))
            act_split(act, 0)
            for k in range(KD):
                act.wait_ge(turned, k + 1)
                nc.scalar.activation(hT_hi[:, k, :], ps[:, k, :], ACT.Copy, scale=cols[:, GM + k:GM + k + 1]).then_inc(h_hi, 1)
            turns = [KD]

            def finish(j):
                g = PG[j]
                s = j % 2
                wait_group(act, j)
                if g["kind"].startswith("rope"):
                    n = NROPE.index(j)
                    if n >= 1:
                        act.wait_ge(turned, KD + n + (NCT + 1 if j > LATE else 0))
                    nc.scalar.activation(rstage[:], bank_set(s), ACT.Copy).then_inc(rope_in, 1)
                elif g["kind"] == "latent":
                    nc.scalar.activation(cbuf[:, :, g["row"]:g["row"] + g["n"]], bank_set(s)[:, :, 0:g["n"]],
                                         ACT.Copy).then_inc(c_rows, 1)
                    act.wait_ge(c_rows, LAT.index(j) + 1)
                    nc.scalar.sem_inc(set_free[s], 1)
                    if j == LAT[-1]:
                        for t in range(NT):
                            link(nc.scalar.activation(sq_dump[:, 0:Q_LORA], cbuf[:, t, 0:Q_LORA], ACT.Square,
                                                      accum_out=stat[:, 8 + t:9 + t]))
                            link(nc.scalar.activation(sq_dump[:, 0:KV_LORA], cbuf[:, t, Q_LORA:Q_LORA + KV_LORA],
                                                      ACT.Square, accum_out=stat[:, 12 + t:13 + t]))
                        nc.scalar.sem_inc(c_rows, 1)
                elif g["kind"] == "gate":
                    wait_stage(act, j)
                    for f in range(4):
                        c = BG + g["row"] // P + f
                        ins = nc.scalar.activation(ostage[store_no[j] % 2][:, f, :], ps[:, 4 * s + f, :], ACT.Sigmoid,
                                                   bias=cols[:, c:c + 1])
                        link(ins)
                    nc.scalar.sem_inc(stage_full, 1)
                    nc.scalar.sem_inc(set_free[s], 1)
                else:
                    wait_stage(act, j)
                    link(nc.scalar.activation(ostage[store_no[j] % 2][:], bank_set(s), ACT.Copy))
                    nc.scalar.sem_inc(stage_full, 1)
                    nc.scalar.sem_inc(set_free[s], 1)

            def finish_turn(j):
                n = NROPE.index(j)
                act.wait_ge(turned, KD + n + 1 + (NCT + 1 if j > LATE else 0))
                wait_stage(act, j)
                link(nc.scalar.activation(ostage[store_no[j] % 2][:], bank_set(j % 2), ACT.Copy))
                nc.scalar.sem_inc(stage_full, 1)
                nc.scalar.sem_inc(set_free[j % 2], 1)

            for j in range(NPG + 2):
                if j < NPG:
                    if j == LATE:
                        finish(j - 1)
                        before = KD + len([r for r in NROPE if r < LATE])
                        for f in range(NCT + 1):
                            act.wait_ge(turned, before + f + 1)
                            if f < NCT:
                                c = GQ + f
                                nc.scalar.activation(cT_hi[:, f, :], ps[:, f % 8, :], ACT.Copy,
                                                     scale=cols[:, c:c + 1]).then_inc(c_hi, 1)
                            else:
                                nc.scalar.activation(krT_hi[:], ps[0:ROPE, f % 8, :], ACT.Copy).then_inc(c_hi, 1)
                    for n in PG[j]["chunks"][:1]:
                        if n:
                            act_split(act, n)
                if j >= 2 and PG[j - 2]["kind"].startswith("rope"):
                    finish_turn(j - 2)
                if j < NPG:
                    for n in PG[j]["chunks"][1:]:
                        act_split(act, n)
                if j == NPG:
                    act_qk(act, da, 0, 0, None, 0)
                if 1 <= j <= NPG and j != LATE:
                    finish(j - 1)
            act_rest(act, link)

        @block.vector
        def _(dve):
            step = [0]

            def link(ins):
                step[0] += 1
                ins.then_inc(dve_step, 1)
                dve.wait_ge(dve_step, step[0])

            a = lambda i: angles[:, i, :]
            dve.wait_ge(angles_in, 32)
            link(nc.vector.tensor_copy(posf[:], posi[:]))
            for t in range(NT):
                link(nc.vector.tensor_scalar(angles[:, 0, t * NF:(t + 1) * NF], invf[:], posf[:, t:t + 1], None, ALU.mult))
            MAGIC = 12582912.0
            TWO_PI = 2 * math.pi
            c1 = 6.28125
            c2 = float(np.float32(round((TWO_PI - c1) * 2 ** 21) / 2 ** 21))
            c3 = float(np.float32(TWO_PI - c1 - c2))
            link(nc.vector.tensor_scalar(a(1), a(0), 1.0 / TWO_PI, MAGIC, ALU.mult, ALU.add))
            link(nc.vector.tensor_scalar(a(1), a(1), -MAGIC, None, ALU.add))
            link(nc.vector.scalar_tensor_tensor(a(2), a(1), -c1, a(0), ALU.mult, ALU.add))
            link(nc.vector.scalar_tensor_tensor(a(2), a(1), -c2, a(2), ALU.mult, ALU.add))
            link(nc.vector.scalar_tensor_tensor(a(2), a(1), -c3, a(2), ALU.mult, ALU.add))
            link(nc.vector.tensor_scalar(a(3), a(2), math.pi / 2, None, ALU.add))
            link(nc.vector.tensor_scalar(a(4), a(3), math.pi, None, ALU.is_gt))
            link(nc.vector.scalar_tensor_tensor(a(3), a(4), -TWO_PI, a(3), ALU.mult, ALU.add))
            PI_IN = 3.1415925
            link(nc.vector.tensor_scalar(a(3), a(3), PI_IN, -PI_IN, ALU.min, ALU.max))
            link(nc.vector.tensor_scalar(a(2), a(2), PI_IN, -PI_IN, ALU.min, ALU.max))
            nc.vector.sem_inc(rope_in, 1)
            dve.wait_ge(lam_in, 64)
            link(nc.vector.tensor_tensor(lamv[:, 4, :], lamv[:, 0, :], lamv[:, 1, :], ALU.mult))
            link(nc.vector.tensor_tensor(lamv[:, 5, :], lamv[:, 2, :], lamv[:, 3, :], ALU.mult))
            link(nc.vector.tensor_reduce(lam[:, 0:2], lamv[:, 4:6, :], AX_X, ALU.add))
            nc.vector.sem_inc(rope_in, 1)
            dve.wait_ge(act_step, NT)
            link(nc.vector.tensor_scalar(stat2[:, 0:4], stat[:, 0:4], 1.0 / D, EPS, ALU.mult, ALU.add))
            nc.vector.sem_inc(ss_ready, 1)
            dve.wait_ge(rs_ready, 1)
            for t in range(NT):
                nc.vector.tensor_scalar(xrows[:, t, :], xrows[:, t, :], stat2[:, t:t + 1], None, ALU.mult).then_inc(c_ready, 1)
            dve_split(dve, 0)
            for k in range(KD):
                dve.wait_ge(h_hi, k + 1)
                ins = nc.vector.scalar_tensor_tensor(hT_lo[:, k, :], ps[:, k, :], cols[:, GM + k:GM + k + 1],
                                                     hT_hi[:, k, :].bitcast(F32), ALU.mult, ALU.subtract)
                ins.then_inc(h_lo, 1)
                if k % 4 == 3:
                    dve.wait_ge(h_lo, k + 1)
                    nc.vector.sem_inc(set_free[k // 4], 1)

            dve.wait_ge(cols_ready, 1)
            link(nc.vector.tensor_scalar(cols[:, GSUB:GSUB + 1], cols[:, GSUB:GSUB + 1], 1.0 - LAM_INIT, None, ALU.mult))
            dve.wait_ge(act_step, NT + 3)
            link(nc.vector.tensor_tensor(lam[:, 4:5], lam[:, 3:4], lam[:, 2:3], ALU.subtract))
            link(nc.vector.tensor_scalar(lam[:, 5:6], lam[:, 4:5], -LAM_INIT, None, ALU.add))
            def rotate(v, f0, nf, groups):
                n = NT * groups * nf
                c4 = cos[:, :, f0:f0 + nf].unsqueeze(2).to_broadcast([P, NT, groups, nf])
                s4 = sin[:, :, f0:f0 + nf].unsqueeze(2).to_broadcast([P, NT, groups, nf])
                x1, x2_ = v[:, :, :, 0:nf], v[:, :, :, nf:2 * nf]
                tm = [rtmp[:, i, 0:n].rearrange("p (t g f) -> p t g f", t=NT, g=groups) for i in range(4)]
                nc.vector.tensor_tensor(tm[0], x1, c4, ALU.mult).then_inc(dve_step, 1)
                nc.vector.tensor_tensor(tm[1], x2_, s4, ALU.mult).then_inc(dve_step, 1)
                nc.vector.tensor_tensor(tm[2], x2_, c4, ALU.mult).then_inc(dve_step, 1)
                nc.vector.tensor_tensor(tm[3], x1, s4, ALU.mult).then_inc(dve_step, 1)
                step[0] += 4
                dve.wait_ge(dve_step, step[0])
                nc.vector.tensor_tensor(x1, tm[0], tm[1], ALU.subtract).then_inc(dve_step, 1)
                nc.vector.tensor_tensor(x2_, tm[2], tm[3], ALU.add).then_inc(dve_step, 1)
                step[0] += 2
                dve.wait_ge(dve_step, step[0])

            def finish(j):
                g = PG[j]
                if g["kind"].startswith("rope"):
                    dve.wait_ge(rope_in, 2 + NROPE.index(j) + 1)
                    v = rstage[:].rearrange("p t (g c) -> p t g c", c=DA_DIM)
                    if g["kind"] == "rope_da":
                        rotate(v, 0, FH, 8)
                    else:
                        rotate(v, FH, FM, 8)
                    nc.vector.sem_inc(roped, 1)
                elif j == LAT[-1]:
                    dve.wait_ge(c_rows, len(LAT) + 1)
                    link(nc.vector.tensor_scalar(stat2[:, 8:12], stat[:, 8:12], 1.0 / Q_LORA, EPS, ALU.mult, ALU.add))
                    link(nc.vector.tensor_scalar(stat2[:, 12:16], stat[:, 12:16], 1.0 / KV_LORA, EPS, ALU.mult, ALU.add))
                    nc.vector.sem_inc(ss_ready, 1)
                    rotate(cbuf[:, :, Q_LORA + KV_LORA:].unsqueeze(2), FH, FM, 1)
                    dve.wait_ge(rs_ready, 2)
                    for t in range(NT):
                        link(nc.vector.tensor_scalar(cbuf[:, t, 0:Q_LORA], cbuf[:, t, 0:Q_LORA],
                                                     stat2[:, 8 + t:9 + t], None, ALU.mult))
                        link(nc.vector.tensor_scalar(cbuf[:, t, Q_LORA:Q_LORA + KV_LORA],
                                                     cbuf[:, t, Q_LORA:Q_LORA + KV_LORA],
                                                     stat2[:, 12 + t:13 + t], None, ALU.mult))
                    nc.vector.sem_inc(c_ready, 1)

            for j in range(NPG + 1):
                if j == LATE:
                    for f in range(NCT + 1):
                        dve.wait_ge(c_hi, f + 1)
                        if f < NCT:
                            c = GQ + f
                            ins = nc.vector.scalar_tensor_tensor(cT_lo[:, f, :], ps[:, f % 8, :], cols[:, c:c + 1],
                                                                 cT_hi[:, f, :].bitcast(F32), ALU.mult, ALU.subtract)
                        else:
                            ins = nc.vector.tensor_tensor(krT_lo[:], ps[0:ROPE, f % 8, :], krT_hi[:].bitcast(F32),
                                                          ALU.subtract)
                        ins.then_inc(c_lo, 1)
                        if f in (3, 7, NCT):
                            dve.wait_ge(c_lo, f + 1)
                            nc.vector.sem_inc(set_free[0 if f != 7 else 1], 1)
                if j < NPG:
                    for n in PG[j]["chunks"]:
                        if n:
                            dve_split(dve, n)
                if j >= 1:
                    finish(j - 1)
            dve_rest(dve, link)

        @block.tensor
        def _(pe):
            pe.wait_ge(consts_in, 16 * N_CONSTS)
            nc.tensor.transpose(ps[:, 7, 0:NCOL], crows[:], ident[0:NCOL, 0:NCOL]).then_inc(cols_turned, 1)
            pe.wait_ge(cols_ready, 1)
            for t in range(NT):
                pe.wait_ge(c_ready, t + 1)
                for k in range(KD):
                    mm = nc.tensor.transpose(ps[:, k, t * P:(t + 1) * P], xrows[:, t, k * P:(k + 1) * P], ident[:])
                    if t == NT - 1:
                        mm.then_inc(turned, 1)
            for j in range(NPG + 1):
                if j == LATE:
                    pe.wait_ge(c_ready, NT + 1)
                    for f in range(NCT + 1):
                        if f == 0:
                            pe.wait_ge(set_free[0], used_before["c0"])
                        if f == 4:
                            pe.wait_ge(set_free[1], used_before["c1"])
                        if f == 8:
                            pe.wait_ge(set_free[0], used_before["c0"] + 1)
                        w = P if f < NCT else ROPE
                        for t in range(NT):
                            mm = nc.tensor.transpose(ps[0:w, f % 8, t * P:(t + 1) * P],
                                                     cbuf[:, t, f * P:f * P + w], ident[:])
                        mm.then_inc(turned, 1)
                    pe.wait_ge(c_lo, NCT + 1)
                if j < NPG:
                    pe_group(pe, j, set_free)
            pe_rest(pe)


_INS = ["x", "positions", "g_mix", "w_in", "lam_q1", "lam_k1", "lam_q2", "lam_k2", "g_subln", "g_q", "g_kv",
        "w_uq", "w_ukv", "w_o_diff", "w_o_mla", "b_gates", "w_out", "g_ffn", "w_router", "b_router", "w_gate",
        "b_gate", "w_up", "b_up", "w_down", "b_down", "g_final"]


def kernel(**inputs):
    import concourse.bacc as bacc
    from concourse.bass_utils import run_bass_kernel_spmd

    nc = bacc.Bacc("TRN2", target_bir_lowering=False, num_devices=1)
    arrays = {name: np.ascontiguousarray(inputs[name]) for name in _INS}
    inv = [np.float32(THETA) ** (-np.arange(0, r, 2, dtype=np.float32) / r) for r in (DA_ROT, ROPE)]
    arrays["inv_freq"] = np.tile(np.concatenate(inv).astype(np.float32), (P, 1))
    arrays["identity"] = np.eye(P, dtype=np.float32)
    aps, feeds = {}, {}
    for name, a in arrays.items():
        feeds[f"in_{name}"] = a
        aps[name] = nc.dram_tensor(f"in_{name}", a.shape, mybir.dt.from_np(a.dtype), kind="ExternalInput").ap()
    out = nc.dram_tensor("out_0", (1, SEQ, D), F32, kind="ExternalOutput").ap()
    hybrid_encoder_layer(nc, out=out, **aps)
    r = run_bass_kernel_spmd(nc, [feeds], core_ids=[0])
    return r.results[0]["out_0"]
```
